# Optimizing a Trainium2 kernel written in Bass

```python
import jax, jax.numpy as jnp
from jax import lax
import numpy as np

D_MODEL = 1024
BATCH = 1
SEQ = 1024
DEPTH = 2
DEC_BATCH = 8
DEC_SEQ = 4
PAST_LEN = 4096
PAGE_SIZE = 128

D_CONV_A = D_MODEL // 2
D_CONV_B = D_MODEL // 2
CONV_A_WIDTH = 31
CONV_B_WIDTH = 3
N_HEADS = 8
Q_LORA = 384
KV_LORA = 256
QK_NOPE = 128
QK_ROPE = 64
V_DIM = 128
ROPE_THETA = 10000.0
SM_SCALE = (QK_NOPE + QK_ROPE) ** -0.5
Q_BLOCK = 128
D_FF = -(-8 * D_MODEL // (3 * 256)) * 256
N_CONV_LAYERS = (DEPTH + 1) // 2
N_MLA_LAYERS = DEPTH // 2
RMS_EPS = 1e-6
LN_EPS = 1e-5

kernel_name = "hybrid_conformer_shortconv_mla_decoder_step"

def rmsnorm(x, g):
    xf = x.astype(jnp.float32)
    y = xf * lax.rsqrt(jnp.mean(xf * xf, axis=-1, keepdims=True) + RMS_EPS)
    return (y * g.astype(jnp.float32)).astype(x.dtype)

def layernorm(x, g, b):
    xf = x.astype(jnp.float32)
    mu = jnp.mean(xf, axis=-1, keepdims=True)
    xc = xf - mu
    var = jnp.mean(xc * xc, axis=-1, keepdims=True)
    return (xc * lax.rsqrt(var + LN_EPS) * g.astype(jnp.float32) + b.astype(jnp.float32)).astype(x.dtype)

def rope(x, pos):
    half = QK_ROPE // 2
    inv_freq = 1.0 / (ROPE_THETA ** (jnp.arange(half, dtype=jnp.float32) * (2.0 / QK_ROPE)))
    ang = pos.astype(jnp.float32)[:, None] * inv_freq[None, :]
    shape = (1, pos.shape[0]) + (1,) * (x.ndim - 3) + (half,)
    cos = jnp.cos(ang).reshape(shape)
    sin = jnp.sin(ang).reshape(shape)
    xf = x.astype(jnp.float32)
    x1, x2 = xf[..., :half], xf[..., half:]
    return jnp.concatenate([x1 * cos - x2 * sin, x1 * sin + x2 * cos], axis=-1).astype(x.dtype)

def causal_dwconv(xpad, w):
    return lax.conv_general_dilated(
        xpad, w[:, None, :].astype(xpad.dtype), window_strides=(1,), padding="VALID",
        dimension_numbers=("NWC", "WIO", "NWC"), feature_group_count=xpad.shape[-1])

def swiglu_ffn(h, wg, wu, wd):
    return (jax.nn.silu(h @ wg) * (h @ wu)) @ wd

def conv_mixer(h, state_a, state_b, w_in, wa, ba, lng, lnb, wb, w_out):
    u = h @ w_in
    a_val, a_gate, b_gate, c_gate, b_in = jnp.split(
        u, [D_CONV_A, 2 * D_CONV_A, 2 * D_CONV_A + D_CONV_B, 2 * D_CONV_A + 2 * D_CONV_B], axis=-1)
    glu = a_val * jax.nn.sigmoid(a_gate)
    apad = jnp.concatenate([state_a.astype(glu.dtype), glu], axis=1)
    a = jax.nn.silu(layernorm(causal_dwconv(apad, wa) + ba, lng, lnb))
    z = c_gate * b_in
    zpad = jnp.concatenate([state_b.astype(z.dtype), z], axis=1)
    b = b_gate * causal_dwconv(zpad, wb)
    out = jnp.concatenate([a, b], axis=-1) @ w_out
    return out, apad[:, -(CONV_A_WIDTH - 1):], zpad[:, -(CONV_B_WIDTH - 1):]

def mla_project(h, pos, w_in, qg, w_uq, kvg, w_uk):
    B, S, _ = h.shape
    u = h @ w_in
    cq, ckv, kr = jnp.split(u, [Q_LORA, Q_LORA + KV_LORA], axis=-1)
    q = (rmsnorm(cq, qg) @ w_uq).reshape(B, S, N_HEADS, QK_NOPE + QK_ROPE)
    q_nope, q_rope = q[..., :QK_NOPE], rope(q[..., QK_NOPE:], pos)
    c_kv = rmsnorm(ckv, kvg)
    k_rope = rope(kr, pos)
    q_lat = jnp.einsum('bshn,lhn->bshl', q_nope, w_uk)
    return q_lat, q_rope, c_kv, k_rope

def mla_attend(q_lat, q_rope, c_kv, k_rope, q_pos, k_pos):
    s = (jnp.einsum('bqhl,bkl->bhqk', q_lat, c_kv)
         + jnp.einsum('bqhr,bkr->bhqk', q_rope, k_rope)).astype(jnp.float32) * SM_SCALE
    mask = k_pos[None, :] <= q_pos[:, None]
    s = jnp.where(mask[None, None], s, -jnp.inf)
    p = jax.nn.softmax(s, axis=-1).astype(c_kv.dtype)
    return jnp.einsum('bhqk,bkl->bqhl', p, c_kv)

def attend_prompt(q_lat, q_rope, c_kv, k_rope):
    B, S, H, L = q_lat.shape
    nb = S // Q_BLOCK
    qlb = q_lat.reshape(B, nb, Q_BLOCK, H, L).transpose(1, 0, 2, 3, 4)
    qrb = q_rope.reshape(B, nb, Q_BLOCK, H, QK_ROPE).transpose(1, 0, 2, 3, 4)
    qpos = jnp.arange(S).reshape(nb, Q_BLOCK)
    kpos = jnp.arange(S)
    out = lax.map(lambda a: mla_attend(a[0], a[1], c_kv, k_rope, a[2], kpos), (qlb, qrb, qpos))
    return out.transpose(1, 0, 2, 3, 4).reshape(B, S, H, L)

def mla_output(o_lat, w_uv, w_o):
    B, Q = o_lat.shape[:2]
    o = jnp.einsum('bqhl,lhv->bqhv', o_lat, w_uv).reshape(B, Q, N_HEADS * V_DIM)
    return o @ w_o

def setup_inputs(seed: int = 0) -> dict:
    key = jax.random.key(seed)
    ks = iter(jax.random.split(key, 40))
    f32 = jnp.float32

    def nrm(shape, scale=1.0):
        return jax.random.normal(next(ks), shape, f32) * scale

    def gain(shape):
        return 1.0 + 0.05 * jax.random.normal(next(ks), shape, f32)

    n_pages = PAST_LEN // PAGE_SIZE
    n_used = DEC_BATCH * n_pages
    n_pool = n_used + n_used // 4
    page_table = jax.random.permutation(next(ks), n_pool)[:n_used].reshape(DEC_BATCH, n_pages).astype(jnp.int32)
    d_in_conv = 2 * D_CONV_A + 3 * D_CONV_B
    return {
        "x_prompt": nrm((BATCH, SEQ, D_MODEL)),
        "x_sample": nrm((DEC_BATCH, DEC_SEQ, D_MODEL)),
        "state_conv_a": nrm((N_CONV_LAYERS, DEC_BATCH, CONV_A_WIDTH - 1, D_CONV_A), 0.5),
        "state_conv_b": nrm((N_CONV_LAYERS, DEC_BATCH, CONV_B_WIDTH - 1, D_CONV_B), 0.5),
        "cache_kv_latent": nrm((N_MLA_LAYERS, n_pool, PAGE_SIZE, KV_LORA)),
        "cache_k_rope": nrm((N_MLA_LAYERS, n_pool, PAGE_SIZE, QK_ROPE)),
        "page_table": page_table,
        "mix_pre_gain": gain((DEPTH, D_MODEL)),
        "mix_post_gain": gain((DEPTH, D_MODEL)),
        "ffn_pre_gain": gain((DEPTH, D_MODEL)),
        "ffn_post_gain": gain((DEPTH, D_MODEL)),
        "w_ffn_gate": nrm((DEPTH, D_MODEL, D_FF), D_MODEL ** -0.5),
        "w_ffn_up": nrm((DEPTH, D_MODEL, D_FF), D_MODEL ** -0.5),
        "w_ffn_down": nrm((DEPTH, D_FF, D_MODEL), D_FF ** -0.5),
        "w_in_conv": nrm((N_CONV_LAYERS, D_MODEL, d_in_conv), D_MODEL ** -0.5),
        "conv_a_w": nrm((N_CONV_LAYERS, CONV_A_WIDTH, D_CONV_A), CONV_A_WIDTH ** -0.5),
        "conv_a_b": nrm((N_CONV_LAYERS, D_CONV_A), 0.02),
        "ln_a_gain": gain((N_CONV_LAYERS, D_CONV_A)),
        "ln_a_bias": nrm((N_CONV_LAYERS, D_CONV_A), 0.02),
        "conv_b_w": nrm((N_CONV_LAYERS, CONV_B_WIDTH, D_CONV_B), CONV_B_WIDTH ** -0.5),
        "w_out_conv": nrm((N_CONV_LAYERS, D_CONV_A + D_CONV_B, D_MODEL), (D_CONV_A + D_CONV_B) ** -0.5),
        "w_in_mla": nrm((N_MLA_LAYERS, D_MODEL, Q_LORA + KV_LORA + QK_ROPE), D_MODEL ** -0.5),
        "q_norm_gain": gain((N_MLA_LAYERS, Q_LORA)),
        "w_uq": nrm((N_MLA_LAYERS, Q_LORA, N_HEADS * (QK_NOPE + QK_ROPE)), Q_LORA ** -0.5),
        "kv_norm_gain": gain((N_MLA_LAYERS, KV_LORA)),
        "w_uk": nrm((N_MLA_LAYERS, KV_LORA, N_HEADS, QK_NOPE), KV_LORA ** -0.5),
        "w_uv": nrm((N_MLA_LAYERS, KV_LORA, N_HEADS, V_DIM), KV_LORA ** -0.5),
        "w_o_mla": nrm((N_MLA_LAYERS, N_HEADS * V_DIM, D_MODEL), (N_HEADS * V_DIM) ** -0.5),
    }

def reference(x_prompt, x_sample, state_conv_a, state_conv_b, cache_kv_latent, cache_k_rope, page_table,
              mix_pre_gain, mix_post_gain, ffn_pre_gain, ffn_post_gain, w_ffn_gate, w_ffn_up, w_ffn_down,
              w_in_conv, conv_a_w, conv_a_b, ln_a_gain, ln_a_bias, conv_b_w, w_out_conv,
              w_in_mla, q_norm_gain, w_uq, kv_norm_gain, w_uk, w_uv, w_o_mla):
    Bp, Sp = x_prompt.shape[:2]
    Bs, Ss = x_sample.shape[:2]
    past_len = page_table.shape[1] * cache_kv_latent.shape[2]
    pos_p = jnp.arange(Sp)
    pos_s = past_len + jnp.arange(Ss)
    k_pos_s = jnp.arange(past_len + Ss)
    yp, ys = x_prompt, x_sample
    ca_p, ca_s, cb_p, cb_s = [], [], [], []
    kv_p, kv_s, kr_p, kr_s = [], [], [], []
    for layer in range(DEPTH):
        hp = rmsnorm(yp, mix_pre_gain[layer])
        hs = rmsnorm(ys, mix_pre_gain[layer])
        if layer % 2 == 0:
            i = layer // 2
            prm = (w_in_conv[i], conv_a_w[i], conv_a_b[i], ln_a_gain[i], ln_a_bias[i], conv_b_w[i], w_out_conv[i])
            zero_a = jnp.zeros((Bp, CONV_A_WIDTH - 1, D_CONV_A), hp.dtype)
            zero_b = jnp.zeros((Bp, CONV_B_WIDTH - 1, D_CONV_B), hp.dtype)
            op, na_p, nb_p = conv_mixer(hp, zero_a, zero_b, *prm)
            os_, na_s, nb_s = conv_mixer(hs, state_conv_a[i], state_conv_b[i], *prm)
            ca_p.append(na_p); ca_s.append(na_s); cb_p.append(nb_p); cb_s.append(nb_s)
        else:
            j = layer // 2
            prm = (w_in_mla[j], q_norm_gain[j], w_uq[j], kv_norm_gain[j], w_uk[j])
            ql_p, qr_p, c_p, r_p = mla_project(hp, pos_p, *prm)
            op = mla_output(attend_prompt(ql_p, qr_p, c_p, r_p), w_uv[j], w_o_mla[j])
            ql_s, qr_s, c_s, r_s = mla_project(hs, pos_s, *prm)
            past_c = cache_kv_latent[j, page_table].reshape(Bs, past_len, KV_LORA).astype(c_s.dtype)
            past_r = cache_k_rope[j, page_table].reshape(Bs, past_len, QK_ROPE).astype(r_s.dtype)
            c_all = jnp.concatenate([past_c, c_s], axis=1)
            r_all = jnp.concatenate([past_r, r_s], axis=1)
            os_ = mla_output(mla_attend(ql_s, qr_s, c_all, r_all, pos_s, k_pos_s), w_uv[j], w_o_mla[j])
            kv_p.append(c_p); kv_s.append(c_s); kr_p.append(r_p); kr_s.append(r_s)
        yp = yp + rmsnorm(op, mix_post_gain[layer])
        ys = ys + rmsnorm(os_, mix_post_gain[layer])
        fp = swiglu_ffn(rmsnorm(yp, ffn_pre_gain[layer]), w_ffn_gate[layer], w_ffn_up[layer], w_ffn_down[layer])
        fs = swiglu_ffn(rmsnorm(ys, ffn_pre_gain[layer]), w_ffn_gate[layer], w_ffn_up[layer], w_ffn_down[layer])
        yp = yp + rmsnorm(fp, ffn_post_gain[layer])
        ys = ys + rmsnorm(fs, ffn_post_gain[layer])
    new_conv_a_prompt = jnp.stack(ca_p)
    new_conv_a_sample = jnp.stack(ca_s)
    new_conv_b_prompt = jnp.stack(cb_p)
    new_conv_b_sample = jnp.stack(cb_s)
    new_kv_latent_prompt = jnp.stack(kv_p)
    new_kv_latent_sample = jnp.stack(kv_s)
    new_k_rope_prompt = jnp.stack(kr_p)
    new_k_rope_sample = jnp.stack(kr_s)
    return (yp, ys, new_conv_a_prompt, new_conv_a_sample, new_conv_b_prompt, new_conv_b_sample,
            new_kv_latent_prompt, new_kv_latent_sample, new_k_rope_prompt, new_k_rope_sample)


_drawn_inputs = setup_inputs


def setup_inputs(seed=0):
    import zlib

    import numpy as np

    out = dict(_drawn_inputs(seed))
    spreads = {}
    factors = {'ln_a_bias': 2.947}
    for name, (base, spread) in spreads.items():
        noise = np.random.default_rng([zlib.crc32(name.encode()), seed]).standard_normal(out[name].shape)
        drawn = base * np.exp(spread * noise) if base else spread * noise
        out[name] = __import__('jax').numpy.asarray(drawn.astype(out[name].dtype))
    for name, factor in factors.items():
        out[name] = (out[name] * factor).astype(out[name].dtype)
    return out
```

```python
from contextlib import ExitStack

import numpy as np

import concourse.bass as bass
from concourse import mybir

F32 = mybir.dt.float32
I32 = mybir.dt.int32
U32 = mybir.dt.uint32
ALU = mybir.AluOpType
ACT = mybir.ActivationFunctionType
AX_X = mybir.AxisListType.X

P = 128
SEQ, DEC_BATCH, DEC_SEQ = 1024, 8, 4
SAMPLE = DEC_BATCH * DEC_SEQ
TOKENS = SEQ + SAMPLE
GROUPS = 3
GW = TOKENS // GROUPS
D = 1024
DC = D // P
D_FF = 2816
FC = D_FF // P
CHAN = 512
CC = CHAN // P
TAPS_A, TAPS_B = 31, 3
PAD_A, PAD_B = TAPS_A - 1, TAPS_B - 1
HEADS = 8
Q_LORA, KV_LORA, ROPE, NOPE, VDIM = 384, 256, 64, 128, 128
QC, LC = Q_LORA // P, KV_LORA // P
QT = SEQ // P
PAGE, PAGES = 128, 32
RUN = 32
RUNS_PER_PAGE = PAGE // RUN
SM_SCALE = float((NOPE + ROPE) ** -0.5)
RMS_EPS, LN_EPS = 1e-6, 1e-5
NEG = -1e30

ROW_MIX_PRE, ROW_MIX_POST, ROW_FFN_PRE, ROW_FFN_POST = 0, 16, 32, 48
ROW_CONV_B = 64
ROW_BIAS_A = ROW_CONV_B + TAPS_B * CC
ROW_LN_G = ROW_BIAS_A + CC
ROW_LN_B = ROW_LN_G + CC
ROW_QN = ROW_LN_B + CC
ROW_KVN = ROW_QN + QC
PARAM_ROWS = ROW_KVN + LC
TAP_ROWS = TAPS_A * CC


def group(t):
    return slice(t * GW, (t + 1) * GW)


def peeled(eng, n, body):
    body(0, True)
    if n > 1:
        with eng.Fori(1, n) as i:
            body(i, False)


class Chip:
    pass


def reuse_semaphores(nc, since):
    nc.clear_and_free_semaphores(nc.allocated_since(since))
    nc.all_engine_barrier()


def load_stage(nc, c, t):
    with ExitStack() as ctx:
        sb = lambda n, s, d=F32: ctx.enter_context(nc.sbuf_tensor(n, s, d))
        sem = lambda n: nc.alloc_semaphore(n)
        rows = [sb(f"token_rows{j}", [P, D]) for j in range(2)]
        tail_rows = sb("sample_rows", [SAMPLE, D])
        param_rows = sb("param_rows", [PARAM_ROWS, P])
        tap_rows = sb("tap_rows", [TAP_ROWS, P])
        state_a = sb("state_a_rows", [4 * PAD_A, 2, CHAN])
        state_b = sb("state_b_rows", [DEC_BATCH * PAD_B, CHAN])
        bank = [ctx.enter_context(nc.psum_tensor(f"turn{j}", [P, 512], F32)) for j in range(4)]
        landed = [sem("even_rows_landed"), sem("odd_rows_landed")]
        consts_landed, small_landed = sem("consts_landed"), sem("small_landed")
        ones_set = sem("ones_set")
        turned, kept = sem("block_turned"), sem("block_kept")
        small_turned, small_kept = sem("small_turned"), sem("small_kept")
        block = ctx.enter_context(nc.Block())
        x = t["x_prompt"].rearrange("a (n p) d -> (a n) p d", p=P)

        small_out = []
        small_in = []

        def small(b, pieces, dst, view):
            small_in.append((b, pieces))
            small_out.append((dst, b, None, view))

        for half in range(2):
            small(half, [(tail_rows[:, (4 * half + k) * P:(4 * half + k + 1) * P], SAMPLE, k * SAMPLE, SAMPLE) for k in range(4)],
                  c.y[:, 4 * half:4 * half + 4, SEQ:TOKENS],
                  lambda bk: bk[:, 0:4 * SAMPLE].rearrange("p (k n) -> p k n", k=4))
        small(2, [(param_rows[:], PARAM_ROWS, 0, PARAM_ROWS), (tap_rows[:], TAP_ROWS, PARAM_ROWS, TAP_ROWS)],
              c.param[:], lambda bk: bk[:, 0:PARAM_ROWS + TAP_ROWS])
        SA = 4 * PAD_A
        for k in range(CC):
            small(3 if k % 2 == 0 else 0,
                  [(state_a[:, g, k * P:(k + 1) * P], SA, g * SA, SA) for g in range(2)]
                  + [(state_b[:, k * P:(k + 1) * P], DEC_BATCH * PAD_B, 2 * SA, DEC_BATCH * PAD_B)],
                  c.state[:, k, :], lambda bk: bk[:, 0:2 * SA + DEC_BATCH * PAD_B])

        @block.sync
        def _(sp):
            sp.dma_start(c.ident[:], t["ident"]).then_inc(consts_landed, 16)

            def step(i, first):
                for j in range(2):
                    if not first:
                        sp.wait_ge(turned, 4 * i - 2 + 2 * j)
                    sp.dma_start(rows[j][:], x[2 * i + j]).then_inc(landed[j], 16)

            peeled(sp, QT // 2, step)

        @block.scalar
        def _(act):
            act.dma_start(tail_rows[:], t["x_sample"].rearrange("b s d -> (b s) d")).then_inc(small_landed, 16)
            r = 0
            for name, n in (("mix_pre_gain", 16), ("mix_post_gain", 16), ("ffn_pre_gain", 16), ("ffn_post_gain", 16)):
                act.dma_start(param_rows[r:r + n, :], t[name].rearrange("l (k p) -> (l k) p", p=P)).then_inc(small_landed, 16)
                r += n
            for name, n in (("conv_b_w", TAPS_B * CC), ):
                act.dma_start(param_rows[r:r + n, :], t[name].rearrange("l w (k p) -> (l w k) p", p=P)).then_inc(small_landed, 16)
                r += n
            for name, n in (("conv_a_b", CC), ("ln_a_gain", CC), ("ln_a_bias", CC), ("q_norm_gain", QC), ("kv_norm_gain", LC)):
                act.dma_start(param_rows[r:r + n, :], t[name].rearrange("l (k p) -> (l k) p", p=P)).then_inc(small_landed, 16)
                r += n
            act.dma_start(tap_rows[:], t["conv_a_w"].rearrange("l w (k p) -> (l w k) p", p=P)).then_inc(small_landed, 16)
            act.dma_start(state_a[:], t["state_conv_a"].rearrange("l b w c -> (l b w) c").rearrange(
                "(g r) c -> r g c", g=2)).then_inc(small_landed, 16)
            act.dma_start(state_b[:], t["state_conv_b"].rearrange("l b w c -> (l b w) c")).then_inc(small_landed, 16)

            def step(i, first):
                for j in range(2):
                    act.wait_ge(turned, 4 * i + 2 * j + 2)
                    act.copy(c.y[:, 4:8, bass.ts(2 * i + j, P)],
                             bank[2 * j + 1][:].rearrange("p (k n) -> p k n", k=4)).then_inc(kept, 1)

            peeled(act, QT // 2, step)

        @block.gpsimd
        def _(pool):
            pool.memset(c.ones[:], 1.0).then_inc(ones_set, 1)

        @block.vector
        def _(dve):
            def step(i, first):
                for j in range(2):
                    dve.wait_ge(turned, 4 * i + 2 * j + 1)
                    dve.tensor_copy(c.y[:, 0:4, bass.ts(2 * i + j, P)],
                                    bank[2 * j][:].rearrange("p (k n) -> p k n", k=4)).then_inc(small_kept, 1)

            peeled(dve, QT // 2, step)
            for n, (dst, b, w, v) in enumerate(small_out):
                dve.wait_ge(small_turned, n + 1)
                dve.tensor_copy(dst, v(bank[b])).then_inc(small_kept, 1)

        @block.tensor
        def _(pe):
            pe.wait_ge(consts_landed, 16)

            def step(i, first):
                for j in range(2):
                    pe.wait_ge(landed[j], 16 * i + 16)
                    for half in range(2):
                        if not first:
                            if half == 0:
                                pe.wait_ge(small_kept, 2 * i + j - 1)
                            else:
                                pe.wait_ge(kept, 2 * i + j - 1)
                        for k in range(4):
                            mm = pe.transpose(bank[2 * j + half][:, k * P:(k + 1) * P],
                                              rows[j][:, (4 * half + k) * P:(4 * half + k + 1) * P], c.ident[:])
                        mm.then_inc(turned, 1)

            peeled(pe, QT // 2, step)
            pe.wait_ge(small_landed, 16 * 14)
            pe.wait_ge(kept, QT)
            for n, (b, pieces) in enumerate(small_in):
                pe.wait_ge(small_kept, QT + max(0, n - 1))
                for src, k_rows, at, width in pieces:
                    mm = pe.transpose(bank[b][:, at:at + width], src, c.ident[0:k_rows, 0:k_rows])
                mm.then_inc(small_turned, 1)


def norm_stage(nc, c, tag, rounds):
    R = len(rounds)
    with ExitStack() as ctx:
        sb = lambda n, s, d=F32: ctx.enter_context(nc.sbuf_tensor(f"{n}_{tag}", s, d))
        sem = lambda n: nc.alloc_semaphore(f"{n}_{tag}")
        most = max(r[1] for r in rounds)
        squares = sb("squares", [P, most, GW])
        mean = sb("mean_square", [P, GW])
        root = sb("root", [P, GW])
        rstd = sb("rstd", [P, GW])
        total = ctx.enter_context(nc.psum_tensor(f"total_{tag}", [P, GW], F32))
        squared, summed = sem("squared"), sem("summed")
        mean_set, root_set, rstd_set = sem("mean_set"), sem("root_set"), sem("rstd_set")
        scaled, applied = sem("scaled"), sem("applied")
        n_scaled = sum(r[1] for r in rounds if r[4] is not None)
        block = ctx.enter_context(nc.Block())

        @block.scalar
        def _(act):
            def step(g, first):
                for j, (src, chunks, col, dst, res) in enumerate(rounds):
                    if j or not first:
                        act.wait_ge(summed, g * R + j)
                    if j:
                        act.wait_ge(applied, g * R + j)
                    act.activation(squares[:, 0:chunks, :], src[:, 0:chunks, bass.ts(g, GW)],
                                   ACT.Square).then_inc(squared, 1)
                    act.wait_ge(mean_set, g * R + j + 1)
                    act.activation(root[:], mean[:], ACT.Sqrt).then_inc(root_set, 1)

            peeled(act, GROUPS, step)

        @block.tensor
        def _(pe):
            def step(g, first):
                for j, (src, chunks, col, dst, res) in enumerate(rounds):
                    pe.wait_ge(squared, g * R + j + 1)
                    if j or not first:
                        pe.wait_ge(mean_set, g * R + j)
                    for k in range(chunks):
                        mm = pe.matmul(total[:], c.ones[:], squares[:, k, :], start=(k == 0), stop=(k == chunks - 1))
                    mm.then_inc(summed, 1)

            peeled(pe, GROUPS, step)

        @block.vector
        def _(dve):
            def step(g, first):
                n = 0
                for j, (src, chunks, col, dst, res) in enumerate(rounds):
                    now = bass.ts(g, GW)
                    dve.wait_ge(summed, g * R + j + 1)
                    if j or not first:
                        dve.wait_ge(root_set, g * R + j)
                    dve.tensor_scalar(mean[:], total[:], 1.0 / (chunks * P), RMS_EPS, ALU.mult, ALU.add).then_inc(mean_set, 1)
                    dve.wait_ge(root_set, g * R + j + 1)
                    dve.reciprocal(rstd[:], root[:]).then_inc(rstd_set, 1)
                    dve.wait_ge(rstd_set, g * R + j + 1)
                    for k in range(chunks):
                        ins = dve.scalar_tensor_tensor(out=(dst if res is None else src)[:, k, now], in0=src[:, k, now],
                                                       scalar=c.param[:, col + k:col + k + 1], in1=rstd[:],
                                                       op0=ALU.mult, op1=ALU.mult)
                        if res is not None:
                            ins.then_inc(scaled, 1)
                            n += 1
                    if res is not None:
                        dve.wait_ge(scaled, g * n_scaled + n)
                        ins = dve.tensor_tensor(res[:, 0:chunks, now], res[:, 0:chunks, now], src[:, 0:chunks, now], ALU.add)
                    ins.then_inc(applied, 1)
                    if res is not None and j + 1 < R:
                        dve.wait_ge(applied, g * R + j + 1)

            peeled(dve, GROUPS, step)


def project_stage(nc, c, tag, w, k_chunks, widths, src, dst):
    pairs = sum(x == P for x in widths) // 2
    with ExitStack() as ctx:
        sem = lambda n: nc.alloc_semaphore(f"{n}_{tag}")
        slot = [ctx.enter_context(nc.sbuf_tensor(f"w{j}_{tag}", [P, k_chunks, P], F32)) for j in range(2)]
        bank = [[ctx.enter_context(nc.psum_tensor(f"out{j}{g}_{tag}", [P, GW], F32)) for g in range(GROUPS)] for j in range(2)]
        landed = [sem(f"weights{j}_landed") for j in range(2)]
        done = [sem(f"product{j}_done") for j in range(2)]
        kept = [sem(f"product{j}_kept") for j in range(2)]
        block = ctx.enter_context(nc.Block())
        w_view = w.rearrange("(k p) n -> p k n", p=P)
        tail = [(j, x) for j, x in enumerate(widths[2 * pairs:])]

        @block.sync
        def _(sp):
            def load(q, j, width, first):
                if not first:
                    sp.wait_ge(done[j], 3 * q)
                sp.dma_start(slot[j][:, :, 0:width], w_view[:, :, bass.ds((2 * q + j) * P, width)]).then_inc(landed[j], 16)

            def step(q, first):
                for j in range(2):
                    load(q, j, P, first)

            peeled(sp, pairs, step)
            for j, width in tail:
                load(pairs, j, width, False)

        @block.tensor
        def _(pe):
            def product(q, j, width, first):
                pe.wait_ge(landed[j], 16 * q + 16)
                for g in range(GROUPS):
                    if not first:
                        pe.wait_ge(kept[j], 3 * q - 2 + g)
                    for k in range(k_chunks):
                        mm = pe.matmul(bank[j][g][0:width, :], slot[j][:, k, 0:width], src[:, k, group(g)],
                                       start=(k == 0), stop=(k == k_chunks - 1))
                    mm.then_inc(done[j], 1)

            def step(q, first):
                for j in range(2):
                    product(q, j, P, first)

            peeled(pe, pairs, step)
            for j, width in tail:
                product(pairs, j, width, False)

        @block.scalar
        def _(act):
            def keep(q, j, width):
                for g in range(GROUPS):
                    act.wait_ge(done[j], 3 * q + g + 1)
                    act.copy(dst[0:width, 2 * q + j, group(g)], bank[j][g][0:width, :]).then_inc(kept[j], 1)

            def step(q, first):
                for j in range(2):
                    keep(q, j, P)

            peeled(act, pairs, step)
            for j, width in tail:
                keep(pairs, j, width)


def conv_stage(nc, c, t, mix):
    A_GATE, A_VAL, B_GATE, C_GATE, B_IN = range(5)
    column = {A_VAL: 0, A_GATE: 1, B_GATE: 2, C_GATE: 3, B_IN: 4}
    with ExitStack() as ctx:
        sb = lambda n, s, d=F32: ctx.enter_context(nc.sbuf_tensor(n, s, d))
        sem = lambda n: nc.alloc_semaphore(n)
        slot = [sb(f"w_in{s}", [P, DC, P]) for s in range(5)]
        sig, bg, cg, bi = (sb(n, [P, TOKENS]) for n in ("a_sigmoid", "b_gate", "c_gate", "b_in"))
        apad = sb("a_prompt", [P, PAD_A + SEQ])
        apad_s = sb("a_sample", [P, DEC_BATCH, PAD_A + DEC_SEQ])
        zpad = sb("z_prompt", [P, PAD_B + SEQ])
        zpad_s = sb("z_sample", [P, DEC_BATCH, PAD_B + DEC_SEQ])
        bank = [[ctx.enter_context(nc.psum_tensor(f"proj{j}{g}", [P, GW], F32)) for g in range(GROUPS)] for j in range(2)]
        landed = [sem(f"w_in{s}_landed") for s in range(5)]
        done, act_kept, glu_done = sem("projection_done"), sem("act_kept"), sem("glu_done")
        z_done, b_done = sem("z_done"), sem("b_conv_done")
        tap, tap_b = sem("tap_added"), sem("tap_b_added")
        state_set, pads_zero, tails_kept = sem("state_set"), sem("pads_zero"), sem("tails_kept")
        block = ctx.enter_context(nc.Block())
        w_view = t["w_in_conv"].rearrange("l (k p) n -> p (l k) n", p=P)
        LAST = SEQ - (GROUPS - 1) * GW
        TA, TB_ = 2 * TAPS_A, 2 * TAPS_B

        @block.sync
        def _(sp):
            def step(i, first):
                for s in range(5):
                    if not first:
                        sp.wait_ge(done, 15 * i - 15 + 3 * s + 3)
                    sp.dma_start(slot[s][:], w_view[:, :, bass.ds(column[s] * CHAN + i * P, P)]).then_inc(landed[s], 16)

            for i in range(CC):
                step(i, i == 0)

        @block.tensor
        def _(pe):
            def step(i, first):
                for s in range(5):
                    pe.wait_ge(landed[s], 16 * i + 16)
                    for g in range(GROUPS):
                        if s == A_GATE and not first:
                            pe.wait_ge(act_kept, 12 * i - 2 + g)
                        if s == A_VAL and not first:
                            pe.wait_ge(act_kept, 12 * i - 5 + g)
                        if s == B_GATE:
                            pe.wait_ge(act_kept, 12 * i + g + 1)
                        if s == C_GATE:
                            pe.wait_ge(glu_done, 4 * i + (g + 1 if g < 2 else 4))
                        if s == B_IN:
                            pe.wait_ge(act_kept, 12 * i + 3 + g + 1)
                        for k in range(DC):
                            mm = pe.matmul(bank[s % 2][g][:], slot[s][:, k, :], c.h[:, k, group(g)],
                                           start=(k == 0), stop=(k == DC - 1))
                        mm.then_inc(done, 1)

            peeled(pe, CC, step)

        @block.scalar
        def _(act):
            def step(i, first):
                for s, out, func in ((A_GATE, sig, ACT.Sigmoid), (B_GATE, bg, ACT.Copy), (C_GATE, cg, ACT.Copy), (B_IN, bi, ACT.Copy)):
                    for g in range(GROUPS):
                        act.wait_ge(done, 15 * i + 3 * s + g + 1)
                        if not first and g == 0:
                            if s == A_GATE:
                                act.wait_ge(glu_done, 4 * i)
                            elif s == B_GATE:
                                act.wait_ge(b_done, i)
                            else:
                                act.wait_ge(z_done, 4 * i)
                        act.activation(out[:, group(g)], bank[s % 2][g][:], func).then_inc(act_kept, 1)

            peeled(act, CC, step)

        @block.gpsimd
        def _(pool):
            pool.memset(apad[:, 0:PAD_A], 0.0).then_inc(pads_zero, 1)
            pool.memset(zpad[:, 0:PAD_B], 0.0).then_inc(pads_zero, 1)
            SA = DEC_BATCH * PAD_A

            def step(i, first):
                if not first:
                    pool.wait_ge(tails_kept, i)
                    pool.wait_ge(tap, TA * i)
                    pool.wait_ge(b_done, i)
                pool.tensor_copy(apad_s[:, :, 0:PAD_A],
                                 c.state[:, i, 0:SA].rearrange("p (b w) -> p b w", b=DEC_BATCH)).then_inc(state_set, 1)
                pool.tensor_copy(zpad_s[:, :, 0:PAD_B],
                                 c.state[:, i, SA:SA + DEC_BATCH * PAD_B].rearrange("p (b w) -> p b w", b=DEC_BATCH)
                                 ).then_inc(state_set, 1)
                pool.wait_ge(glu_done, 4 * i + 4)
                pool.wait_ge(state_set, 2 * i + 2)
                pool.tensor_copy(c.tails[:, i, 0:PAD_A], apad[:, SEQ:SEQ + PAD_A])
                pool.tensor_copy(c.tails[:, i, PAD_A:PAD_A + SA].rearrange("p (b w) -> p b w", b=DEC_BATCH),
                                 apad_s[:, :, DEC_SEQ:DEC_SEQ + PAD_A])
                pool.wait_ge(z_done, 4 * i + 4)
                o = PAD_A + SA
                pool.tensor_copy(c.tails[:, i, o:o + PAD_B], zpad[:, SEQ:SEQ + PAD_B])
                pool.tensor_copy(c.tails[:, i, o + PAD_B:o + PAD_B + DEC_BATCH * PAD_B].rearrange("p (b w) -> p b w", b=DEC_BATCH),
                                 zpad_s[:, :, DEC_SEQ:DEC_SEQ + PAD_B]).then_inc(tails_kept, 1)

            peeled(pool, CC, step)

        @block.vector
        def _(dve):
            def steps_view(x):
                return x.rearrange("p (b s) -> p b s", b=DEC_BATCH)

            def step(i, first):
                if first:
                    dve.wait_ge(pads_zero, 2)
                else:
                    dve.wait_ge(tails_kept, i)
                for g in range(GROUPS):
                    dve.wait_ge(done, 15 * i + 3 * A_VAL + g + 1)
                    dve.wait_ge(act_kept, 12 * i + g + 1)
                    n = GW if g < GROUPS - 1 else LAST
                    dve.tensor_tensor(apad[:, PAD_A + g * GW:PAD_A + g * GW + n], bank[A_VAL % 2][g][:, 0:n],
                                      sig[:, g * GW:g * GW + n], ALU.mult).then_inc(glu_done, 1)
                dve.tensor_tensor(apad_s[:, :, PAD_A:], steps_view(bank[A_VAL % 2][GROUPS - 1][:, LAST:]),
                                  steps_view(sig[:, SEQ:]), ALU.mult).then_inc(glu_done, 1)
                dve.wait_ge(glu_done, 4 * i + 4)
                dve.wait_ge(state_set, 2 * i + 2)
                for w in range(TAPS_A):
                    wcol = c.param[:, bass.ds(PARAM_ROWS + w * CC + i, 1)]
                    for part, (src, out) in enumerate(((apad[:, w:w + SEQ], mix[:, i, 0:SEQ]),
                                                       (apad_s[:, :, w:w + DEC_SEQ], steps_view(mix[:, i, SEQ:TOKENS])))):
                        if w == 0:
                            dve.tensor_scalar(out, src, wcol, c.param[:, bass.ds(ROW_BIAS_A + i, 1)],
                                              ALU.mult, ALU.add).then_inc(tap, 1)
                        else:
                            dve.wait_ge(tap, TA * i + 2 * w + part - 1)
                            dve.scalar_tensor_tensor(out=out, in0=src, scalar=wcol, in1=out,
                                                     op0=ALU.mult, op1=ALU.add).then_inc(tap, 1)
                dve.wait_ge(act_kept, 12 * i + 12)
                for g in range(GROUPS):
                    n = GW if g < GROUPS - 1 else LAST
                    dve.tensor_tensor(zpad[:, PAD_B + g * GW:PAD_B + g * GW + n], cg[:, g * GW:g * GW + n],
                                      bi[:, g * GW:g * GW + n], ALU.mult).then_inc(z_done, 1)
                dve.tensor_tensor(zpad_s[:, :, PAD_B:], steps_view(cg[:, SEQ:]), steps_view(bi[:, SEQ:]),
                                  ALU.mult).then_inc(z_done, 1)
                dve.wait_ge(z_done, 4 * i + 4)
                for w in range(TAPS_B):
                    wcol = c.param[:, bass.ds(ROW_CONV_B + w * CC + i, 1)]
                    for part, (src, out) in enumerate(((zpad[:, w:w + SEQ], mix[:, CC + i, 0:SEQ]),
                                                       (zpad_s[:, :, w:w + DEC_SEQ], steps_view(mix[:, CC + i, SEQ:TOKENS])))):
                        if w == 0:
                            dve.tensor_scalar(out, src, wcol, None, ALU.mult).then_inc(tap_b, 1)
                        else:
                            dve.wait_ge(tap_b, TB_ * i + 2 * w + part - 1)
                            dve.scalar_tensor_tensor(out=out, in0=src, scalar=wcol, in1=out,
                                                     op0=ALU.mult, op1=ALU.add).then_inc(tap_b, 1)
                dve.wait_ge(tap_b, TB_ * i + TB_)
                dve.tensor_tensor(mix[:, CC + i, :], mix[:, CC + i, :], bg[:], ALU.mult).then_inc(b_done, 1)

            peeled(dve, CC, step)


def conv_norm_stage(nc, c, t, mix):
    SA = DEC_BATCH * PAD_A
    HALF = SA // 2
    with ExitStack() as ctx:
        sb = lambda n, s, d=F32: ctx.enter_context(nc.sbuf_tensor(n, s, d))
        sem = lambda n: nc.alloc_semaphore(n)
        squares = sb("ln_squares", [P, CC, GW])
        mean, var, root, rstd = (sb(n, [P, GW]) for n in ("ln_mean", "ln_var", "ln_root", "ln_rstd"))
        total, total2 = (ctx.enter_context(nc.psum_tensor(n, [P, GW], F32)) for n in ("ln_total", "ln_total2"))
        bank = [ctx.enter_context(nc.psum_tensor(f"state_out{j}", [P, 512], F32)) for j in range(5)]
        out_ap, out_bp = sb("new_a_prompt", [PAD_A, CHAN]), sb("new_b_prompt", [PAD_B, CHAN])
        out_as = sb("new_a_sample", [HALF, 2, CHAN])
        out_bs = sb("new_b_sample", [DEC_BATCH * PAD_B, CHAN])
        summed, mean_set, centred, squared = sem("ln_summed"), sem("ln_mean_set"), sem("ln_centred"), sem("ln_squared")
        summed2, var_set, root_set, rstd_set, scaled = (sem(n) for n in ("ln_summed2", "ln_var_set", "ln_root_set", "ln_rstd_set", "ln_scaled"))
        silu_done, turned, kept, stored = sem("ln_silu_done"), sem("state_turned"), sem("state_kept"), sem("state_stored")
        block = ctx.enter_context(nc.Block())
        pieces = [(0, PAD_A, out_ap[:]), (PAD_A, HALF, out_as[:, 0, :]), (PAD_A + HALF, HALF, out_as[:, 1, :]),
                  (PAD_A + SA, PAD_B, out_bp[:]), (PAD_A + SA + PAD_B, DEC_BATCH * PAD_B, out_bs[:])]

        @block.tensor
        def _(pe):
            for n, (at, width, out) in enumerate(pieces):
                for k in range(CC):
                    mm = pe.transpose(bank[n][0:width, k * P:(k + 1) * P], c.tails[:, k, at:at + width], c.ident[:])
                mm.then_inc(turned, 1)
            def step(g, first):
                if not first:
                    pe.wait_ge(mean_set, g)
                for k in range(CC):
                    mm = pe.matmul(total[:], c.ones[:], mix[:, k, bass.ts(g, GW)], start=(k == 0), stop=(k == CC - 1))
                mm.then_inc(summed, 1)
                pe.wait_ge(squared, g + 1)
                for k in range(CC):
                    mm = pe.matmul(total2[:], c.ones[:], squares[:, k, :], start=(k == 0), stop=(k == CC - 1))
                mm.then_inc(summed2, 1)

            peeled(pe, GROUPS, step)

        @block.scalar
        def _(act):
            def step(g, first):
                act.wait_ge(centred, 4 * g + 4)
                act.activation(squares[:], mix[:, 0:CC, bass.ts(g, GW)], ACT.Square).then_inc(squared, 1)
                act.wait_ge(var_set, g + 1)
                act.activation(root[:], var[:], ACT.Sqrt).then_inc(root_set, 1)

            peeled(act, GROUPS, step)
            def step(g, first):
                act.wait_ge(scaled, 4 * g + 4)
                for k in range(CC):
                    act.activation(mix[:, k, bass.ts(g, GW)], mix[:, k, bass.ts(g, GW)], ACT.Silu,
                                   bias=c.param[:, ROW_LN_B + k:ROW_LN_B + k + 1],
                                   scale=c.param[:, ROW_LN_G + k:ROW_LN_G + k + 1]).then_inc(silu_done, 1)

            peeled(act, GROUPS, step)

        @block.vector
        def _(dve):
            for n, (at, width, out) in enumerate(pieces):
                dve.wait_ge(turned, n + 1)
                dve.tensor_copy(out, bank[n][0:width, :]).then_inc(kept, 1)
            def step(g, first):
                now = bass.ts(g, GW)
                dve.wait_ge(summed, g + 1)
                dve.tensor_scalar(mean[:], total[:], 1.0 / CHAN, None, ALU.mult).then_inc(mean_set, 1)
                dve.wait_ge(mean_set, g + 1)
                for k in range(CC):
                    dve.tensor_tensor(mix[:, k, now], mix[:, k, now], mean[:], ALU.subtract).then_inc(centred, 1)
                dve.wait_ge(summed2, g + 1)
                dve.tensor_scalar(var[:], total2[:], 1.0 / CHAN, LN_EPS, ALU.mult, ALU.add).then_inc(var_set, 1)
                dve.wait_ge(root_set, g + 1)
                dve.reciprocal(rstd[:], root[:]).then_inc(rstd_set, 1)
                dve.wait_ge(rstd_set, g + 1)
                for k in range(CC):
                    dve.tensor_tensor(mix[:, k, now], mix[:, k, now], rstd[:], ALU.mult).then_inc(scaled, 1)

            peeled(dve, GROUPS, step)

        @block.sync
        def _(sp):
            sp.wait_ge(kept, len(pieces))
            sp.dma_start(t["new_conv_a_prompt"].rearrange("l b w c -> (l b w) c"), out_ap[:]).then_inc(stored, 16)
            a_s = t["new_conv_a_sample"].rearrange("l b w c -> (l b w) c")
            for j in range(2):
                sp.dma_start(a_s[j * HALF:(j + 1) * HALF, :], out_as[:, j, :]).then_inc(stored, 16)
            sp.dma_start(t["new_conv_b_prompt"].rearrange("l b w c -> (l b w) c"), out_bp[:]).then_inc(stored, 16)
            sp.dma_start(t["new_conv_b_sample"].rearrange("l b w c -> (l b w) c"), out_bs[:]).then_inc(stored, 16)
            sp.wait_ge(stored, 80)


def ffn_stage(nc, c, layer, t):
    NB = DC * GROUPS
    with ExitStack() as ctx:
        sb = lambda n, s, d=F32: ctx.enter_context(nc.sbuf_tensor(f"{n}{layer}", s, d))
        sem = lambda n: nc.alloc_semaphore(f"{n}{layer}")
        ps = lambda n, s: ctx.enter_context(nc.psum_tensor(f"{n}{layer}", s, F32))
        w_gate, w_up, w_down = sb("w_gate", [P, DC, P]), sb("w_up", [P, DC, P]), sb("w_down", [P, D])
        silu, hidden = sb("silu", [P, TOKENS]), sb("hidden", [P, TOKENS])
        gate_bank = [ps(f"gate_bank{g}_", [P, GW]) for g in range(GROUPS)]
        up_bank = [ps(f"up_bank{g}_", [P, GW]) for g in range(GROUPS)]
        down_bank = [ps(f"down_bank{j}_", [P, GW]) for j in range(2)]
        gate_landed, up_landed, down_landed = sem("gate_landed"), sem("up_landed"), sem("down_landed")
        gate_done, up_done, down_done = sem("gate_done"), sem("up_done"), sem("down_done")
        silu_done, hidden_set = sem("silu_done"), sem("hidden_set")
        down_free = sem("down_bank_free")
        block = ctx.enter_context(nc.Block())
        gate_view = t["w_ffn_gate"][layer].rearrange("(k p) f -> p k f", p=P)
        up_view = t["w_ffn_up"][layer].rearrange("(k p) f -> p k f", p=P)
        down_view = t["w_ffn_down"][layer].rearrange("(f p) n -> f p n", p=P)

        @block.sync
        def _(sp):
            def load_gate(f):
                sp.dma_start(w_gate[:], gate_view[:, :, bass.ds(f * P, P)]).then_inc(gate_landed, 16)

            def load_up(f):
                sp.dma_start(w_up[:], up_view[:, :, bass.ds(f * P, P)]).then_inc(up_landed, 16)

            load_gate(0)
            load_up(0)

            def step(f, first):
                sp.wait_ge(gate_done, 3 * f + 3)
                load_gate(f + 1)
                if not first:
                    sp.wait_ge(down_done, NB * f)
                sp.dma_start(w_down[:], down_view[f]).then_inc(down_landed, 16)
                sp.wait_ge(up_done, 3 * f + 3)
                load_up(f + 1)

            peeled(sp, FC - 1, step)
            sp.wait_ge(down_done, NB * (FC - 1))
            sp.dma_start(w_down[:], down_view[FC - 1]).then_inc(down_landed, 16)

        @block.tensor
        def _(pe):
            def down(f):
                pe.wait_ge(down_landed, 16 * f + 16)
                for m in range(DC):
                    for g in range(GROUPS):
                        n = m * GROUPS + g
                        if m == 0:
                            pe.wait_ge(hidden_set, 3 * f + g + 1)
                        pe.wait_ge(down_free, NB * f + n + 1)
                        pe.matmul(down_bank[n % 2][:], w_down[:, m * P:(m + 1) * P], hidden[:, group(g)],
                                  start=True, stop=True).then_inc(down_done, 1)

            def half(f, first, landed, weights, bank, used, done):
                pe.wait_ge(landed, 16 * f + 16)
                for g in range(GROUPS):
                    if not first:
                        pe.wait_ge(used, 3 * f - 2 + g)
                    for k in range(DC):
                        mm = pe.matmul(bank[g][:], weights[:, k, :], c.h[:, k, group(g)], start=(k == 0), stop=(k == DC - 1))
                    mm.then_inc(done, 1)

            def step(f, first):
                half(f, first, gate_landed, w_gate, gate_bank, silu_done, gate_done)
                if not first:
                    down(f - 1)
                half(f, first, up_landed, w_up, up_bank, hidden_set, up_done)

            peeled(pe, FC, step)
            down(FC - 1)

        @block.scalar
        def _(act):
            def step(f, first):
                for g in range(GROUPS):
                    act.wait_ge(gate_done, 3 * f + g + 1)
                    if not first:
                        act.wait_ge(hidden_set, 3 * f - 2 + g)
                    act.activation(silu[:, group(g)], gate_bank[g][:], ACT.Silu).then_inc(silu_done, 1)

            peeled(act, FC, step)

        @block.vector
        def _(dve):
            for j in range(2):
                dve.memset(c.acc[:, j * DC // 2:(j + 1) * DC // 2, :], 0.0).then_inc(down_free, 1)
            dve.wait_ge(down_free, 2)

            def add(f):
                for m in range(DC):
                    for g in range(GROUPS):
                        n = m * GROUPS + g
                        dve.wait_ge(down_done, NB * f + n + 1)
                        if n == 0:
                            dve.wait_ge(down_free, NB * f + 2)
                        dve.tensor_tensor(c.acc[:, m, group(g)], c.acc[:, m, group(g)], down_bank[n % 2][:],
                                          ALU.add).then_inc(down_free, 1)

            def step(f, first):
                if not first:
                    add(f - 1)
                for g in range(GROUPS):
                    dve.wait_ge(up_done, 3 * f + g + 1)
                    dve.wait_ge(silu_done, 3 * f + g + 1)
                    dve.tensor_tensor(hidden[:, group(g)], up_bank[g][:], silu[:, group(g)], ALU.mult).then_inc(hidden_set, 1)

            peeled(dve, FC, step)
            add(FC - 1)


def latent_stage(nc, c, t, k):
    with ExitStack() as ctx:
        sb = lambda n, s, d=F32: ctx.enter_context(nc.sbuf_tensor(n, s, d))
        sem = lambda n: nc.alloc_semaphore(n)
        by_cos, by_sin = sb("key_by_cos", [ROPE, GROUPS, GW]), sb("key_by_sin", [ROPE, GROUPS, GW])
        key_rows = sb("key_rows", [P, QT + 1, ROPE])
        rot = [ctx.enter_context(nc.psum_tensor(f"key_rotated{g}", [P, GW], F32)) for g in range(GROUPS)]
        bank = [ctx.enter_context(nc.psum_tensor(f"latent_turn{j}", [P, 512], F32)) for j in range(2)]
        consts, rotated, parts, key_set = sem("rope_consts"), sem("key_turned"), sem("key_parts"), sem("key_set")
        turned, kept, stored = sem("latent_turned"), sem("latent_kept"), sem("latent_stored")
        copied = sem("sample_keys_copied")
        block = ctx.enter_context(nc.Block())
        raw = c.acc[:, QC + LC, :]

        @block.scalar
        def _(act):
            act.dma_start(k.cos[:], t["rope_cos"]).then_inc(consts, 16)
            act.dma_start(k.sin[:], t["rope_sin"]).then_inc(consts, 16)
            act.dma_start(k.swap[:], t["rope_swap"]).then_inc(consts, 16)
            act.dma_start(k.causal[:], t["causal"]).then_inc(consts, 16)

        @block.tensor
        def _(pe):
            pe.wait_ge(consts, 64)
            for g in range(GROUPS):
                pe.matmul(rot[g][:], k.swap[:], raw[0:ROPE, group(g)], start=True, stop=True).then_inc(rotated, 1)
            pe.wait_ge(key_set, GROUPS)
            for i in range(QT + 1):
                if i >= 2:
                    pe.wait_ge(kept, 2 * i - 2)
                width = P if i < QT else SAMPLE
                cols = slice(i * P, i * P + width)
                for l in range(LC):
                    pe.transpose(bank[i % 2][0:width, l * P:(l + 1) * P], k.latent[:, l, cols], c.ident[:])
                pe.transpose(bank[i % 2][0:width, KV_LORA:KV_LORA + ROPE], k.key[:, cols],
                             c.ident[0:ROPE, 0:ROPE]).then_inc(turned, 1)

        @block.vector
        def _(dve):
            dve.wait_ge(consts, 64)
            for g in range(GROUPS):
                dve.tensor_tensor(by_cos[:, g, :], raw[0:ROPE, group(g)], k.cos[:, group(g)], ALU.mult).then_inc(parts, 1)
                dve.wait_ge(rotated, g + 1)
                dve.tensor_tensor(by_sin[:, g, :], rot[g][0:ROPE, :], k.sin[:, group(g)], ALU.mult).then_inc(parts, 1)
            for g in range(GROUPS):
                dve.wait_ge(parts, 2 * GROUPS)
                dve.tensor_tensor(k.key[:, group(g)], by_cos[:, g, :], by_sin[:, g, :], ALU.add).then_inc(key_set, 1)
            for i in range(QT + 1):
                dve.wait_ge(turned, i + 1)
                width = P if i < QT else SAMPLE
                dve.tensor_copy(k.rows[0:width, i, :], bank[i % 2][0:width, 0:KV_LORA]).then_inc(kept, 1)
                dve.tensor_copy(key_rows[0:width, i, :], bank[i % 2][0:width, KV_LORA:KV_LORA + ROPE]).then_inc(kept, 1)
            dve.wait_ge(kept, 2 * QT + 2)
            dve.tensor_copy(c.new_latent[:], k.latent[:, :, SEQ:TOKENS]).then_inc(copied, 1)
            dve.tensor_copy(c.new_key[:], k.key[:, SEQ:TOKENS]).then_inc(copied, 1)
            dve.tensor_copy(c.new_rows[:], k.rows[0:SAMPLE, QT, :]).then_inc(copied, 1)

        @block.sync
        def _(sp):
            sp.wait_ge(kept, 2 * QT + 2)
            sp.dma_start(t["new_kv_latent_prompt"].rearrange("l b (n p) d -> p (l b n) d", p=P), k.rows[:, 0:QT, :]).then_inc(stored, 16)
            sp.dma_start(t["new_kv_latent_sample"].rearrange("l b s d -> (l b s) d"), k.rows[0:SAMPLE, QT, :]).then_inc(stored, 16)
            sp.dma_start(t["new_k_rope_prompt"].rearrange("l b (n p) d -> p (l b n) d", p=P), key_rows[:, 0:QT, :]).then_inc(stored, 16)
            sp.dma_start(t["new_k_rope_sample"].rearrange("l b s d -> (l b s) d"), key_rows[0:SAMPLE, QT, :]).then_inc(stored, 16)
            sp.wait_ge(stored, 64)


ORDER = ["S0", "S1", "T0", "S2", "T1", "S3", "T2", "S4", "T3", "L0", "S5", "T4", "V0", "S6", "T5", "S7", "T6", "T7", "L1", "V1"]


def banks_of(i):
    return [list(range(a, min(a + 4, i + 1))) for a in range(0, i + 1, 4)]


def attention_stage(nc, c, t, k, cq):
    with ExitStack() as ctx:
        sb = lambda n, s, d=F32: ctx.enter_context(nc.sbuf_tensor(n, s, d))
        sem = lambda n: nc.alloc_semaphore(n)
        ps = lambda n, s: ctx.enter_context(nc.psum_tensor(n, s, F32))
        w_q, w_uk, w_uv = sb("w_q", [P, QC, NOPE + ROPE]), sb("w_uk", [P, LC, NOPE]), sb("w_uv", [P, LC, VDIM])
        w_ukT = sb("w_uk_turned", [P, LC, P])
        q_nope, q_raw = sb("q_nope", [P, TOKENS]), sb("q_raw", [ROPE, TOKENS])
        by_cos, by_sin = sb("q_by_cos", [ROPE, GROUPS, GW]), sb("q_by_sin", [ROPE, GROUPS, GW])
        q_rope, q_lat = sb("q_rope", [ROPE, TOKENS]), sb("q_lat", [P, LC, TOKENS])
        prob = [sb(f"prob{j}", [P, SEQ]) for j in range(2)]
        probT = sb("prob_turned", [P, QT, 512])
        o_lat = sb("o_lat", [P, LC, SEQ])
        top, bias, total, inv = (sb(n, [P, QT]) for n in ("row_max", "row_bias", "row_total", "row_inverse"))
        score = [ps(f"score{j}", [P, SEQ]) for j in range(2)]
        sum_bank = [ps(f"sum_bank{j}", [P, 512]) for j in range(2)]
        misc = [ps(f"misc{j}", [P, 512]) for j in range(2)]
        q_landed, uk_landed, uv_landed = sem("w_q_landed"), sem("w_uk_landed"), sem("w_uv_landed")
        misc_done, misc_kept = sem("misc_done"), sem("misc_kept")
        sum_done, sum_kept = sem("sum_done"), sem("sum_kept")
        cos_done, rope_set, stashed = sem("cos_done"), sem("rope_set"), sem("stashed")
        scored, masked, topped, biased = sem("scored"), sem("masked"), sem("topped"), sem("biased")
        exp_done, inverted, prob_set = sem("exp_done"), sem("inverted"), sem("prob_set")
        block = ctx.enter_context(nc.Block())

        MISC = {}
        for l in range(LC):
            MISC["uk", l] = len(MISC)
        for name in ("nope", "rope"):
            for g in range(GROUPS):
                MISC[name, g] = len(MISC)
        for l in range(LC):
            for g in range(GROUPS):
                MISC["lat", l, g] = len(MISC)
        for what in ORDER:
            if what[0] == "T":
                for j in range(len(banks_of(int(what[1])))):
                    MISC[what, j] = len(MISC)
            if what[0] == "V":
                MISC[what] = len(MISC)
        M = len(MISC)
        assert M % 2 == 0
        SUMS = GROUPS + 2 * LC

        w_uq = t["w_uq"].rearrange("l (k p) n -> p (l k) n", p=P)
        uk_view = t["w_uk"].rearrange("l (k p) h n -> p (l k) (h n)", p=P)
        uv_view = t["w_uv"].rearrange("l (k p) h n -> p (l k) (h n)", p=P)

        @block.sync
        def _(sp):
            def step(h, first):
                if not first:
                    sp.wait_ge(misc_done, M * h - M + MISC["uk", LC - 1] + 1)
                sp.dma_start(w_uk[:], uk_view[:, :, bass.ds(h * NOPE, NOPE)]).then_inc(uk_landed, 16)
                if not first:
                    sp.wait_ge(misc_done, M * h - M + MISC["rope", GROUPS - 1] + 1)
                sp.dma_start(w_q[:], w_uq[:, :, bass.ds(h * (NOPE + ROPE), NOPE + ROPE)]).then_inc(q_landed, 16)
                if not first:
                    sp.wait_ge(misc_done, M * h)
                sp.dma_start(w_uv[:], uv_view[:, :, bass.ds(h * VDIM, VDIM)]).then_inc(uv_landed, 16)

            peeled(sp, HEADS, step)

        @block.tensor
        def _(pe):
            def step(h, first):
                def misc_bank(*key):
                    u = MISC[key if len(key) > 1 else key[0]]
                    if not (first and u < 2):
                        pe.wait_ge(misc_kept, M * h + u - 1)
                    return misc[u % 2]

                pe.wait_ge(uk_landed, 16 * h + 16)
                for l in range(LC):
                    b = misc_bank("uk", l)
                    pe.transpose(b[:, 0:P], w_uk[:, l, :], c.ident[:]).then_inc(misc_done, 1)
                pe.wait_ge(q_landed, 16 * h + 16)
                for name, cols, n in (("nope", slice(0, NOPE), NOPE), ("rope", slice(NOPE, NOPE + ROPE), ROPE)):
                    for g in range(GROUPS):
                        b = misc_bank(name, g)
                        for j in range(QC):
                            mm = pe.matmul(b[0:n, 0:GW], w_q[:, j, cols], cq[:, j, group(g)], start=(j == 0), stop=(j == QC - 1))
                        mm.then_inc(misc_done, 1)
                for g in range(GROUPS):
                    pe.wait_ge(misc_kept, M * h + MISC["rope", g] + 1)
                    pe.wait_ge(sum_kept, SUMS * h + max(0, g - 1))
                    pe.matmul(sum_bank[g % 2][:, 0:GW], k.swap[:], q_raw[:, group(g)], start=True, stop=True).then_inc(sum_done, 1)
                for l in range(LC):
                    for g in range(GROUPS):
                        b = misc_bank("lat", l, g)
                        pe.matmul(b[:, 0:GW], w_ukT[:, l, :], q_nope[:, group(g)], start=True, stop=True).then_inc(misc_done, 1)
                pe.wait_ge(misc_kept, M * h + MISC["lat", LC - 1, GROUPS - 1] + 1)
                pe.wait_ge(rope_set, GROUPS * h + GROUPS)
                for what in ORDER:
                    i = int(what[1])
                    if what[0] == "S":
                        if not (first and i < 2):
                            pe.wait_ge(exp_done, QT * h + i - 1)
                        q = slice(i * P, (i + 1) * P)
                        for a in range(0, (i + 1) * P, 512):
                            keys = slice(a, min(a + 512, (i + 1) * P))
                            for l in range(LC):
                                pe.matmul(score[i % 2][:, keys], q_lat[:, l, q], k.latent[:, l, keys], start=(l == 0), stop=False)
                            mm = pe.matmul(score[i % 2][:, keys], q_rope[:, q], k.key[:, keys], start=False, stop=True)
                        mm.then_inc(scored, 1)
                    elif what[0] == "T":
                        pe.wait_ge(prob_set, QT * h + i + 1)
                        for j, tiles in enumerate(banks_of(i)):
                            b = misc_bank(what, j)
                            for n, kt in enumerate(tiles):
                                mm = pe.transpose(b[:, n * P:(n + 1) * P], prob[i % 2][:, kt * P:(kt + 1) * P], c.ident[:])
                            mm.then_inc(misc_done, 1)
                    elif what[0] == "L":
                        last = f"T{4 * i + 3}"
                        pe.wait_ge(misc_kept, M * h + MISC[last, len(banks_of(4 * i + 3)) - 1] + 1)
                        for l in range(LC):
                            pe.wait_ge(sum_kept, SUMS * h + GROUPS + (LC * (i - 1) + l + 1 if i else 0))
                            for kt in range(4 * i + 4):
                                q0 = max(kt - 4 * i, 0) * P
                                mm = pe.matmul(sum_bank[l][:, q0:512], k.rows[:, kt, l * P:(l + 1) * P], probT[:, kt, q0:512],
                                               start=(kt == 0), stop=(kt == 4 * i + 3))
                            mm.then_inc(sum_done, 1)
                    else:
                        pe.wait_ge(uv_landed, 16 * h + 16)
                        pe.wait_ge(sum_kept, SUMS * h + GROUPS + LC * (i + 1))
                        b = misc_bank(what)
                        for l in range(LC):
                            mm = pe.matmul(b[:], w_uv[:, l, :], o_lat[:, l, i * 512:(i + 1) * 512], start=(l == 0), stop=(l == LC - 1))
                        mm.then_inc(misc_done, 1)

            peeled(pe, HEADS, step)

        @block.scalar
        def _(act):
            def step(h, first):
                def keep(key, dst, src):
                    act.wait_ge(misc_done, M * h + MISC[key] + 1)
                    act.copy(dst, src(misc[MISC[key] % 2])).then_inc(misc_kept, 1)

                for l in range(LC):
                    keep(("uk", l), w_ukT[:, l, :], lambda b: b[:, 0:P])
                for g in range(GROUPS):
                    keep(("nope", g), q_nope[:, group(g)], lambda b: b[:, 0:GW])
                for g in range(GROUPS):
                    keep(("rope", g), q_raw[:, group(g)], lambda b: b[0:ROPE, 0:GW])
                for l in range(LC):
                    for g in range(GROUPS):
                        keep(("lat", l, g), q_lat[:, l, group(g)], lambda b: b[:, 0:GW])
                for what in ORDER:
                    i = int(what[1])
                    if what[0] == "S":
                        act.wait_ge(biased, QT * h + i + 1)
                        act.activation(prob[i % 2][:, 0:(i + 1) * P], score[i % 2][:, 0:(i + 1) * P], ACT.Exp,
                                       bias=bias[:, i:i + 1], scale=SM_SCALE, accum_out=total[:, i:i + 1]).then_inc(exp_done, 1)
                    elif what[0] == "T":
                        for j, tiles in enumerate(banks_of(i)):
                            n = len(tiles)
                            keep((what, j), probT[:, tiles[0]:tiles[0] + n, (i % 4) * P:(i % 4 + 1) * P],
                                 lambda b: b[:, 0:n * P].rearrange("p (n q) -> p n q", n=n))
                    elif what[0] == "V":
                        keep(what, c.h[:, h, i * 512:(i + 1) * 512], lambda b: b[:])

            peeled(act, HEADS, step)

        @block.vector
        def _(dve):
            def step(h, first):
                for g in range(GROUPS):
                    dve.wait_ge(misc_kept, M * h + MISC["rope", g] + 1)
                    dve.tensor_tensor(by_cos[:, g, :], q_raw[:, group(g)], k.cos[:, group(g)], ALU.mult).then_inc(cos_done, 1)
                    dve.wait_ge(sum_done, SUMS * h + g + 1)
                    dve.tensor_tensor(by_sin[:, g, :], sum_bank[g % 2][0:ROPE, 0:GW], k.sin[:, group(g)], ALU.mult).then_inc(sum_kept, 1)
                    dve.wait_ge(cos_done, GROUPS * h + g + 1)
                    dve.wait_ge(sum_kept, SUMS * h + g + 1)
                    dve.tensor_tensor(q_rope[:, group(g)], by_cos[:, g, :], by_sin[:, g, :], ALU.add).then_inc(rope_set, 1)
                dve.wait_ge(misc_kept, M * h + MISC["lat", LC - 1, GROUPS - 1] + 1)
                dve.wait_ge(rope_set, GROUPS * h + GROUPS)
                dve.tensor_copy(c.q_lat_s[:, :, h, :], q_lat[:, :, SEQ:TOKENS]).then_inc(stashed, 1)
                dve.tensor_copy(c.q_rope_s[:, h, :], q_rope[:, SEQ:TOKENS]).then_inc(stashed, 1)

                def maximum(i):
                    n = QT * h + i + 1
                    dve.wait_ge(scored, n)
                    own = slice(i * P, (i + 1) * P)
                    dve.tensor_tensor(score[i % 2][:, own], score[i % 2][:, own], k.causal[:], ALU.add).then_inc(masked, 1)
                    dve.wait_ge(masked, n)
                    dve.tensor_reduce(top[:, i:i + 1], score[i % 2][:, 0:(i + 1) * P], AX_X, ALU.max).then_inc(topped, 1)
                    dve.wait_ge(topped, n)
                    dve.tensor_scalar(bias[:, i:i + 1], top[:, i:i + 1], -SM_SCALE, None, ALU.mult).then_inc(biased, 1)

                def normalise(i):
                    n = QT * h + i + 1
                    dve.wait_ge(exp_done, n)
                    dve.reciprocal(inv[:, i:i + 1], total[:, i:i + 1]).then_inc(inverted, 1)
                    dve.wait_ge(inverted, n)
                    dve.tensor_scalar(prob[i % 2][:, 0:(i + 1) * P], prob[i % 2][:, 0:(i + 1) * P], inv[:, i:i + 1], None,
                                      ALU.mult).then_inc(prob_set, 1)

                for what in ORDER:
                    i = int(what[1])
                    if what[0] == "S":
                        maximum(i)
                    elif what[0] == "T":
                        normalise(i)
                    elif what[0] == "V":
                        for l in range(LC):
                            dve.wait_ge(sum_done, SUMS * h + GROUPS + LC * i + l + 1)
                            dve.tensor_copy(o_lat[:, l, i * 512:(i + 1) * 512], sum_bank[l][:]).then_inc(sum_kept, 1)

            peeled(dve, HEADS, step)


def sample_stage(nc, c, t):
    CG = RUN // 4
    KEYS = RUN * P
    ROWS = HEADS * DEC_SEQ
    with ExitStack() as ctx:
        sb = lambda n, s, d=F32: ctx.enter_context(nc.sbuf_tensor(n, s, d))
        sem = lambda n: nc.alloc_semaphore(n)
        ps = lambda n, s: ctx.enter_context(nc.psum_tensor(n, s, F32))
        pages, run_ids = sb("pages", [P, DEC_BATCH], I32), sb("run_ids", [P, DEC_BATCH], U32)
        offset = sb("run_offset", [P, 1])
        new_mask = sb("new_mask", [ROWS, DEC_BATCH, SAMPLE])
        latent = [sb(f"cache_latent{j}", [P, RUN * KV_LORA]) for j in range(2)]
        rope = [sb(f"cache_rope{j}", [P, RUN * ROPE]) for j in range(2)]
        probT = sb("sample_prob_turned", [P, RUN + 1, ROWS])
        q_b, qr_b = sb("q_lat_batch", [P, LC, HEADS, DEC_SEQ]), sb("q_rope_batch", [ROPE, HEADS, DEC_SEQ])
        tops, top, bias, total, inv = (sb(n, [ROWS, w]) for n, w in (("s_tops", CG + 1), ("s_top", 1), ("s_bias", 1), ("s_total", 1), ("s_inv", 1)))
        flat = c.acc[:].rearrange("p a n -> p (a n)")
        s_all = flat[0:ROWS, 0:KEYS + SAMPLE]
        keysT = [flat[:, 4352 + 1536 * j:4352 + 1536 * (j + 1)].rearrange("p (a n) -> p a n", a=3) for j in range(2)]
        turn = [[ps(f"turn_bank{j}{a}", [P, 512]) for a in range(3)] for j in range(2)]
        score = ps("s_score", [ROWS, 512])
        work = ps("s_work", [P, 512])
        consts, ids_set = sem("s_consts"), sem("ids_set")
        landed = [[sem(f"latent{j}_landed"), sem(f"rope{j}_landed")] for j in range(2)]
        batch_done, q_set = sem("batch_done"), sem("q_set")
        turned, act_kept, dve_kept = sem("keys_turned"), sem("keys_kept_act"), sem("keys_kept_dve")
        scored, score_kept, topped, biased = sem("s_scored"), sem("s_score_kept"), sem("s_topped"), sem("s_biased")
        exp_done, prob_set, p_turned, p_kept = sem("s_exp_done"), sem("s_prob_set"), sem("s_p_turned"), sem("s_p_kept")
        o_kept, inverted = sem("s_o_kept"), sem("s_inverted")
        block = ctx.enter_context(nc.Block())
        cache_l = t["cache_kv_latent"].rearrange("l n (r s) d -> (l n r) (s d)", s=RUN)
        cache_r = t["cache_k_rope"].rearrange("l n (r s) d -> (l n r) (s d)", s=RUN)

        @block.sync
        def _(sp):
            sp.dma_start(pages[:], t["pages"]).then_inc(consts, 16)
            sp.dma_start(offset[:], t["run_offset"]).then_inc(consts, 16)
            sp.dma_start(new_mask[:], t["new_mask"]).then_inc(consts, 16)

        @block.gpsimd
        def _(pool):
            pool.wait_ge(ids_set, 1)

            for b in range(DEC_BATCH):
                j = b % 2
                if b >= 2:
                    pool.wait_ge(batch_done, b - 1)
                for dst, src, n in ((latent[j], cache_l, 0), (rope[j], cache_r, 1)):
                    pool.indirect_dma_start(dst[:], None, src, bass.IndirectOffsetOnAxis(ap=run_ids[:, b:b + 1], axis=0)
                                            ).then_inc(landed[j][n], 16)

        @block.tensor
        def _(pe):
            def batch(q, j, first):
                b = 2 * q + j
                pe.wait_ge(landed[j][0], 16 * q + 16)
                pe.wait_ge(landed[j][1], 16 * q + 16)
                pe.wait_ge(q_set, 2 * b + 2)

                def turn_keys(n):
                    s = n % 2
                    if not (first and n < 2):
                        pe.wait_ge(act_kept, 2 * (CG * b + n - 1))
                        pe.wait_ge(dve_kept, CG * b + n - 1)
                    for r in range(4):
                        at = (4 * n + r)
                        for l in range(LC):
                            pe.transpose(turn[s][l][:, r * P:(r + 1) * P],
                                         latent[j][:, at * KV_LORA + l * P:at * KV_LORA + (l + 1) * P], c.ident[:])
                        mm = pe.transpose(turn[s][2][0:ROPE, r * P:(r + 1) * P],
                                          rope[j][:, at * ROPE:(at + 1) * ROPE], c.ident[:])
                    mm.then_inc(turned, 1)

                turn_keys(0)
                for n in range(CG + 1):
                    if n + 1 < CG:
                        turn_keys(n + 1)
                    if n < CG:
                        pe.wait_ge(act_kept, 2 * (CG * b + n + 1))
                        pe.wait_ge(dve_kept, CG * b + n + 1)
                    if not (first and n == 0):
                        pe.wait_ge(score_kept, (CG + 1) * b + n)
                    width = 512 if n < CG else SAMPLE
                    for l in range(LC):
                        pe.matmul(score[:, 0:width], q_b[:, l].rearrange("p h s -> p (h s)"),
                                  keysT[n % 2][:, l, :] if n < CG else c.new_latent[:, l, :], start=(l == 0), stop=False)
                    pe.matmul(score[:, 0:width], qr_b[:].rearrange("p h s -> p (h s)"),
                              keysT[n % 2][0:ROPE, 2, :] if n < CG else c.new_key[:], start=False, stop=True).then_inc(scored, 1)
                pe.wait_ge(prob_set, b + 1)
                for a in range(2):
                    if a:
                        pe.wait_ge(p_kept, 3 * b + 1)
                    elif not first:
                        pe.wait_ge(o_kept, b)
                    for r in range(16):
                        mm = pe.matmul(work[:, r * ROWS:(r + 1) * ROWS], s_all[:, (16 * a + r) * P:(16 * a + r + 1) * P],
                                       c.ident[0:ROWS, 0:ROWS], start=True, stop=True)
                    if a:
                        mm = pe.matmul(score[0:SAMPLE, 0:ROWS], s_all[:, KEYS:KEYS + SAMPLE], c.ident[0:ROWS, 0:ROWS],
                                       start=True, stop=True)
                    mm.then_inc(p_turned, 1)
                pe.wait_ge(p_kept, 3 * b + 3)
                for l in range(LC):
                    for r in range(RUN):
                        pe.matmul(work[:, l * ROWS:(l + 1) * ROWS], latent[j][:, r * KV_LORA + l * P:r * KV_LORA + (l + 1) * P],
                                  probT[:, r, :], start=(r == 0), stop=False)
                    mm = pe.matmul(work[:, l * ROWS:(l + 1) * ROWS], c.new_rows[:, l * P:(l + 1) * P],
                                   probT[0:SAMPLE, RUN, :], start=False, stop=True)
                mm.then_inc(batch_done, 1)

            def step(q, first):
                for j in range(2):
                    batch(q, j, first and j == 0)

            peeled(pe, DEC_BATCH // 2, step)

        @block.scalar
        def _(act):
            def step(q, first):
                for j in range(2):
                    b = 2 * q + j
                    for n in range(CG):
                        act.wait_ge(turned, CG * b + n + 1)
                        if not (first and j == 0 and n < 2):
                            act.wait_ge(scored, (CG + 1) * b + n - 1 if n >= 2 else (CG + 1) * b + n - 2)
                        for a, rows in ((0, P), (2, ROPE)):
                            act.copy(keysT[n % 2][0:rows, a, :], turn[n % 2][a][0:rows, :]).then_inc(act_kept, 1)
                    act.wait_ge(biased, b + 1)
                    act.activation(s_all, s_all, ACT.Exp, bias=bias[:], scale=SM_SCALE, accum_out=total[:]).then_inc(exp_done, 1)

            peeled(act, DEC_BATCH // 2, step)

        @block.vector
        def _(dve):
            dve.wait_ge(consts, 48)
            dve.tensor_scalar(run_ids[:], pages[:], float(RUNS_PER_PAGE), offset[:], ALU.mult, ALU.add).then_inc(ids_set, 1)

            def batch(q, j, first):
                b = 2 * q + j
                for dst, src in ((q_b, c.q_lat_s[:, :, :, bass.ds(b * DEC_SEQ, DEC_SEQ)]),
                                 (qr_b, c.q_rope_s[:, :, bass.ds(b * DEC_SEQ, DEC_SEQ)])):
                    dve.tensor_copy(dst[:], src).then_inc(q_set, 1)
                for n in range(CG + 1):
                    if n < CG:
                        dve.wait_ge(turned, CG * b + n + 1)
                        if not (first and n < 2):
                            dve.wait_ge(scored, (CG + 1) * b + n - 1 if n >= 2 else (CG + 1) * b + n - 2)
                        dve.tensor_copy(keysT[n % 2][:, 1, :], turn[n % 2][1][:]).then_inc(dve_kept, 1)
                    if n >= 1:
                        keep(b, n - 1, first)
                keep(b, CG, first)
                dve.wait_ge(topped, (CG + 2) * b + CG + 1)
                dve.tensor_reduce(top[:], tops[:], AX_X, ALU.max).then_inc(topped, 1)
                dve.wait_ge(topped, (CG + 2) * b + CG + 2)
                dve.wait_ge(score_kept, (CG + 1) * b + CG + 1)
                dve.tensor_scalar(bias[:], top[:], -SM_SCALE, None, ALU.mult).then_inc(biased, 1)
                dve.wait_ge(exp_done, b + 1)
                dve.reciprocal(inv[:], total[:]).then_inc(inverted, 1)
                dve.wait_ge(inverted, b + 1)
                dve.tensor_scalar(s_all, s_all, inv[:], None, ALU.mult).then_inc(prob_set, 1)
                for a in range(2):
                    dve.wait_ge(p_turned, 2 * b + a + 1)
                    dve.tensor_copy(probT[:, 16 * a:16 * a + 16, :], work[:].rearrange("p (r q) -> p r q", r=16)).then_inc(p_kept, 1)
                dve.tensor_copy(probT[0:SAMPLE, RUN, :], score[0:SAMPLE, 0:ROWS]).then_inc(p_kept, 1)
                dve.wait_ge(batch_done, b + 1)
                dve.tensor_copy(c.o_lat_s[:, :, :, bass.ds(b * DEC_SEQ, DEC_SEQ)],
                                work[:, 0:LC * ROWS].rearrange("p (l h s) -> p l h s", l=LC, h=HEADS)).then_inc(o_kept, 1)

            def keep(b, n, first):
                dve.wait_ge(scored, (CG + 1) * b + n + 1)
                if n < CG:
                    dve.tensor_copy(s_all[:, n * 512:(n + 1) * 512], score[:]).then_inc(score_kept, 1)
                    at = slice(n * 512, (n + 1) * 512)
                else:
                    dve.tensor_tensor(s_all[:, KEYS:KEYS + SAMPLE], score[:, 0:SAMPLE], new_mask[:, b, :], ALU.add).then_inc(score_kept, 1)
                    at = slice(KEYS, KEYS + SAMPLE)
                dve.wait_ge(score_kept, (CG + 1) * b + n + 1)
                dve.tensor_reduce(tops[:, n:n + 1], s_all[:, at], AX_X, ALU.max).then_inc(topped, 1)

            def step(q, first):
                for j in range(2):
                    batch(q, j, first and j == 0)

            peeled(dve, DEC_BATCH // 2, step)


def sample_value_stage(nc, c, t):
    with ExitStack() as ctx:
        sem = lambda n: nc.alloc_semaphore(n)
        w_uv = ctx.enter_context(nc.sbuf_tensor("w_uv_all", [P, LC, HEADS * VDIM], F32))
        bank = ctx.enter_context(nc.psum_tensor("value_bank", [P, HEADS, SAMPLE], F32))
        landed, done, kept = sem("w_uv_all_landed"), sem("values_done"), sem("values_kept")
        block = ctx.enter_context(nc.Block())

        @block.sync
        def _(sp):
            sp.dma_start(w_uv[:], t["w_uv"].rearrange("l (k p) h n -> p (l k) (h n)", p=P)).then_inc(landed, 16)

        @block.tensor
        def _(pe):
            pe.wait_ge(landed, 16)
            for h in range(HEADS):
                for l in range(LC):
                    mm = pe.matmul(bank[:, h, :], w_uv[:, l, h * VDIM:(h + 1) * VDIM], c.o_lat_s[:, l, h, :],
                                   start=(l == 0), stop=(l == LC - 1))
            mm.then_inc(done, 1)

        @block.vector
        def _(dve):
            dve.wait_ge(done, 1)
            dve.tensor_copy(c.h[:, :, SEQ:TOKENS], bank[:]).then_inc(kept, 1)


def store_stage(nc, c, t):
    with ExitStack() as ctx:
        sem = lambda n: nc.alloc_semaphore(n)
        rows = ctx.enter_context(nc.sbuf_tensor("out_rows", [P, 2, D], F32))
        bank = [ctx.enter_context(nc.psum_tensor(f"out_bank{j}", [P, 512], F32)) for j in range(4)]
        turned, kept = sem("out_turned"), sem("out_kept")
        stored = [sem(f"out_stored{j}") for j in range(2)]
        block = ctx.enter_context(nc.Block())
        y = t["y_prompt"].rearrange("a (n p) d -> (a n) p d", p=P)
        tiles = [(i, P if i < QT else SAMPLE) for i in range(QT + 1)]

        @block.tensor
        def _(pe):
            for i, width in tiles:
                for half in range(2):
                    if i >= 2:
                        pe.wait_ge(kept, 2 * i - 3 + half)
                    for n in range(4):
                        mm = pe.transpose(bank[2 * (i % 2) + half][0:width, n * P:(n + 1) * P],
                                          c.y[:, 4 * half + n, i * P:i * P + width], c.ident[:])
                    mm.then_inc(turned, 1)

        @block.vector
        def _(dve):
            for i, width in tiles:
                for half in range(2):
                    dve.wait_ge(turned, 2 * i + half + 1)
                    if i >= 2:
                        dve.wait_ge(stored[i % 2], 16 * (i // 2))
                    dve.tensor_copy(rows[0:width, i % 2, half * 512:(half + 1) * 512],
                                    bank[2 * (i % 2) + half][0:width, :]).then_inc(kept, 1)

        @block.sync
        def _(sp):
            for i, width in tiles:
                sp.wait_ge(kept, 2 * i + 2)
                out = y[i] if i < QT else t["y_sample"].rearrange("b s d -> (b s) d")
                sp.dma_start(out, rows[0:width, i % 2, :]).then_inc(stored[i % 2], 16)
            sp.wait_ge(stored[0], 16 * 5)
            sp.wait_ge(stored[1], 16 * 4)


def trunk(nc, t):
    c = Chip()
    start = nc.snapshot_sems()
    with ExitStack() as ctx:
        sb = lambda n, s, d=F32: ctx.enter_context(nc.sbuf_tensor(n, s, d))
        c.ident, c.ones = sb("ident_sb", [P, P]), sb("ones_sb", [P, P])
        c.param = sb("params", [P, PARAM_ROWS + TAP_ROWS])
        c.y, c.h, c.acc = (sb(n, [P, DC, TOKENS]) for n in ("residual", "normed", "summed"))
        SA = DEC_BATCH * PAD_A
        with ExitStack() as conv:
            csb = lambda n, s, d=F32: conv.enter_context(nc.sbuf_tensor(n, s, d))
            c.state = csb("states", [P, CC, SA + DEC_BATCH * PAD_B])
            c.tails = csb("state_tails", [P, CC, PAD_A + SA + PAD_B + DEC_BATCH * PAD_B])
            load_stage(nc, c, t)
            norm_stage(nc, c, "mix0", [(c.y, DC, ROW_MIX_PRE, c.h, None)])
            mix = csb("mixed", [P, 2 * CC, TOKENS])
            conv_stage(nc, c, t, mix)
            conv_norm_stage(nc, c, t, mix)
            project_stage(nc, c, "w_out", t["w_out_conv"][0], DC, [P] * DC, mix, c.acc)
        norm_stage(nc, c, "ffn0", [(c.acc, DC, ROW_MIX_POST, None, c.y), (c.y, DC, ROW_FFN_PRE, c.h, None)])
        reuse_semaphores(nc, start)
        ffn_stage(nc, c, 0, t)
        norm_stage(nc, c, "mix1", [(c.acc, DC, ROW_FFN_POST, None, c.y), (c.y, DC, ROW_MIX_PRE + DC, c.h, None)])
        c.new_latent, c.new_key, c.new_rows = sb("new_latent", [P, LC, SAMPLE]), sb("new_key", [ROPE, SAMPLE]), sb("new_rows", [SAMPLE, KV_LORA])
        c.q_lat_s, c.q_rope_s = sb("q_lat_sample", [P, LC, HEADS, SAMPLE]), sb("q_rope_sample", [ROPE, HEADS, SAMPLE])
        c.o_lat_s = sb("o_lat_sample", [P, LC, HEADS, SAMPLE])
        project_stage(nc, c, "w_mla", t["w_in_mla"][0], DC, [P] * 5 + [ROPE], c.h, c.acc)
        with ExitStack() as mla:
            msb = lambda n, s, d=F32: mla.enter_context(nc.sbuf_tensor(n, s, d))
            k = Chip()
            k.latent, k.key = msb("latent", [P, LC, TOKENS]), msb("key", [ROPE, TOKENS])
            k.rows = msb("latent_rows", [P, QT + 1, KV_LORA])
            k.cos, k.sin = msb("cos_sb", [ROPE, TOKENS]), msb("sin_sb", [ROPE, TOKENS])
            k.swap, k.causal = msb("swap_sb", [ROPE, P]), msb("causal_sb", [P, P])
            ckv = c.acc[:, QC:QC + LC, :]
            norm_stage(nc, c, "lat", [(c.acc, QC, ROW_QN, c.acc, None), (ckv, LC, ROW_KVN, k.latent, None)])
            latent_stage(nc, c, t, k)
            attention_stage(nc, c, t, k, c.acc)
        reuse_semaphores(nc, start)
        sample_stage(nc, c, t)
        sample_value_stage(nc, c, t)
        project_stage(nc, c, "w_o", t["w_o_mla"][0], DC, [P] * DC, c.h, c.acc)
        norm_stage(nc, c, "ffn1", [(c.acc, DC, ROW_MIX_POST + DC, None, c.y), (c.y, DC, ROW_FFN_PRE + DC, c.h, None)])
        ffn_stage(nc, c, 1, t)
        norm_stage(nc, c, "out", [(c.acc, DC, ROW_FFN_POST + DC, None, c.y)])
        store_stage(nc, c, t)


_OUTS = [("y_prompt", (1, SEQ, D)), ("y_sample", (DEC_BATCH, DEC_SEQ, D)),
         ("new_conv_a_prompt", (1, 1, PAD_A, CHAN)), ("new_conv_a_sample", (1, DEC_BATCH, PAD_A, CHAN)),
         ("new_conv_b_prompt", (1, 1, PAD_B, CHAN)), ("new_conv_b_sample", (1, DEC_BATCH, PAD_B, CHAN)),
         ("new_kv_latent_prompt", (1, 1, SEQ, KV_LORA)), ("new_kv_latent_sample", (1, DEC_BATCH, DEC_SEQ, KV_LORA)),
         ("new_k_rope_prompt", (1, 1, SEQ, ROPE)), ("new_k_rope_sample", (1, DEC_BATCH, DEC_SEQ, ROPE))]


def _constants():
    f = np.float32
    half = ROPE // 2
    inv_freq = (f(1.0) / (f(10000.0) ** (np.arange(half, dtype=f) * f(2.0 / ROPE)))).astype(f)
    pos = np.concatenate([np.arange(SEQ), np.tile(PAGES * PAGE + np.arange(DEC_SEQ), DEC_BATCH)]).astype(f)
    ang = (inv_freq[:, None] * pos[None, :]).astype(f)
    swap = np.zeros((ROPE, P), f)
    for r in range(half):
        swap[half + r, r] = -1.0
        swap[r, half + r] = 1.0
    q = np.arange(P)
    row_step = np.arange(HEADS * DEC_SEQ) % DEC_SEQ
    key_batch, key_step = np.arange(SAMPLE) // DEC_SEQ, np.arange(SAMPLE) % DEC_SEQ
    ok = (key_batch[None, None, :] == np.arange(DEC_BATCH)[None, :, None]) & (key_step[None, None, :] <= row_step[:, None, None])
    return {
        "ident": np.eye(P, dtype=f),
        "rope_cos": np.ascontiguousarray(np.tile(np.cos(ang), (2, 1))),
        "rope_sin": np.ascontiguousarray(np.tile(np.sin(ang), (2, 1))),
        "rope_swap": swap,
        "causal": np.where(q[None, :] <= q[:, None], 0.0, NEG).astype(f),
        "new_mask": np.where(ok, 0.0, NEG).astype(f),
        "run_offset": (q % RUNS_PER_PAGE).astype(f)[:, None],
    }


def kernel(**inputs):
    import concourse.bacc as _bacc
    from concourse.bass_utils import run_bass_kernel_spmd as _run

    nc = _bacc.Bacc("TRN2", target_bir_lowering=False, num_devices=1)
    given = {n: np.ascontiguousarray(a) for n, a in inputs.items() if n != "page_table"}
    given["pages"] = np.ascontiguousarray(np.repeat(np.asarray(inputs["page_table"]), RUNS_PER_PAGE, axis=1).T)
    given.update(_constants())
    arrays, t = {}, {}
    for name, a in given.items():
        arrays[f"in_{name}"] = a
        t[name] = nc.dram_tensor(f"in_{name}", a.shape, mybir.dt.from_np(a.dtype), kind="ExternalInput").ap()
    for name, shape in _OUTS:
        t[name] = nc.dram_tensor(f"out_{name}", shape, F32, kind="ExternalOutput").ap()
    trunk(nc, t)
    r = _run(nc, [arrays], core_ids=[0])
    return tuple(r.results[0][f"out_{name}"] for name, _ in _OUTS)
```

```python
from contextlib import ExitStack

import numpy as np

import concourse.bass as bass
from concourse import mybir

F32 = mybir.dt.float32
F32R = mybir.dt.float32r
I32 = mybir.dt.int32
U32 = mybir.dt.uint32
ALU = mybir.AluOpType
ACT = mybir.ActivationFunctionType
AX_X = mybir.AxisListType.X

P = 128
SEQ, DEC_BATCH, DEC_SEQ = 1024, 8, 4
SAMPLE = DEC_BATCH * DEC_SEQ
TOKENS = SEQ + SAMPLE
GROUPS = 3
GW = TOKENS // GROUPS
D = 1024
DC = D // P
D_FF = 2816
FC = D_FF // P
CHAN = 512
CC = CHAN // P
TAPS_A, TAPS_B = 31, 3
PAD_A, PAD_B = TAPS_A - 1, TAPS_B - 1
HEADS = 8
Q_LORA, KV_LORA, ROPE, NOPE, VDIM = 384, 256, 64, 128, 128
QC, LC = Q_LORA // P, KV_LORA // P
QT = SEQ // P
PAGE, PAGES = 128, 32
RUN = 32
RUNS_PER_PAGE = PAGE // RUN
SM_SCALE = float((NOPE + ROPE) ** -0.5)
RMS_EPS, LN_EPS = 1e-6, 1e-5
NEG = -1e30

ROW_MIX_PRE, ROW_MIX_POST, ROW_FFN_PRE, ROW_FFN_POST = 0, 16, 32, 48
ROW_CONV_B = 64
ROW_BIAS_A = ROW_CONV_B + TAPS_B * CC
ROW_LN_G = ROW_BIAS_A + CC
ROW_LN_B = ROW_LN_G + CC
ROW_QN = ROW_LN_B + CC
ROW_KVN = ROW_QN + QC
PARAM_ROWS = ROW_KVN + LC
TAP_ROWS = TAPS_A * CC


def group(t):
    return slice(t * GW, (t + 1) * GW)


def peeled(eng, n, body):
    body(0, True)
    if n > 1:
        with eng.Fori(1, n) as i:
            body(i, False)


def three_ends(eng, n, body):
    body(0, True, False)
    with eng.Fori(1, n - 1) as i:
        body(i, False, False)
    body(n - 1, False, True)


def split_product(pe, out, w_hi, w_lo, x_hi, x_lo, chunks):
    for k in range(chunks):
        pe.matmul(out, w_hi(k), x_hi(k), start=(k == 0), stop=False)
        pe.matmul(out, w_hi(k), x_lo(k), start=False, stop=False)
        mm = pe.matmul(out, w_lo(k), x_hi(k), start=False, stop=(k == chunks - 1))
    return mm


class Chip:
    pass


class Norm:

    SPACE = DC * GW + 3 * GW

    def __init__(self, nc, ctx, c, tag, post=None, pre=None, space=None):
        self.c = c
        rounds = [r for r in (("post", post), ("pre", pre)) if r[1] is not None]
        if len(rounds) == 2:
            order = [(0, 0), (1, 0), (0, 1), (2, 0), (1, 1), (2, 1)]
        else:
            order = [(g, 0) for g in range(GROUPS)]
        self.units = [(g, *rounds[r]) for g, r in order]
        sem = lambda n: nc.alloc_semaphore(f"{n}_{tag}")
        if space is None:
            space = ctx.enter_context(nc.sbuf_tensor(f"norm_space_{tag}", [P, self.SPACE], F32))[:]
        half = DC // 2 * GW
        self.squares = [space[:, j * half:(j + 1) * half].rearrange("p (k n) -> p k n", n=GW) for j in range(2)]
        self.mean, self.root, self.rstd = (space[:, a:a + GW] for a in range(2 * half, self.SPACE, GW))
        self.total = ctx.enter_context(nc.psum_tensor(f"total_{tag}", [P, GW], F32))
        self.squared, self.half_summed, self.mean_set, self.root_set = sem("squared"), sem("half_summed"), sem("mean_set"), sem("root_set")
        self.rstd_set, self.scaled, self.residual_set = sem("rstd_set"), sem("scaled"), sem("residual_set")
        self.hi_set, self.lo_set = sem("normed_hi"), sem("normed_lo")

    def count(self, u, kind):
        return sum(k == kind for _, k, _ in self.units[:u + 1])

    def wait_residual(self, eng, u):
        for v in range(u):
            if self.units[v][:2] == (self.units[u][0], "post"):
                eng.wait_ge(self.residual_set, self.count(v, "post"))

    def act(self, act):
        c = self.c

        def split(u):
            g, kind, _ = self.units[u]
            if kind == "pre":
                act.wait_ge(self.scaled, u + 1)
                act.copy(c.hi[:, :, group(g)], c.acc[:, :, group(g)]).then_inc(self.hi_set, 1)

        for u, (g, kind, _) in enumerate(self.units):
            if kind == "pre":
                self.wait_residual(act, u)
            src = c.acc if kind == "post" else c.y
            for j in range(2):
                if u:
                    act.wait_ge(self.half_summed, 2 * u - 1 + j)
                act.activation(self.squares[j], src[:, 4 * j:4 * j + 4, group(g)], ACT.Square).then_inc(self.squared, 1)
            act.wait_ge(self.mean_set, u + 1)
            act.activation(self.root, self.mean, ACT.Sqrt).then_inc(self.root_set, 1)
            if u:
                split(u - 1)
        split(len(self.units) - 1)

    def pe(self, pe):
        for u in range(len(self.units)):
            for j in range(2):
                pe.wait_ge(self.squared, 2 * u + j + 1)
                if u and j == 0:
                    pe.wait_ge(self.mean_set, u)
                for k in range(DC // 2):
                    mm = pe.matmul(self.total[:], self.c.ones[:], self.squares[j][:, k, :], start=(j + k == 0),
                                   stop=(j == 1 and k == DC // 2 - 1))
                mm.then_inc(self.half_summed, 1)

    def dve(self, dve):
        c = self.c
        for u, (g, kind, col) in enumerate(self.units):
            dve.wait_ge(self.half_summed, 2 * u + 2)
            if u:
                dve.wait_ge(self.root_set, u)
            dve.tensor_scalar(self.mean, self.total[:], 1.0 / D, RMS_EPS, ALU.mult, ALU.add).then_inc(self.mean_set, 1)
            dve.wait_ge(self.root_set, u + 1)
            if u:
                dve.wait_ge(self.scaled, u)
            dve.reciprocal(self.rstd, self.root).then_inc(self.rstd_set, 1)
            dve.wait_ge(self.rstd_set, u + 1)
            if kind == "pre":
                self.wait_residual(dve, u)
            src = c.acc if kind == "post" else c.y
            for k in range(DC):
                ins = dve.scalar_tensor_tensor(out=c.acc[:, k, group(g)], in0=src[:, k, group(g)],
                                               scalar=c.param[:, col + k:col + k + 1], in1=self.rstd,
                                               op0=ALU.mult, op1=ALU.mult)
            ins.then_inc(self.scaled, 1)

    def pool(self, pool):
        c = self.c
        for u, (g, kind, _) in enumerate(self.units):
            if kind == "post":
                pool.wait_ge(self.scaled, u + 1)
                pool.tensor_tensor(c.y[:, :, group(g)], c.y[:, :, group(g)], c.acc[:, :, group(g)], ALU.add).then_inc(self.residual_set, 1)
            else:
                pool.wait_ge(self.hi_set, self.count(u, "pre"))
                pool.tensor_tensor(c.lo[:, :, group(g)], c.acc[:, :, group(g)], c.hi[:, :, group(g)].bitcast(F32),
                                   ALU.subtract).then_inc(self.lo_set, 1)


class Split:

    def __init__(self, nc, c, tag):
        self.c = c
        self.hi_set, self.lo_set = nc.alloc_semaphore(f"values_hi_{tag}"), nc.alloc_semaphore(f"values_lo_{tag}")

    def act(self, act):
        for g in range(GROUPS):
            act.copy(self.c.hi[:, :, group(g)], self.c.acc[:, :, group(g)]).then_inc(self.hi_set, 1)

    def pe(self, pe):
        pass

    def dve(self, dve):
        c = self.c
        for g in range(GROUPS):
            dve.wait_ge(self.hi_set, g + 1)
            dve.tensor_tensor(c.lo[:, :, group(g)], c.acc[:, :, group(g)], c.hi[:, :, group(g)].bitcast(F32),
                              ALU.subtract).then_inc(self.lo_set, 1)

    def pool(self, pool):
        pass


def reuse_semaphores(nc, since):
    nc.clear_and_free_semaphores(nc.allocated_since(since))
    nc.all_engine_barrier()


def load_stage(nc, c, t):
    with ExitStack() as ctx:
        sb = lambda n, s, d=F32: ctx.enter_context(nc.sbuf_tensor(n, s, d))
        sem = lambda n: nc.alloc_semaphore(n)
        rows = [sb(f"token_rows{j}", [P, D]) for j in range(2)]
        tail_rows = sb("sample_rows", [SAMPLE, D])
        param_rows = sb("param_rows", [PARAM_ROWS, P])
        tap_rows = sb("tap_rows", [TAP_ROWS, P])
        state_a = sb("state_a_rows", [4 * PAD_A, 2, CHAN])
        state_b = sb("state_b_rows", [DEC_BATCH * PAD_B, CHAN])
        bank = [ctx.enter_context(nc.psum_tensor(f"turn{j}", [P, 512], F32)) for j in range(4)]
        landed = [sem("even_rows_landed"), sem("odd_rows_landed")]
        consts_landed, small_landed = sem("consts_landed"), sem("small_landed")
        ones_set = sem("ones_set")
        turned, kept = sem("block_turned"), sem("block_kept")
        small_turned, small_kept = sem("small_turned"), sem("small_kept")
        block = ctx.enter_context(nc.Block())
        x = t["x_prompt"].rearrange("a (n p) d -> (a n) p d", p=P)

        small_out = []
        small_in = []

        def small(b, pieces, dst, view):
            small_in.append((b, pieces))
            small_out.append((dst, b, None, view))

        for half in range(2):
            small(half, [(tail_rows[:, (4 * half + k) * P:(4 * half + k + 1) * P], SAMPLE, k * SAMPLE, SAMPLE) for k in range(4)],
                  c.y[:, 4 * half:4 * half + 4, SEQ:TOKENS],
                  lambda bk: bk[:, 0:4 * SAMPLE].rearrange("p (k n) -> p k n", k=4))
        small(2, [(param_rows[:], PARAM_ROWS, 0, PARAM_ROWS), (tap_rows[:], TAP_ROWS, PARAM_ROWS, TAP_ROWS)],
              c.param[:], lambda bk: bk[:, 0:PARAM_ROWS + TAP_ROWS])
        SA = 4 * PAD_A
        for k in range(CC):
            small(3 if k % 2 == 0 else 0,
                  [(state_a[:, g, k * P:(k + 1) * P], SA, g * SA, SA) for g in range(2)]
                  + [(state_b[:, k * P:(k + 1) * P], DEC_BATCH * PAD_B, 2 * SA, DEC_BATCH * PAD_B)],
                  c.state[:, k, :], lambda bk: bk[:, 0:2 * SA + DEC_BATCH * PAD_B])

        @block.sync
        def _(sp):
            sp.dma_start(c.ident[:], t["ident"]).then_inc(consts_landed, 16)

            def step(i, first):
                for j in range(2):
                    if not first:
                        sp.wait_ge(turned, 4 * i - 2 + 2 * j)
                    sp.dma_start(rows[j][:], x[2 * i + j]).then_inc(landed[j], 16)

            peeled(sp, QT // 2, step)

        @block.scalar
        def _(act):
            act.dma_start(tail_rows[:], t["x_sample"].rearrange("b s d -> (b s) d")).then_inc(small_landed, 16)
            r = 0
            for name, n in (("mix_pre_gain", 16), ("mix_post_gain", 16), ("ffn_pre_gain", 16), ("ffn_post_gain", 16)):
                act.dma_start(param_rows[r:r + n, :], t[name].rearrange("l (k p) -> (l k) p", p=P)).then_inc(small_landed, 16)
                r += n
            for name, n in (("conv_b_w", TAPS_B * CC), ):
                act.dma_start(param_rows[r:r + n, :], t[name].rearrange("l w (k p) -> (l w k) p", p=P)).then_inc(small_landed, 16)
                r += n
            for name, n in (("conv_a_b", CC), ("ln_a_gain", CC), ("ln_a_bias", CC), ("q_norm_gain", QC), ("kv_norm_gain", LC)):
                act.dma_start(param_rows[r:r + n, :], t[name].rearrange("l (k p) -> (l k) p", p=P)).then_inc(small_landed, 16)
                r += n
            act.dma_start(tap_rows[:], t["conv_a_w"].rearrange("l w (k p) -> (l w k) p", p=P)).then_inc(small_landed, 16)
            act.dma_start(state_a[:], t["state_conv_a"].rearrange("l b w c -> (l b w) c").rearrange(
                "(g r) c -> r g c", g=2)).then_inc(small_landed, 16)
            act.dma_start(state_b[:], t["state_conv_b"].rearrange("l b w c -> (l b w) c")).then_inc(small_landed, 16)

            def step(i, first):
                for j in range(2):
                    act.wait_ge(turned, 4 * i + 2 * j + 2)
                    act.copy(c.y[:, 4:8, bass.ts(2 * i + j, P)],
                             bank[2 * j + 1][:].rearrange("p (k n) -> p k n", k=4)).then_inc(kept, 1)

            peeled(act, QT // 2, step)

        @block.gpsimd
        def _(pool):
            pool.memset(c.ones[:], 1.0).then_inc(ones_set, 1)

        @block.vector
        def _(dve):
            def step(i, first):
                for j in range(2):
                    dve.wait_ge(turned, 4 * i + 2 * j + 1)
                    dve.tensor_copy(c.y[:, 0:4, bass.ts(2 * i + j, P)],
                                    bank[2 * j][:].rearrange("p (k n) -> p k n", k=4)).then_inc(small_kept, 1)

            peeled(dve, QT // 2, step)
            for n, (dst, b, w, v) in enumerate(small_out):
                dve.wait_ge(small_turned, n + 1)
                dve.tensor_copy(dst, v(bank[b])).then_inc(small_kept, 1)

        @block.tensor
        def _(pe):
            pe.wait_ge(consts_landed, 16)

            def step(i, first):
                for j in range(2):
                    pe.wait_ge(landed[j], 16 * i + 16)
                    for half in range(2):
                        if not first:
                            if half == 0:
                                pe.wait_ge(small_kept, 2 * i + j - 1)
                            else:
                                pe.wait_ge(kept, 2 * i + j - 1)
                        for k in range(4):
                            mm = pe.transpose(bank[2 * j + half][:, k * P:(k + 1) * P],
                                              rows[j][:, (4 * half + k) * P:(4 * half + k + 1) * P], c.ident[:])
                        mm.then_inc(turned, 1)

            peeled(pe, QT // 2, step)
            pe.wait_ge(small_landed, 16 * 14)
            pe.wait_ge(kept, QT)
            for n, (b, pieces) in enumerate(small_in):
                pe.wait_ge(small_kept, QT + max(0, n - 1))
                for src, k_rows, at, width in pieces:
                    mm = pe.transpose(bank[b][:, at:at + width], src, c.ident[0:k_rows, 0:k_rows])
                mm.then_inc(small_turned, 1)


def norm_stage(nc, c, tag, rounds):
    R = len(rounds)
    with ExitStack() as ctx:
        sb = lambda n, s, d=F32: ctx.enter_context(nc.sbuf_tensor(f"{n}_{tag}", s, d))
        sem = lambda n: nc.alloc_semaphore(f"{n}_{tag}")
        most = max(r[1] for r in rounds)
        squares = sb("squares", [P, most, GW])
        mean = sb("mean_square", [P, GW])
        root = sb("root", [P, GW])
        rstd = sb("rstd", [P, GW])
        total = ctx.enter_context(nc.psum_tensor(f"total_{tag}", [P, GW], F32))
        squared, summed = sem("squared"), sem("summed")
        mean_set, root_set, rstd_set = sem("mean_set"), sem("root_set"), sem("rstd_set")
        scaled, applied = sem("scaled"), sem("applied")
        n_scaled = sum(r[1] for r in rounds if r[4] is not None)
        block = ctx.enter_context(nc.Block())

        @block.scalar
        def _(act):
            def step(g, first):
                for j, (src, chunks, col, dst, res) in enumerate(rounds):
                    if j or not first:
                        act.wait_ge(summed, g * R + j)
                    if j:
                        act.wait_ge(applied, g * R + j)
                    act.activation(squares[:, 0:chunks, :], src[:, 0:chunks, bass.ts(g, GW)],
                                   ACT.Square).then_inc(squared, 1)
                    act.wait_ge(mean_set, g * R + j + 1)
                    act.activation(root[:], mean[:], ACT.Sqrt).then_inc(root_set, 1)

            peeled(act, GROUPS, step)

        @block.tensor
        def _(pe):
            def step(g, first):
                for j, (src, chunks, col, dst, res) in enumerate(rounds):
                    pe.wait_ge(squared, g * R + j + 1)
                    if j or not first:
                        pe.wait_ge(mean_set, g * R + j)
                    for k in range(chunks):
                        mm = pe.matmul(total[:], c.ones[:], squares[:, k, :], start=(k == 0), stop=(k == chunks - 1))
                    mm.then_inc(summed, 1)

            peeled(pe, GROUPS, step)

        @block.vector
        def _(dve):
            def step(g, first):
                n = 0
                for j, (src, chunks, col, dst, res) in enumerate(rounds):
                    now = bass.ts(g, GW)
                    dve.wait_ge(summed, g * R + j + 1)
                    if j or not first:
                        dve.wait_ge(root_set, g * R + j)
                    dve.tensor_scalar(mean[:], total[:], 1.0 / (chunks * P), RMS_EPS, ALU.mult, ALU.add).then_inc(mean_set, 1)
                    dve.wait_ge(root_set, g * R + j + 1)
                    dve.reciprocal(rstd[:], root[:]).then_inc(rstd_set, 1)
                    dve.wait_ge(rstd_set, g * R + j + 1)
                    for k in range(chunks):
                        ins = dve.scalar_tensor_tensor(out=(dst if res is None else src)[:, k, now], in0=src[:, k, now],
                                                       scalar=c.param[:, col + k:col + k + 1], in1=rstd[:],
                                                       op0=ALU.mult, op1=ALU.mult)
                        if res is not None:
                            ins.then_inc(scaled, 1)
                            n += 1
                    if res is not None:
                        dve.wait_ge(scaled, g * n_scaled + n)
                        ins = dve.tensor_tensor(res[:, 0:chunks, now], res[:, 0:chunks, now], src[:, 0:chunks, now], ALU.add)
                    ins.then_inc(applied, 1)
                    if res is not None and j + 1 < R:
                        dve.wait_ge(applied, g * R + j + 1)

            peeled(dve, GROUPS, step)


def project_stage(nc, c, tag, w, widths, dst, norm=None, split=False, twice=False):
    pairs = (len(widths) - twice) // 2
    with ExitStack() as ctx:
        sem = lambda n: nc.alloc_semaphore(f"{n}_{tag}")
        sb = lambda n, d: [ctx.enter_context(nc.sbuf_tensor(f"{n}{j}_{tag}", [P, DC, P], d)) for j in range(2)]
        raw, w_hi, w_lo = sb("raw", F32), sb("w_hi", F32R), sb("w_lo", F32R)
        bank = [[ctx.enter_context(nc.psum_tensor(f"out{j}{g}_{tag}", [P, GW], F32)) for g in range(GROUPS)] for j in range(2)]
        norm = Split(nc, c, tag) if split else norm and Norm(nc, ctx, c, tag, **norm)
        landed = [sem(f"weights{j}_landed") for j in range(2)]
        hi_set = [sem(f"weights{j}_hi") for j in range(2)]
        lo_set = [sem(f"weights{j}_lo") for j in range(2)]
        done = [sem(f"product{j}_done") for j in range(2)]
        kept = [sem(f"product{j}_kept") for j in range(2)]
        block = ctx.enter_context(nc.Block())
        w_view = w.rearrange("(k p) n -> p k n", p=P)
        tail = [(j, x) for j, x in enumerate(widths[2 * pairs:])]

        def tiles(eng, one, after_first=lambda: None):
            def step(q, first):
                for j in range(2):
                    one(q, j, P, first)

            step(0, True)
            after_first()
            with eng.Fori(1, pairs) as q:
                step(q, False)
            for j, width in tail:
                one(pairs, j, width, False, twice and j == len(tail) - 1)

        @block.sync
        def _(sp):
            def load(q, j, width, first, double=False):
                if not first:
                    sp.wait_ge(lo_set[j], q)
                if double:
                    for i in range(2):
                        sp.dma_start(raw[j][:, :, i * ROPE:(i + 1) * ROPE], w_view[:, :, bass.ds((2 * q + j) * P, ROPE)]).then_inc(landed[j], 16)
                else:
                    sp.dma_start(raw[j][:, :, 0:width], w_view[:, :, bass.ds((2 * q + j) * P, width)]).then_inc(landed[j], 16)

            tiles(sp, load)

        @block.scalar
        def _(act):
            def round_hi(q, j, width, first, double=False):
                act.wait_ge(landed[j], 16 * q + (32 if double else 16))
                if not first:
                    act.wait_ge(done[j], 3 * q)
                act.copy(w_hi[j][:, :, 0:width], raw[j][:, :, 0:width]).then_inc(hi_set[j], 1)

            tiles(act, round_hi, lambda: norm and norm.act(act))

        @block.gpsimd
        def _(pool):
            def rest(q, j, width, first, double=False):
                pool.wait_ge(hi_set[j], q + 1)
                pool.tensor_tensor(w_lo[j][:, :, 0:width], raw[j][:, :, 0:width], w_hi[j][:, :, 0:width].bitcast(F32),
                                   ALU.subtract).then_inc(lo_set[j], 1)

            tiles(pool, rest, lambda: norm and norm.pool(pool))

        @block.tensor
        def _(pe):
            if norm:
                norm.pe(pe)

            def product(q, j, width, first, double=False):
                pe.wait_ge(lo_set[j], q + 1)
                for g in range(GROUPS):
                    if not first:
                        pe.wait_ge(kept[j], 3 * q - 2 + g)
                    elif norm and j == 0:
                        pe.wait_ge(norm.lo_set, g + 1)
                    split_product(pe, bank[j][g][0:width, :], lambda k: w_hi[j][:, k, 0:width], lambda k: w_lo[j][:, k, 0:width],
                                  lambda k: c.hi[:, k, group(g)], lambda k: c.lo[:, k, group(g)], DC).then_inc(done[j], 1)

            tiles(pe, product)

        @block.vector
        def _(dve):
            if norm:
                norm.dve(dve)
                dve.wait_ge(norm.lo_set, GROUPS)

            def keep(q, j, width, first, double=False):
                for g in range(GROUPS):
                    dve.wait_ge(done[j], 3 * q + g + 1)
                    dve.tensor_copy(dst[0:width, 2 * q + j, group(g)], bank[j][g][0:width, :]).then_inc(kept[j], 1)

            tiles(dve, keep)


def conv_stage(nc, c, t, mix):
    A_GATE, A_VAL, B_GATE, C_GATE, B_IN = range(5)
    column = {A_VAL: 0, A_GATE: 1, B_GATE: 2, C_GATE: 3, B_IN: 4}
    with ExitStack() as ctx:
        sb = lambda n, s, d=F32: ctx.enter_context(nc.sbuf_tensor(n, s, d))
        sem = lambda n: nc.alloc_semaphore(n)
        SLOT = (0, 1, 0, 1, 2)
        raw, w_hi, w_lo = ([sb(f"{n}{j}", [P, DC, P], d) for j in range(3)] for n, d in (("raw_in", F32), ("w_in_hi", F32R), ("w_in_lo", F32R)))
        gates = sb("gates", [P, 4 * TOKENS])[:]
        sig, bg, cg, bi = (gates[:, j * TOKENS:(j + 1) * TOKENS] for j in range(4))
        apad = sb("a_prompt", [P, PAD_A + SEQ])
        apad_s = sb("a_sample", [P, DEC_BATCH, PAD_A + DEC_SEQ])
        zpad = sb("z_prompt", [P, PAD_B + SEQ])
        zpad_s = sb("z_sample", [P, DEC_BATCH, PAD_B + DEC_SEQ])
        bank = [[ctx.enter_context(nc.psum_tensor(f"proj{j}{g}", [P, GW], F32)) for g in range(GROUPS)] for j in range(2)]
        landed = [sem(f"w_in{s}_landed") for s in range(5)]
        done, act_kept, glu_done = sem("projection_done"), sem("act_kept"), sem("glu_done")
        z_done, b_done = sem("z_done"), sem("b_conv_done")
        tap, tap_b = sem("tap_added"), sem("tap_b_added")
        state_set, pads_zero, tails_kept = sem("state_set"), sem("pads_zero"), sem("tails_kept")
        hi_set, lo_set = [sem(f"w_in{s}_hi") for s in range(5)], [sem(f"w_in{s}_lo") for s in range(5)]
        norm = Norm(nc, ctx, c, "mix0", pre=ROW_MIX_PRE, space=gates[:, 0:Norm.SPACE])
        block = ctx.enter_context(nc.Block())
        w_view = t["w_in_conv"].rearrange("l (k p) n -> p (l k) n", p=P)
        LAST = SEQ - (GROUPS - 1) * GW
        TA, TB_ = 2 * TAPS_A, 2 * TAPS_B

        @block.sync
        def _(sp):
            def step(i, first):
                for s in range(5):
                    if s in (B_GATE, C_GATE):
                        sp.wait_ge(lo_set[s - 2], i + 1)
                    elif not first:
                        sp.wait_ge(lo_set[s + 2 if s < 2 else s], i)
                    sp.dma_start(raw[SLOT[s]][:], w_view[:, :, bass.ds(column[s] * CHAN + i * P, P)]).then_inc(landed[s], 16)

            for i in range(CC):
                step(i, i == 0)

        @block.tensor
        def _(pe):
            norm.pe(pe)

            def step(i, first):
                for s in range(5):
                    pe.wait_ge(lo_set[s], i + 1)
                    for g in range(GROUPS):
                        if s == 0 and first:
                            pe.wait_ge(norm.lo_set, g + 1)
                        if s == A_GATE and not first:
                            pe.wait_ge(act_kept, 12 * i - 2 + g)
                        if s == A_VAL and not first:
                            pe.wait_ge(act_kept, 12 * i - 5 + g)
                        if s == B_GATE:
                            pe.wait_ge(act_kept, 12 * i + g + 1)
                        if s == C_GATE:
                            pe.wait_ge(glu_done, 4 * i + (g + 1 if g < 2 else 4))
                        if s == B_IN:
                            pe.wait_ge(act_kept, 12 * i + 3 + g + 1)
                        split_product(pe, bank[s % 2][g][:], lambda k: w_hi[SLOT[s]][:, k, :], lambda k: w_lo[SLOT[s]][:, k, :],
                                      lambda k: c.hi[:, k, group(g)], lambda k: c.lo[:, k, group(g)], DC).then_inc(done, 1)

            peeled(pe, CC, step)

        @block.scalar
        def _(act):
            def round_hi(i, s, first):
                act.wait_ge(landed[s], 16 * i + 16)
                if s in (B_GATE, C_GATE):
                    act.wait_ge(done, 15 * i + 3 * (s - 2) + 3)
                elif not first:
                    act.wait_ge(done, 15 * i - 15 + 3 * (s + 2 if s < 2 else s) + 3)
                act.copy(w_hi[SLOT[s]][:], raw[SLOT[s]][:]).then_inc(hi_set[s], 1)

            def keep(i, s, out, func, first):
                for g in range(GROUPS):
                    act.wait_ge(done, 15 * i + 3 * s + g + 1)
                    if not first and g == 0:
                        if s == A_GATE:
                            act.wait_ge(glu_done, 4 * i)
                        elif s == B_GATE:
                            act.wait_ge(b_done, i)
                        else:
                            act.wait_ge(z_done, 4 * i)
                    act.activation(out[:, group(g)], bank[s % 2][g][:], func).then_inc(act_kept, 1)

            def step(i, first, last):
                keep(i, A_GATE, sig, ACT.Sigmoid, first)
                round_hi(i, B_GATE, first)
                round_hi(i, C_GATE, first)
                keep(i, B_GATE, bg, ACT.Copy, first)
                keep(i, C_GATE, cg, ACT.Copy, first)
                if not last:
                    round_hi(i + 1, A_GATE, False)
                    round_hi(i + 1, A_VAL, False)
                keep(i, B_IN, bi, ACT.Copy, first)
                if not last:
                    round_hi(i + 1, B_IN, False)

            for s in (A_GATE, A_VAL, B_IN):
                round_hi(0, s, True)
            norm.act(act)
            three_ends(act, CC, step)

        @block.gpsimd
        def _(pool):
            pool.memset(apad[:, 0:PAD_A], 0.0).then_inc(pads_zero, 1)
            pool.memset(zpad[:, 0:PAD_B], 0.0).then_inc(pads_zero, 1)
            SA = DEC_BATCH * PAD_A

            def rest(i, s):
                pool.wait_ge(hi_set[s], i + 1)
                pool.tensor_tensor(w_lo[SLOT[s]][:], raw[SLOT[s]][:], w_hi[SLOT[s]][:].bitcast(F32), ALU.subtract).then_inc(lo_set[s], 1)

            def step(i, first, last):
                if not first:
                    pool.wait_ge(tails_kept, i)
                    pool.wait_ge(tap, TA * i)
                    pool.wait_ge(b_done, i)
                pool.tensor_copy(apad_s[:, :, 0:PAD_A],
                                 c.state[:, i, 0:SA].rearrange("p (b w) -> p b w", b=DEC_BATCH)).then_inc(state_set, 1)
                pool.tensor_copy(zpad_s[:, :, 0:PAD_B],
                                 c.state[:, i, SA:SA + DEC_BATCH * PAD_B].rearrange("p (b w) -> p b w", b=DEC_BATCH)
                                 ).then_inc(state_set, 1)
                rest(i, B_GATE)
                rest(i, C_GATE)
                pool.wait_ge(glu_done, 4 * i + 4)
                pool.wait_ge(state_set, 2 * i + 2)
                pool.tensor_copy(c.tails[:, i, 0:PAD_A], apad[:, SEQ:SEQ + PAD_A])
                pool.tensor_copy(c.tails[:, i, PAD_A:PAD_A + SA].rearrange("p (b w) -> p b w", b=DEC_BATCH),
                                 apad_s[:, :, DEC_SEQ:DEC_SEQ + PAD_A])
                if not last:
                    for s in (A_GATE, A_VAL, B_IN):
                        rest(i + 1, s)
                pool.wait_ge(z_done, 4 * i + 4)
                o = PAD_A + SA
                pool.tensor_copy(c.tails[:, i, o:o + PAD_B], zpad[:, SEQ:SEQ + PAD_B])
                pool.tensor_copy(c.tails[:, i, o + PAD_B:o + PAD_B + DEC_BATCH * PAD_B].rearrange("p (b w) -> p b w", b=DEC_BATCH),
                                 zpad_s[:, :, DEC_SEQ:DEC_SEQ + PAD_B]).then_inc(tails_kept, 1)

            for s in (A_GATE, A_VAL, B_IN):
                rest(0, s)
            norm.pool(pool)
            three_ends(pool, CC, step)

        @block.vector
        def _(dve):
            def steps_view(x):
                return x.rearrange("p (b s) -> p b s", b=DEC_BATCH)

            norm.dve(dve)

            def step(i, first):
                if first:
                    dve.wait_ge(pads_zero, 2)
                    dve.wait_ge(norm.lo_set, GROUPS)
                else:
                    dve.wait_ge(tails_kept, i)
                for g in range(GROUPS):
                    dve.wait_ge(done, 15 * i + 3 * A_VAL + g + 1)
                    dve.wait_ge(act_kept, 12 * i + g + 1)
                    n = GW if g < GROUPS - 1 else LAST
                    dve.tensor_tensor(apad[:, PAD_A + g * GW:PAD_A + g * GW + n], bank[A_VAL % 2][g][:, 0:n],
                                      sig[:, g * GW:g * GW + n], ALU.mult).then_inc(glu_done, 1)
                dve.tensor_tensor(apad_s[:, :, PAD_A:], steps_view(bank[A_VAL % 2][GROUPS - 1][:, LAST:]),
                                  steps_view(sig[:, SEQ:]), ALU.mult).then_inc(glu_done, 1)
                dve.wait_ge(glu_done, 4 * i + 4)
                dve.wait_ge(state_set, 2 * i + 2)
                for w in range(TAPS_A):
                    wcol = c.param[:, bass.ds(PARAM_ROWS + w * CC + i, 1)]
                    for part, (src, out) in enumerate(((apad[:, w:w + SEQ], mix[:, i, 0:SEQ]),
                                                       (apad_s[:, :, w:w + DEC_SEQ], steps_view(mix[:, i, SEQ:TOKENS])))):
                        if w == 0:
                            dve.tensor_scalar(out, src, wcol, c.param[:, bass.ds(ROW_BIAS_A + i, 1)],
                                              ALU.mult, ALU.add).then_inc(tap, 1)
                        else:
                            dve.wait_ge(tap, TA * i + 2 * w + part - 1)
                            dve.scalar_tensor_tensor(out=out, in0=src, scalar=wcol, in1=out,
                                                     op0=ALU.mult, op1=ALU.add).then_inc(tap, 1)
                dve.wait_ge(act_kept, 12 * i + 12)
                for g in range(GROUPS):
                    n = GW if g < GROUPS - 1 else LAST
                    dve.tensor_tensor(zpad[:, PAD_B + g * GW:PAD_B + g * GW + n], cg[:, g * GW:g * GW + n],
                                      bi[:, g * GW:g * GW + n], ALU.mult).then_inc(z_done, 1)
                dve.tensor_tensor(zpad_s[:, :, PAD_B:], steps_view(cg[:, SEQ:]), steps_view(bi[:, SEQ:]),
                                  ALU.mult).then_inc(z_done, 1)
                dve.wait_ge(z_done, 4 * i + 4)
                for w in range(TAPS_B):
                    wcol = c.param[:, bass.ds(ROW_CONV_B + w * CC + i, 1)]
                    for part, (src, out) in enumerate(((zpad[:, w:w + SEQ], mix[:, CC + i, 0:SEQ]),
                                                       (zpad_s[:, :, w:w + DEC_SEQ], steps_view(mix[:, CC + i, SEQ:TOKENS])))):
                        if w == 0:
                            dve.tensor_scalar(out, src, wcol, None, ALU.mult).then_inc(tap_b, 1)
                        else:
                            dve.wait_ge(tap_b, TB_ * i + 2 * w + part - 1)
                            dve.scalar_tensor_tensor(out=out, in0=src, scalar=wcol, in1=out,
                                                     op0=ALU.mult, op1=ALU.add).then_inc(tap_b, 1)
                dve.wait_ge(tap_b, TB_ * i + TB_)
                dve.tensor_tensor(mix[:, CC + i, :], mix[:, CC + i, :], bg, ALU.mult).then_inc(b_done, 1)

            peeled(dve, CC, step)


def conv_norm_stage(nc, c, t, mix):
    SA = DEC_BATCH * PAD_A
    HALF = SA // 2
    with ExitStack() as ctx:
        sb = lambda n, s, d=F32: ctx.enter_context(nc.sbuf_tensor(n, s, d))
        sem = lambda n: nc.alloc_semaphore(n)
        squares = sb("ln_squares", [P, CC, GW])
        mean, var, root, rstd = (sb(n, [P, GW]) for n in ("ln_mean", "ln_var", "ln_root", "ln_rstd"))
        total, total2 = (ctx.enter_context(nc.psum_tensor(n, [P, GW], F32)) for n in ("ln_total", "ln_total2"))
        bank = [ctx.enter_context(nc.psum_tensor(f"state_out{j}", [P, 512], F32)) for j in range(5)]
        out_ap, out_bp = sb("new_a_prompt", [PAD_A, CHAN]), sb("new_b_prompt", [PAD_B, CHAN])
        out_as = sb("new_a_sample", [HALF, 2, CHAN])
        out_bs = sb("new_b_sample", [DEC_BATCH * PAD_B, CHAN])
        summed, mean_set, centred, squared = sem("ln_summed"), sem("ln_mean_set"), sem("ln_centred"), sem("ln_squared")
        summed2, var_set, root_set, rstd_set, scaled = (sem(n) for n in ("ln_summed2", "ln_var_set", "ln_root_set", "ln_rstd_set", "ln_scaled"))
        hi_set, lo_set = sem("mixed_hi"), sem("mixed_lo")
        silu_done, turned, kept, stored = sem("ln_silu_done"), sem("state_turned"), sem("state_kept"), sem("state_stored")
        block = ctx.enter_context(nc.Block())
        pieces = [(0, PAD_A, out_ap[:]), (PAD_A, HALF, out_as[:, 0, :]), (PAD_A + HALF, HALF, out_as[:, 1, :]),
                  (PAD_A + SA, PAD_B, out_bp[:]), (PAD_A + SA + PAD_B, DEC_BATCH * PAD_B, out_bs[:])]

        @block.tensor
        def _(pe):
            for n, (at, width, out) in enumerate(pieces):
                for k in range(CC):
                    mm = pe.transpose(bank[n][0:width, k * P:(k + 1) * P], c.tails[:, k, at:at + width], c.ident[:])
                mm.then_inc(turned, 1)
            def step(g, first):
                if not first:
                    pe.wait_ge(mean_set, g)
                for k in range(CC):
                    mm = pe.matmul(total[:], c.ones[:], mix[:, k, bass.ts(g, GW)], start=(k == 0), stop=(k == CC - 1))
                mm.then_inc(summed, 1)
                pe.wait_ge(squared, g + 1)
                for k in range(CC):
                    mm = pe.matmul(total2[:], c.ones[:], squares[:, k, :], start=(k == 0), stop=(k == CC - 1))
                mm.then_inc(summed2, 1)

            peeled(pe, GROUPS, step)

        @block.scalar
        def _(act):
            def step(g, first):
                act.wait_ge(centred, 4 * g + 4)
                act.activation(squares[:], mix[:, 0:CC, bass.ts(g, GW)], ACT.Square).then_inc(squared, 1)
                act.wait_ge(var_set, g + 1)
                act.activation(root[:], var[:], ACT.Sqrt).then_inc(root_set, 1)

            peeled(act, GROUPS, step)
            def step(g, first):
                act.wait_ge(scaled, 4 * g + 4)
                for k in range(CC):
                    act.activation(mix[:, k, bass.ts(g, GW)], mix[:, k, bass.ts(g, GW)], ACT.Silu,
                                   bias=c.param[:, ROW_LN_B + k:ROW_LN_B + k + 1],
                                   scale=c.param[:, ROW_LN_G + k:ROW_LN_G + k + 1]).then_inc(silu_done, 1)
                act.wait_ge(silu_done, 4 * g + 4)
                act.copy(c.hi[:, :, bass.ts(g, GW)], mix[:, :, bass.ts(g, GW)]).then_inc(hi_set, 1)

            peeled(act, GROUPS, step)

        @block.vector
        def _(dve):
            for n, (at, width, out) in enumerate(pieces):
                dve.wait_ge(turned, n + 1)
                dve.tensor_copy(out, bank[n][0:width, :]).then_inc(kept, 1)
            def step(g, first):
                now = bass.ts(g, GW)
                dve.wait_ge(summed, g + 1)
                dve.tensor_scalar(mean[:], total[:], 1.0 / CHAN, None, ALU.mult).then_inc(mean_set, 1)
                dve.wait_ge(mean_set, g + 1)
                for k in range(CC):
                    dve.tensor_tensor(mix[:, k, now], mix[:, k, now], mean[:], ALU.subtract).then_inc(centred, 1)
                dve.wait_ge(summed2, g + 1)
                dve.tensor_scalar(var[:], total2[:], 1.0 / CHAN, LN_EPS, ALU.mult, ALU.add).then_inc(var_set, 1)
                dve.wait_ge(root_set, g + 1)
                dve.reciprocal(rstd[:], root[:]).then_inc(rstd_set, 1)
                dve.wait_ge(rstd_set, g + 1)
                for k in range(CC):
                    dve.tensor_tensor(mix[:, k, now], mix[:, k, now], rstd[:], ALU.mult).then_inc(scaled, 1)

            peeled(dve, GROUPS, step)
            for g in range(GROUPS):
                dve.wait_ge(hi_set, g + 1)
                dve.tensor_tensor(c.lo[:, :, group(g)], mix[:, :, group(g)], c.hi[:, :, group(g)].bitcast(F32),
                                  ALU.subtract).then_inc(lo_set, 1)

        @block.sync
        def _(sp):
            sp.wait_ge(kept, len(pieces))
            sp.dma_start(t["new_conv_a_prompt"].rearrange("l b w c -> (l b w) c"), out_ap[:]).then_inc(stored, 16)
            a_s = t["new_conv_a_sample"].rearrange("l b w c -> (l b w) c")
            for j in range(2):
                sp.dma_start(a_s[j * HALF:(j + 1) * HALF, :], out_as[:, j, :]).then_inc(stored, 16)
            sp.dma_start(t["new_conv_b_prompt"].rearrange("l b w c -> (l b w) c"), out_bp[:]).then_inc(stored, 16)
            sp.dma_start(t["new_conv_b_sample"].rearrange("l b w c -> (l b w) c"), out_bs[:]).then_inc(stored, 16)
            sp.wait_ge(stored, 80)


def ffn_stage(nc, c, layer, t, norm):
    NB = DC * GROUPS
    with ExitStack() as ctx:
        sb = lambda n, s, d=F32: ctx.enter_context(nc.sbuf_tensor(f"{n}{layer}", s, d))
        sem = lambda n: nc.alloc_semaphore(f"{n}{layer}")
        ps = lambda n, s: ctx.enter_context(nc.psum_tensor(f"{n}{layer}", s, F32))
        names = ("gate", "up", "down")
        raw = {n: sb(f"raw_{n}", [P, DC, P]) for n in names}
        w_hi, w_lo = {n: sb(f"w_{n}_hi", [P, DC, P], F32R) for n in names}, {n: sb(f"w_{n}_lo", [P, DC, P], F32R) for n in names}
        hidden = sb("hidden", [P, TOKENS])
        hid_hi, hid_lo = sb("hidden_hi", [P, TOKENS], F32R), sb("hidden_lo", [P, TOKENS], F32R)
        norm = Norm(nc, ctx, c, f"ffn{layer}", **norm)
        gate_bank = [ps(f"gate_bank{g}_", [P, GW]) for g in range(GROUPS)]
        up_bank = [ps(f"up_bank{g}_", [P, GW]) for g in range(GROUPS)]
        down_bank = [norm.total, ps("down_bank1_", [P, GW])]
        landed, hi_set, lo_set = ({n: sem(f"{n}_{what}") for n in names} for what in ("landed", "hi", "lo"))
        gate_done, up_done, down_done = sem("gate_done"), sem("up_done"), sem("down_done")
        silu_done, hidden_set, hid_hi_set, hid_lo_set = sem("silu_done"), sem("hidden_set"), sem("hidden_hi_set"), sem("hidden_lo_set")
        down_free = sem("down_bank_free")
        block = ctx.enter_context(nc.Block())
        gate_view = t["w_ffn_gate"][layer].rearrange("(k p) f -> p k f", p=P)
        up_view = t["w_ffn_up"][layer].rearrange("(k p) f -> p k f", p=P)
        down_view = t["w_ffn_down"][layer].rearrange("(f p) (k n) -> f p k n", p=P, n=P)

        @block.sync
        def _(sp):
            def load(name, f, src, first):
                if not first:
                    sp.wait_ge(lo_set[name], f)
                sp.dma_start(raw[name][:], src).then_inc(landed[name], 16)

            load("gate", 0, gate_view[:, :, 0:P], True)
            load("up", 0, up_view[:, :, 0:P], True)

            def step(f, first):
                load("gate", f + 1, gate_view[:, :, bass.ds(f * P + P, P)], False)
                load("down", f, down_view[f], first)
                load("up", f + 1, up_view[:, :, bass.ds(f * P + P, P)], False)

            peeled(sp, FC - 1, step)
            load("down", FC - 1, down_view[FC - 1], False)

        @block.tensor
        def _(pe):
            norm.pe(pe)

            def down(f):
                pe.wait_ge(lo_set["down"], f + 1)
                for m in range(DC):
                    for g in range(GROUPS):
                        n = m * GROUPS + g
                        if m == 0:
                            pe.wait_ge(hid_lo_set, 3 * f + g + 1)
                        pe.wait_ge(down_free, NB * f + n + 1)
                        split_product(pe, down_bank[n % 2][:], lambda k: w_hi["down"][:, m, :], lambda k: w_lo["down"][:, m, :],
                                      lambda k: hid_hi[:, group(g)], lambda k: hid_lo[:, group(g)], 1).then_inc(down_done, 1)

            def half(f, first, name, bank, used, done):
                pe.wait_ge(lo_set[name], f + 1)
                for g in range(GROUPS):
                    if not first:
                        pe.wait_ge(used, 3 * f - 2 + g)
                    elif name == "gate":
                        pe.wait_ge(norm.lo_set, g + 1)
                    split_product(pe, bank[g][:], lambda k: w_hi[name][:, k, :], lambda k: w_lo[name][:, k, :],
                                  lambda k: c.hi[:, k, group(g)], lambda k: c.lo[:, k, group(g)], DC).then_inc(done, 1)

            def step(f, first):
                half(f, first, "gate", gate_bank, silu_done, gate_done)
                if not first:
                    down(f - 1)
                half(f, first, "up", up_bank, hidden_set, up_done)

            peeled(pe, FC, step)
            down(FC - 1)

        @block.scalar
        def _(act):
            def round_hi(name, f, left, count):
                act.wait_ge(landed[name], 16 * f + 16)
                if left is not None:
                    act.wait_ge(left, count)
                act.copy(w_hi[name][:], raw[name][:]).then_inc(hi_set[name], 1)

            def step(f, first, last):
                for g in range(GROUPS):
                    act.wait_ge(gate_done, 3 * f + g + 1)
                    if not first:
                        act.wait_ge(hid_lo_set, 3 * f - 2 + g)
                    act.activation(hidden[:, group(g)], gate_bank[g][:], ACT.Silu).then_inc(silu_done, 1)
                if not last:
                    round_hi("gate", f + 1, gate_done, 3 * f + 3)
                round_hi("down", f, None if first else down_done, NB * f)
                for g in range(GROUPS):
                    act.wait_ge(hidden_set, 3 * f + g + 1)
                    act.copy(hid_hi[:, group(g)], hidden[:, group(g)]).then_inc(hid_hi_set, 1)
                if not last:
                    round_hi("up", f + 1, up_done, 3 * f + 3)

            round_hi("gate", 0, None, 0)
            round_hi("up", 0, None, 0)
            norm.act(act)
            three_ends(act, FC, step)

        @block.gpsimd
        def _(pool):
            def rest(name, f):
                pool.wait_ge(hi_set[name], f + 1)
                pool.tensor_tensor(w_lo[name][:], raw[name][:], w_hi[name][:].bitcast(F32), ALU.subtract).then_inc(lo_set[name], 1)

            def step(f, first):
                rest("gate", f + 1)
                rest("down", f)
                rest("up", f + 1)

            rest("gate", 0)
            rest("up", 0)
            norm.pool(pool)
            peeled(pool, FC - 1, step)
            rest("down", FC - 1)

        @block.vector
        def _(dve):
            norm.dve(dve)
            dve.wait_ge(norm.lo_set, GROUPS)
            for j in range(2):
                dve.memset(c.acc[:, j * DC // 2:(j + 1) * DC // 2, :], 0.0).then_inc(down_free, 1)

            def add(f):
                dve.wait_ge(down_free, NB * f + 2)
                for m in range(DC):
                    for g in range(GROUPS):
                        n = m * GROUPS + g
                        dve.wait_ge(down_done, NB * f + n + 1)
                        dve.tensor_tensor(c.acc[:, m, group(g)], c.acc[:, m, group(g)], down_bank[n % 2][:],
                                          ALU.add).then_inc(down_free, 1)

            def step(f, first):
                if not first:
                    add(f - 1)
                for g in range(GROUPS):
                    dve.wait_ge(up_done, 3 * f + g + 1)
                    dve.wait_ge(silu_done, 3 * f + g + 1)
                    dve.tensor_tensor(hidden[:, group(g)], up_bank[g][:], hidden[:, group(g)], ALU.mult).then_inc(hidden_set, 1)
                for g in range(GROUPS):
                    dve.wait_ge(hid_hi_set, 3 * f + g + 1)
                    dve.tensor_tensor(hid_lo[:, group(g)], hidden[:, group(g)], hid_hi[:, group(g)].bitcast(F32),
                                      ALU.subtract).then_inc(hid_lo_set, 1)

            peeled(dve, FC, step)
            add(FC - 1)


def latent_stage(nc, c, t, k):
    with ExitStack() as ctx:
        sb = lambda n, s, d=F32: ctx.enter_context(nc.sbuf_tensor(n, s, d))
        sem = lambda n: nc.alloc_semaphore(n)
        by_cos, by_sin = sb("key_by_cos", [P, GROUPS, GW]), sb("key_by_sin", [P, GROUPS, GW])
        key_rows, latent_rows = sb("key_rows", [P, QT + 1, ROPE]), sb("latent_rows", [P, QT + 1, KV_LORA])
        rot = [ctx.enter_context(nc.psum_tensor(f"key_rotated{g}", [P, GW], F32)) for g in range(GROUPS)]
        bank = [ctx.enter_context(nc.psum_tensor(f"latent_turn{j}", [P, 512], F32)) for j in range(2)]
        consts, rotated, parts, key_set = sem("rope_consts"), sem("key_turned"), sem("key_parts"), sem("key_set")
        turned, kept, stored = sem("latent_turned"), sem("latent_kept"), sem("latent_stored")
        copied, zeroed = sem("sample_keys_copied"), sem("rows_zeroed")
        block = ctx.enter_context(nc.Block())
        raw = c.acc[:, QC + LC, :]

        @block.scalar
        def _(act):
            act.dma_start(k.cos[:], t["rope_cos"]).then_inc(consts, 16)
            act.dma_start(k.sin[:], t["rope_sin"]).then_inc(consts, 16)
            act.dma_start(k.swap[:], t["rope_swap"]).then_inc(consts, 16)
            act.dma_start(k.causal[:], t["causal"]).then_inc(consts, 16)

        @block.tensor
        def _(pe):
            pe.wait_ge(consts, 64)
            for g in range(GROUPS):
                pe.matmul(rot[g][:], k.swap[:], raw[:, group(g)], start=True, stop=True).then_inc(rotated, 1)
            pe.wait_ge(key_set, 2 * GROUPS)
            for i in range(QT + 1):
                if i >= 2:
                    pe.wait_ge(kept, 2 * i - 2)
                width = P if i < QT else SAMPLE
                cols = slice(i * P, i * P + width)
                for l in range(LC):
                    pe.transpose(bank[i % 2][0:width, l * P:(l + 1) * P], k.latent[:, l, cols], c.ident[:])
                pe.transpose(bank[i % 2][0:width, KV_LORA:KV_LORA + ROPE], k.key[0][0:ROPE, cols],
                             c.ident[0:ROPE, 0:ROPE]).then_inc(turned, 1)

        @block.vector
        def _(dve):
            dve.memset(k.key[0][ROPE:P, :], 0.0).then_inc(zeroed, 1)
            dve.memset(k.key[1][0:ROPE, :], 0.0).then_inc(zeroed, 1)
            dve.wait_ge(consts, 64)
            for g in range(GROUPS):
                dve.tensor_tensor(by_cos[:, g, :], raw[:, group(g)], k.cos[:, group(g)], ALU.mult).then_inc(parts, 1)
                dve.wait_ge(rotated, g + 1)
                dve.tensor_tensor(by_sin[:, g, :], rot[g][:], k.sin[:, group(g)], ALU.mult).then_inc(parts, 1)
            for g in range(GROUPS):
                dve.wait_ge(parts, 2 * GROUPS)
                for j in range(2):
                    own = slice(j * ROPE, (j + 1) * ROPE)
                    dve.tensor_tensor(k.key[j][own, group(g)], by_cos[own, g, :], by_sin[own, g, :], ALU.add).then_inc(key_set, 1)
            for i in range(QT + 1):
                dve.wait_ge(turned, i + 1)
                width = P if i < QT else SAMPLE
                dve.tensor_copy(latent_rows[0:width, i, :], bank[i % 2][0:width, 0:KV_LORA]).then_inc(kept, 1)
                dve.tensor_copy(key_rows[0:width, i, :], bank[i % 2][0:width, KV_LORA:KV_LORA + ROPE]).then_inc(kept, 1)
            dve.wait_ge(kept, 2 * QT + 2)
            dve.tensor_copy(c.new_latent[:], k.latent[:, :, SEQ:TOKENS]).then_inc(copied, 1)
            dve.tensor_copy(c.new_key[:], k.key[0][:, SEQ:TOKENS]).then_inc(copied, 1)
            dve.tensor_copy(c.new_rows[:], latent_rows[0:SAMPLE, QT, :]).then_inc(copied, 1)

        @block.sync
        def _(sp):
            sp.wait_ge(kept, 2 * QT + 2)
            sp.dma_start(t["new_kv_latent_prompt"].rearrange("l b (n p) d -> p (l b n) d", p=P), latent_rows[:, 0:QT, :]).then_inc(stored, 16)
            sp.dma_start(t["new_kv_latent_sample"].rearrange("l b s d -> (l b s) d"), latent_rows[0:SAMPLE, QT, :]).then_inc(stored, 16)
            sp.dma_start(t["new_k_rope_prompt"].rearrange("l b (n p) d -> p (l b n) d", p=P), key_rows[:, 0:QT, :]).then_inc(stored, 16)
            sp.dma_start(t["new_k_rope_sample"].rearrange("l b s d -> (l b s) d"), key_rows[0:SAMPLE, QT, :]).then_inc(stored, 16)
            sp.wait_ge(stored, 64)


ORDER = ("S0 M0 E0 S1 M1 E1 N0 F0 F1 S2 M2 T0 N1 E2 F2 S3 M3 T1 N2 E3 F3 S4 M4 T2 N3 E4 F4 S5 M5 T3 N4 E5 P0 O0 "
         "F5 S6 M6 T4 N5 E6 F6 S7 M7 T5 N6 E7 F7 T6 N7 A0 F8 T7 P1 O1").split()
PREPARE = [("QN0", "QN1"), ("QN2", "QR0"), ("KN0", "QR1"), ("KN1", "QR2"), ("SW0", "V0"), ("SW1", "V1"), ("SW2", "UK"), (), ("LAT",)]


def banks_of(i):
    return [list(range(a, min(a + 4, i + 1))) for a in range(0, i + 1, 4)]


def prepare_items(f, pair_first):
    return [x for x in PREPARE[f] if pair_first or x[:2] not in ("QR", "SW")]


def attention_stage(nc, c, t, k, cq):
    with ExitStack() as ctx:
        sb = lambda n, s, d=F32: ctx.enter_context(nc.sbuf_tensor(n, s, d))
        sem = lambda n: nc.alloc_semaphore(n)
        ps = lambda n, s: ctx.enter_context(nc.psum_tensor(n, s, F32))
        two = lambda n, s: [sb(f"{n}{j}", s) for j in range(2)]
        w_qn, w_uk, w_uv = two("w_q_nope", [P, QC, NOPE]), two("w_uk", [P, LC, NOPE]), two("w_uv", [P, LC, VDIM])
        w_qr, w_ukT = sb("w_q_rope", [P, QC, 2, ROPE]), sb("w_uk_turned", [P, LC, P])
        q_nope, q_rope, q_raw, by_sin = [c.acc[:, QC + j, :] for j in range(2)], c.acc[:, QC + 2, :], c.acc[:, QC + 3, :], c.acc[:, QC + 4, :]
        k_nope, v_rows = two("k_nope", [P, SEQ]), two("v_rows", [P, QT, VDIM])
        prob = two("prob", [P, SEQ])
        probT = [sb(f"prob_turned{i}", [P, 4 * (i + 1), 512]) for i in range(2)]
        top, bias, total, inv = (sb(n, [P, QT]) for n in ("row_max", "row_bias", "row_total", "row_inverse"))
        score = [ps(f"score{j}", [P, SEQ]) for j in range(2)]
        sum_bank = [ps(f"sum_bank{j}", [P, 512]) for j in range(2)]
        misc = [ps(f"misc{j}", [P, 512]) for j in range(2)]
        w_landed, w_qr_landed = [sem(f"head_weights{j}_landed") for j in range(2)], sem("rope_weights_landed")
        misc_done, kept = sem("misc_done"), {"act": sem("misc_kept_act"), "dve": sem("misc_kept_dve")}
        sum_done, sum_kept = sem("sum_done"), sem("sum_kept")
        by_cos_set, rope_added, stashed = sem("by_cos_set"), sem("rope_added"), sem("stashed")
        scored, masked, topped, biased = sem("scored"), sem("masked"), sem("topped"), sem("biased")
        exp_done, inverted, prob_set = sem("exp_done"), sem("inverted"), sem("prob_set")
        block = ctx.enter_context(nc.Block())
        PAIRS = HEADS // 2

        def keeper(name):
            return "dve" if name[:2] == "SW" else "act"

        FIRST = [(1, x) for f in range(len(PREPARE)) for x in prepare_items(f, True)]
        PAIR = []
        for j in range(2):
            for what in ORDER:
                if what[0] == "F":
                    PAIR += [(j, x) for x in prepare_items(int(what[1]), j == 1)]
                elif what[0] == "T":
                    PAIR += [(j, f"{what}.{n}") for n in range(len(banks_of(int(what[1]))))]
        LAST = [u for u in PAIR if u[0] == 0 or u[1][0] == "T"]
        assert len(PAIR) % 2 == 0 and all(keeper(u[1]) == "act" for u in FIRST[-2:] + PAIR[-2:])

        class Use:

            def __init__(self, p, j, name):
                self.uses = FIRST if p is None else LAST if isinstance(p, int) and p == PAIRS - 1 else PAIR
                self.p, self.n = p, self.uses.index((j, name))
                self.keeper = keeper(name)
                self.index = self.n if p is None else len(PAIR) * p + len(FIRST) + self.n
                self.bank = misc[(self.n + (0 if p is None else len(FIRST))) % 2]
                self.done = self.index + 1

            def kept_with(self, n, who):
                of = lambda uses: sum(keeper(x) == who for _, x in uses)
                start = 0 if self.p is None else of(PAIR) * self.p + of(FIRST)
                return start + (of(self.uses[:n + 1]) if n >= 0 else -of(PAIR[len(PAIR) + n + 1:]))

            def wait_free(self, pe):
                n = self.n - 2
                if n >= 0 or self.p is not None:
                    who = keeper((self.uses if n >= 0 else PAIR)[n][1])
                    pe.wait_ge(kept[who], self.kept_with(n, who))

            def wait_kept(self, eng):
                eng.wait_ge(kept[self.keeper], self.kept_with(self.n, self.keeper))

        def prepared_in(p, j, first, name):
            if j == 1:
                return Use(p, 0, name)
            return Use(None, 1, name) if first else Use(p - 1, 1, name)

        w_uq = t["w_uq"].rearrange("l (k p) n -> p (l k) n", p=P)
        uk_view = t["w_uk"].rearrange("l (k p) h n -> p (l k) (h n)", p=P)
        uv_view = t["w_uv"].rearrange("l (k p) h n -> p (l k) (h n)", p=P)

        @block.sync
        def _(sp):
            def load_head(h):
                j = h % 2
                if h >= 2:
                    sp.wait_ge(misc_done, prepared_in(h // 2 - 1, j, h == 2, "LAT").done)
                at = h * (NOPE + ROPE)
                sp.dma_start(w_qn[j][:], w_uq[:, :, at:at + NOPE]).then_inc(w_landed[j], 16)
                sp.dma_start(w_uk[j][:], uk_view[:, :, h * NOPE:(h + 1) * NOPE]).then_inc(w_landed[j], 16)
                sp.dma_start(w_uv[j][:], uv_view[:, :, h * VDIM:(h + 1) * VDIM]).then_inc(w_landed[j], 16)
                if j == 0:
                    for i in range(2):
                        at = (h + i) * (NOPE + ROPE) + NOPE
                        sp.dma_start(w_qr[:, :, i, :], w_uq[:, :, at:at + ROPE]).then_inc(w_qr_landed, 16)

            for h in range(HEADS):
                load_head(h)

        @block.tensor
        def _(pe):
            def item(p, j, name, n, s):
                use = Use(p, j, name)
                if name == "QN0":
                    pe.wait_ge(w_landed[s], 48 * n + 48)
                if name == "QR0":
                    pe.wait_ge(w_qr_landed, 32 * n + 32)
                if name == "LAT":
                    Use(p, j, "UK").wait_kept(pe)
                if name[:2] == "SW":
                    Use(p, j, "QR" + name[2]).wait_kept(pe)
                use.wait_free(pe)
                b, g = use.bank, int(name[-1]) if name[-1].isdigit() else 0
                if name[:2] in ("QN", "QR"):
                    for i in range(QC):
                        w = w_qn[s][:, i, :] if name[1] == "N" else w_qr[:, i].rearrange("p j n -> p (j n)")
                        mm = pe.matmul(b[:, 0:GW], w, cq[:, i, group(g)], start=(i == 0), stop=(i == QC - 1))
                elif name[:2] == "SW":
                    mm = pe.matmul(b[:, 0:GW], k.swap[:], q_raw[:, group(g)], start=True, stop=True)
                elif name[:2] == "KN":
                    for l in range(LC):
                        mm = pe.matmul(b[:], w_uk[s][:, l, :], k.latent[:, l, g * 512:(g + 1) * 512], start=(l == 0), stop=(l == LC - 1))
                elif name[0] == "V":
                    for i in range(4):
                        keys = slice((4 * g + i) * P, (4 * g + i + 1) * P)
                        for l in range(LC):
                            mm = pe.matmul(b[:, i * P:(i + 1) * P], k.latent[:, l, keys], w_uv[s][:, l, :], start=(l == 0), stop=(l == LC - 1))
                elif name == "UK":
                    for l in range(LC):
                        mm = pe.transpose(b[:, l * P:(l + 1) * P], w_uk[s][:, l, :], c.ident[:])
                else:
                    for l in range(LC):
                        mm = pe.matmul(b[:, l * SAMPLE:(l + 1) * SAMPLE], w_ukT[:, l, :], q_nope[s][:, SEQ:TOKENS], start=True, stop=True)
                mm.then_inc(misc_done, 1)

            def head(p, j, first, last):
                prepared_in(p, j, first, "LAT").wait_kept(pe)
                if j == 0:
                    pe.wait_ge(rope_added, p + 1)
                n = 2 * QT * p + QT * j
                for what in ORDER:
                    i = int(what[1])
                    if what[0] == "S":
                        if not (first and j == 0 and i < 2):
                            pe.wait_ge(exp_done, n + i - 1)
                        q = slice(i * P, (i + 1) * P)
                        for a in range(0, (i + 1) * P, 512):
                            keys = slice(a, min(a + 512, (i + 1) * P))
                            pe.matmul(score[i % 2][:, keys], q_nope[j][:, q], k_nope[j][:, keys], start=True, stop=False)
                            mm = pe.matmul(score[i % 2][:, keys], q_rope[:, q], k.key[j][:, keys], start=False, stop=True)
                        mm.then_inc(scored, 1)
                    elif what[0] == "T":
                        pe.wait_ge(prob_set, n + i + 1)
                        for m, tiles in enumerate(banks_of(i)):
                            use = Use(p, j, f"{what}.{m}")
                            use.wait_free(pe)
                            for x, kt in enumerate(tiles):
                                mm = pe.transpose(use.bank[:, x * P:(x + 1) * P], prob[i % 2][:, kt * P:(kt + 1) * P], c.ident[:])
                            mm.then_inc(misc_done, 1)
                    elif what[0] == "P":
                        Use(p, j, f"T{4 * i + 3}.{i}").wait_kept(pe)
                        if not (first and j == 0):
                            pe.wait_ge(sum_kept, 4 * p + 2 * j + i - 1)
                        tiles = 4 * (i + 1)
                        for kt in range(tiles):
                            q0 = max(kt - 4 * i, 0) * P
                            mm = pe.matmul(sum_bank[i][:, q0:512], v_rows[j][:, kt, :], probT[i][:, kt, q0:512],
                                           start=(kt == 0), stop=(kt == tiles - 1))
                        mm.then_inc(sum_done, 1)
                    elif what[0] == "F" and not (last and j == 1):
                        for name in prepare_items(i, j == 1):
                            item(p, j, name, p + j, 1 - j)

            for _, name in FIRST:
                item(None, 1, name, 0, 0)

            def pair(p, first, last):
                for j in range(2):
                    head(p, j, first, last)

            three_ends(pe, PAIRS, pair)

        @block.scalar
        def _(act):
            def item(p, j, name, n, s, first):
                use = Use(p, j, name)
                if use.keeper != "act":
                    return
                b, g = use.bank, int(name[-1]) if name[-1].isdigit() else 0
                act.wait_ge(misc_done, use.done)
                if name == "QR0" and not first:
                    act.wait_ge(rope_added, n)
                if name[:2] in ("QN", "QR"):
                    dst, src = (q_nope[s] if name[1] == "N" else q_raw)[:, group(g)], b[:, 0:GW]
                elif name[:2] == "KN":
                    dst, src = k_nope[s][:, g * 512:(g + 1) * 512], b[:]
                elif name[0] == "V":
                    dst, src = v_rows[s][:, 4 * g:4 * g + 4, :], b[:].rearrange("p (k n) -> p k n", k=4)
                elif name == "UK":
                    dst, src = w_ukT[:], b[:, 0:LC * P].rearrange("p (l n) -> p l n", l=LC)
                else:
                    dst = c.q_lat_s[:, :, bass.ds(2 * n + s, 1), :].rearrange("p l h n -> p l (h n)")
                    src = b[:, 0:LC * SAMPLE].rearrange("p (l n) -> p l n", l=LC)
                act.copy(dst, src).then_inc(kept["act"], 1)

            def pair(p, first, last):
                for j in range(2):
                    for what in ORDER:
                        i = int(what[1])
                        if what[0] == "E":
                            act.wait_ge(biased, 2 * QT * p + QT * j + i + 1)
                            act.activation(prob[i % 2][:, 0:(i + 1) * P], score[i % 2][:, 0:(i + 1) * P], ACT.Exp,
                                           bias=bias[:, i:i + 1], scale=SM_SCALE, accum_out=total[:, i:i + 1]).then_inc(exp_done, 1)
                        elif what[0] == "T":
                            for m, tiles in enumerate(banks_of(i)):
                                use, n = Use(p, j, f"{what}.{m}"), len(tiles)
                                act.wait_ge(misc_done, use.done)
                                act.copy(probT[i // 4][:, tiles[0]:tiles[0] + n, (i % 4) * P:(i % 4 + 1) * P],
                                         use.bank[:, 0:n * P].rearrange("p (n q) -> p n q", n=n)).then_inc(kept["act"], 1)
                        elif what[0] == "F" and not (last and j == 1):
                            for name in prepare_items(i, j == 1):
                                item(p, j, name, p + j, 1 - j, False)

            for _, name in FIRST:
                item(None, 1, name, 0, 0, True)
            three_ends(act, PAIRS, pair)

        @block.vector
        def _(dve):
            def rotate(p, name, n, first):
                use, g = Use(p, 1, name), int(name[2])
                dve.wait_ge(misc_done, use.done)
                if g == 0 and not first:
                    dve.wait_ge(rope_added, n)
                dve.tensor_tensor(by_sin[:, group(g)], use.bank[:, 0:GW], k.sin[:, group(g)], ALU.mult).then_inc(kept["dve"], 1)
                dve.tensor_tensor(q_raw[:, group(g)], q_raw[:, group(g)], k.cos[:, group(g)], ALU.mult).then_inc(by_cos_set, 1)

            def add(n):
                dve.wait_ge(kept["dve"], GROUPS * n + GROUPS)
                dve.wait_ge(by_cos_set, GROUPS * n + GROUPS)
                dve.tensor_tensor(q_rope, q_raw, by_sin, ALU.add).then_inc(rope_added, 1)
                dve.wait_ge(rope_added, n + 1)
                dve.tensor_copy(c.q_rope_s[:, bass.ds(n, 1), :].rearrange("p h n -> p (h n)"), q_rope[:, SEQ:TOKENS]).then_inc(stashed, 1)

            def pair(p, first, last):
                for j in range(2):
                    base = 2 * QT * p + QT * j
                    for what in ORDER:
                        i = int(what[1])
                        n = base + i + 1
                        if what[0] == "M":
                            dve.wait_ge(scored, n)
                            own = slice(i * P, (i + 1) * P)
                            dve.tensor_tensor(score[i % 2][:, own], score[i % 2][:, own], k.causal[:], ALU.add).then_inc(masked, 1)
                            dve.wait_ge(masked, n)
                            dve.tensor_reduce(top[:, i:i + 1], score[i % 2][:, 0:(i + 1) * P], AX_X, ALU.max).then_inc(topped, 1)
                            dve.wait_ge(topped, n)
                            dve.tensor_scalar(bias[:, i:i + 1], top[:, i:i + 1], -SM_SCALE, None, ALU.mult).then_inc(biased, 1)
                        elif what[0] == "N":
                            dve.wait_ge(exp_done, n)
                            dve.reciprocal(inv[:, i:i + 1], total[:, i:i + 1]).then_inc(inverted, 1)
                            dve.wait_ge(inverted, n)
                            dve.tensor_scalar(prob[i % 2][:, 0:(i + 1) * P], prob[i % 2][:, 0:(i + 1) * P], inv[:, i:i + 1], None,
                                              ALU.mult).then_inc(prob_set, 1)
                        elif what[0] == "O":
                            dve.wait_ge(sum_done, 4 * p + 2 * j + i + 1)
                            dve.tensor_copy(c.value[:, bass.ds(2 * p + j, 1), i * 512:(i + 1) * 512].rearrange("p h n -> p (h n)"),
                                            sum_bank[i][:]).then_inc(sum_kept, 1)
                        elif j == 1 and not last:
                            if what[0] == "F":
                                for name in prepare_items(i, True):
                                    if keeper(name) == "dve":
                                        rotate(p, name, p + 1, False)
                            elif what[0] == "A":
                                add(p + 1)

            for g in range(GROUPS):
                rotate(None, f"SW{g}", 0, True)
            add(0)
            three_ends(dve, PAIRS, pair)


def sample_stage(nc, c, t):
    PER = 4
    PAIRS = RUN // (2 * PER)
    ROWS = HEADS * DEC_SEQ
    HALF = PER * P
    KEYS = 2 * HALF
    with ExitStack() as ctx:
        sb = lambda n, s, d=F32: ctx.enter_context(nc.sbuf_tensor(n, s, d))
        sem = lambda n: nc.alloc_semaphore(n)
        ps = lambda n, s: ctx.enter_context(nc.psum_tensor(n, s, F32))
        pages, run_ids = sb("pages", [P, DEC_BATCH], I32), sb("run_ids", [P, DEC_BATCH], U32)
        offset = sb("run_offset", [P, 1])
        new_mask = sb("new_mask", [ROWS, DEC_BATCH, SAMPLE])
        own_query = sb("own_query", [P, 2, ROWS])
        latent = [sb(f"cache_latent{j}", [P, RUN * KV_LORA]) for j in range(2)]
        rope = [sb(f"cache_rope{j}", [P, RUN * ROPE]) for j in range(2)]
        rope_both = sb("q_rope_both", [P, 2, HEADS, SAMPLE])
        q_b = [sb(f"q_lat_batch{j}", [P, LC, HEADS, DEC_SEQ]) for j in range(2)]
        qr_b = [sb(f"q_rope_batch{j}", [P, 2, HEADS, DEC_SEQ]) for j in range(2)]
        row_max, bias, row_total = sb("s_row_max", [P, 1]), sb("s_bias", [P, 1]), sb("s_row_total", [P, 1])
        diagonal, query_max, own_max = sb("s_max_diagonal", [P, P]), sb("s_query_max", [P, ROWS]), sb("s_own_max", [P, ROWS])
        inv, out_rows = sb("s_inverse", [ROWS, 1]), sb("s_out_rows", [ROWS, KV_LORA])
        flat = c.acc[:].rearrange("p a n -> p (a n)")
        at = iter(range(0, DC * TOKENS, ROWS))

        def scratch(n):
            taken = [next(at) for _ in range(n // ROWS)]
            return flat[:, taken[0]:taken[0] + n]

        scores, probs = scratch(KEYS + SAMPLE), scratch(KEYS + SAMPLE)
        probT, new_probT = scratch(KEYS).rearrange("p (k q) -> p k q", q=P), scratch(ROWS)
        keysT = [{k: scratch(HALF) for k in ((0, 0), (0, 1), (1, 0), (1, 1), "rope")} for _ in range(2)]
        ring = [ps(f"turn_bank{s}", [P, HALF]) for s in range(4)]
        score = [ps(f"s_score{s}", [P, HALF]) for s in range(2)]
        out_bank, work = ps("s_out", [ROWS, KV_LORA]), ps("s_work", [P, 512])
        spread_max, total, new_score = work[:, 0:P], work[0:ROWS, P:P + 1], work[0:ROWS, 160:160 + SAMPLE]
        consts, crossed, ids_set = sem("s_consts"), sem("q_rope_crossed"), sem("ids_set")
        landed = [[sem(f"latent{j}_landed"), sem(f"rope{j}_landed")] for j in range(2)]
        zeroed, q_half_set, q_set, new_empty = sem("s_zeroed"), sem("q_rope_half_set"), sem("s_q_set"), sem("s_new_empty")
        turned = sem("s_turned")
        kept = {"act": sem("s_turned_kept_act"), "dve": sem("s_turned_kept_dve")}
        scored, score_kept = sem("s_scored"), sem("s_score_kept")
        maxed, diagonal_set, max_spread, query_maxed, own_set, biased = (sem(f"s_{n}") for n in (
            "row_maxed", "diagonal_set", "max_spread", "query_maxed", "own_max_set", "biased"))
        exp_done, batch_done, inverted, out_set = sem("s_exp_done"), sem("s_batch_done"), sem("s_inverted"), sem("s_out_set")
        block = ctx.enter_context(nc.Block())
        cache_l = t["cache_kv_latent"].rearrange("l n (r s) d -> (l n r) (s d)", s=RUN)
        cache_r = t["cache_k_rope"].rearrange("l n (r s) d -> (l n r) (s d)", s=RUN)

        def keys_uses(m):
            return [(("keys", m, (0, 0)), "act"), (("keys", m, (0, 1)), "dve"), (("keys", m, (1, 0)), "act"),
                    (("keys", m, (1, 1)), "dve"), (("keys", m, "rope"), "act")]

        EARLIER = [(("probs", 0), "act"), (("probs", 1), "dve"), (("new",), "dve")]
        OUT = [(("out",), "dve")]
        USES = keys_uses(0) + keys_uses(1) + EARLIER + keys_uses(2) + OUT + keys_uses(3)
        FIRST = sum((keys_uses(m) for m in range(PAIRS)), [])
        LISTS = {0: FIRST, 1: USES, 2: USES, "after": EARLIER + OUT}
        assert USES[-4:] == FIRST[-4:] and len(FIRST) % 4 == 0 and len(USES) % 4 == 0

        class Use:

            def __init__(self, b, before, key):
                uses = LISTS[before]
                n = [k for k, _ in uses].index(key)
                self.base = len(USES) * b + len(FIRST) - len(USES) if before else 0
                self.uses, self.b, self.before, self.n = uses, b, before, n
                self.bank, self.keeper, self.done = ring[n % 4], uses[n][1], self.base + n + 1

            def kept_with(self, n, who):
                of = lambda uses: sum(e == who for _, e in uses)
                start = of(USES) * self.b + of(FIRST) - of(USES) if self.before else 0
                return start + (of(self.uses[:n + 1]) if n >= 0 else -of(USES[len(USES) + n + 1:]))

            def wait_free(self, pe):
                n = self.n - 4
                if n >= 0 or self.before:
                    who = (self.uses if n >= 0 else USES)[n][1]
                    pe.wait_ge(kept[who], self.kept_with(n, who))

        def batches(eng, batch):
            batch(0, 0, 0, 0)
            batch(1, 0, 1, 1)
            with eng.Fori(1, DEC_BATCH // 2) as q:
                for j in range(2):
                    batch(2 * q + j, q, j, 2)

        LAST = DEC_BATCH - 1

        @block.sync
        def _(sp):
            sp.dma_start(pages[:], t["pages"]).then_inc(consts, 16)
            sp.dma_start(offset[:], t["run_offset"]).then_inc(consts, 16)
            sp.dma_start(new_mask[:], t["new_mask"]).then_inc(consts, 16)
            sp.dma_start(own_query[:], t["own_query"]).then_inc(consts, 16)
            sp.wait_ge(zeroed, 1)
            for j in range(2):
                sp.dma_start(rope_both[(1 - j) * ROPE:(2 - j) * ROPE, 1 - j, j::2, :], c.q_rope_s[j * ROPE:(j + 1) * ROPE]).then_inc(crossed, 16)

        @block.gpsimd
        def _(pool):
            pool.wait_ge(ids_set, 1)
            for b in range(DEC_BATCH):
                j = b % 2
                if b >= 2:
                    pool.wait_ge(batch_done, b - 1)
                for dst, src, n in ((latent[j], cache_l, 0), (rope[j], cache_r, 1)):
                    pool.indirect_dma_start(dst[:], None, src, bass.IndirectOffsetOnAxis(ap=run_ids[:, b:b + 1], axis=0)
                                            ).then_inc(landed[j][n], 16)

        @block.tensor
        def _(pe):
            def turn_keys(b, j, m, before):
                for (_, _, what), _ in keys_uses(m):
                    use = Use(b, before, ("keys", m, what))
                    use.wait_free(pe)
                    for i in range(PER):
                        row = 2 * PER * m + 2 * i
                        if what == "rope":
                            src = rope[j][:, row * ROPE:(row + 2) * ROPE]
                        else:
                            odd, l = what
                            src = latent[j][:, (row + odd) * KV_LORA + l * P:(row + odd) * KV_LORA + (l + 1) * P]
                        mm = pe.transpose(use.bank[:, i * P:(i + 1) * P], src, c.ident[:])
                    mm.then_inc(turned, 1)

            def score_pair(b, j, m, before):
                for what in ((1, 1), "rope"):
                    use = Use(b, before, ("keys", m, what))
                    pe.wait_ge(kept[use.keeper], use.kept_with(use.n, use.keeper))
                if m == 0:
                    pe.wait_ge(q_set, 2 * b + 2)
                if before and m in (0, PAIRS // 2):
                    pe.wait_ge(score_kept, 3 * b - 2 + (m != 0))
                half, g = score[m // 2], 2 * (m % 2)
                keys = keysT[m % 2]
                pe.matmul(half[g * ROWS:(g + 2) * ROWS, :], qr_b[j][:].rearrange("p j h s -> p (j h s)"), keys["rope"],
                          start=True, stop=False)
                for odd in range(2):
                    for l in range(LC):
                        mm = pe.matmul(half[(g + odd) * ROWS:(g + odd + 1) * ROWS, :], q_b[j][:, l].rearrange("p h s -> p (h s)"),
                                       keys[odd, l], start=False, stop=(l == LC - 1))
                if m == PAIRS - 1:
                    for l in range(LC):
                        pe.matmul(new_score, q_b[j][:, l].rearrange("p h s -> p (h s)"), c.new_latent[:, l, :],
                                  start=(l == 0), stop=False)
                    mm = pe.matmul(new_score, qr_b[j][:, 0].rearrange("p h s -> p (h s)"), c.new_key[:], start=False, stop=True)
                mm.then_inc(scored, 1)

            def spread(p):
                pe.wait_ge(diagonal_set, p + 1)
                pe.matmul(spread_max, c.ones[:], diagonal[:], start=True, stop=True).then_inc(max_spread, 1)

            def turn_probs(b, p, before):
                pe.wait_ge(exp_done, p + 1)
                for a in range(2):
                    use = Use(b, before, ("probs", a))
                    use.wait_free(pe)
                    for i in range(PER):
                        mm = pe.transpose(use.bank[:, i * P:(i + 1) * P], probs[:, (PER * a + i) * P:(PER * a + i + 1) * P], c.ident[:])
                    mm.then_inc(turned, 1)
                use = Use(b, before, ("new",))
                use.wait_free(pe)
                pe.matmul(use.bank[0:SAMPLE, 0:ROWS], probs[:, KEYS:KEYS + SAMPLE], c.ident[:, 0:ROWS],
                          start=True, stop=True).then_inc(turned, 1)

            def sum_latents(b, p, j, before):
                for key in (("probs", 0), ("new",)):
                    use = Use(b, before, key)
                    pe.wait_ge(kept[use.keeper], use.kept_with(use.n, use.keeper))
                for k in range(2 * PER):
                    for g in range(PER):
                        row = 16 * (k // PER) + 8 * (g // 2) + 2 * (k % PER) + g % 2
                        pe.matmul(out_bank[:], probT[:, k, g * ROWS:(g + 1) * ROWS],
                                  latent[j][:, row * KV_LORA:(row + 1) * KV_LORA], start=(k + g == 0), stop=False)
                pe.matmul(out_bank[:], new_probT[0:SAMPLE, :], c.new_rows[:], start=False, stop=True)
                pe.matmul(total, own_query[:, 1, :], row_total[:], start=True, stop=True).then_inc(batch_done, 1)

            def turn_out(b, p, before):
                use = Use(b, before, ("out",))
                use.wait_free(pe)
                pe.wait_ge(out_set, p + 1)
                for l in range(LC):
                    mm = pe.matmul(use.bank[:, l * ROWS:(l + 1) * ROWS], out_rows[:, l * P:(l + 1) * P], c.ident[0:ROWS, 0:ROWS],
                                   start=True, stop=True)
                mm.then_inc(turned, 1)

            def batch(b, q, j, before):
                for n in range(2):
                    pe.wait_ge(landed[j][n], 16 * q + 16)
                turn_keys(b, j, 0, before)
                if before:
                    spread(b - 1)
                turn_keys(b, j, 1, before)
                score_pair(b, j, 0, before)
                if before:
                    turn_probs(b, b - 1, before)
                turn_keys(b, j, 2, before)
                if before:
                    sum_latents(b, b - 1, 1 - j, before)
                score_pair(b, j, 1, before)
                if before:
                    turn_out(b, b - 1, before)
                turn_keys(b, j, 3, before)
                score_pair(b, j, 2, before)
                score_pair(b, j, 3, before)

            pe.wait_ge(consts, 64)
            batches(pe, batch)
            spread(LAST)
            turn_probs(DEC_BATCH, LAST, "after")
            sum_latents(DEC_BATCH, LAST, LAST % 2, "after")
            turn_out(DEC_BATCH, LAST, "after")

        def keep(eng, who, copy, b, before, key, dst):
            use = Use(b, before, key)
            if use.keeper == who:
                eng.wait_ge(turned, use.done)
                if key[0] == "keys" and (before or key[1] >= 2):
                    eng.wait_ge(scored, PAIRS * b + key[1] - 1)
                copy(dst, use.bank).then_inc(kept[who], 1)

        @block.scalar
        def _(act):
            def keep_keys(b, m, before):
                for (_, _, what), who in keys_uses(m):
                    keep(act, "act", lambda d, s: act.copy(d, s[:]), b, before, ("keys", m, what), keysT[m % 2][what])

            def exponential(p):
                act.wait_ge(biased, p + 1)
                act.activation(probs, scores, ACT.Exp, bias=bias[:], scale=SM_SCALE, accum_out=row_total[:]).then_inc(exp_done, 1)

            def keep_probs(b, before):
                keep(act, "act", lambda d, s: act.copy(d, s[:].rearrange("p (k q) -> p k q", q=P)), b, before, ("probs", 0), probT[:, 0:PER, :])

            def batch(b, q, j, before):
                keep_keys(b, 0, before)
                keep_keys(b, 1, before)
                if before:
                    exponential(b - 1)
                    keep_probs(b, before)
                keep_keys(b, 2, before)
                keep_keys(b, 3, before)

            batches(act, batch)
            exponential(LAST)
            keep_probs(DEC_BATCH, "after")

        @block.vector
        def _(dve):
            def keep_keys(b, m, before):
                for (_, _, what), who in keys_uses(m):
                    keep(dve, "dve", lambda d, s: dve.tensor_copy(d, s[:]), b, before, ("keys", m, what), keysT[m % 2][what])

            def keep_half(b, half, before):
                dve.wait_ge(scored, PAIRS * b + 2 * half + 2)
                if before:
                    dve.wait_ge(exp_done, b)
                dve.tensor_copy(scores[:, half * HALF:(half + 1) * HALF], score[half][:]).then_inc(score_kept, 1)

            def keep_new(b):
                dve.tensor_tensor(scores[0:ROWS, KEYS:KEYS + SAMPLE], new_score,
                                  new_mask[:, bass.ds(b, 1), :].rearrange("p b n -> p (b n)"), ALU.add).then_inc(score_kept, 1)

            def maximum(p):
                dve.wait_ge(score_kept, 3 * p + 3)
                dve.tensor_reduce(row_max[:], scores, AX_X, ALU.max).then_inc(maxed, 1)
                dve.wait_ge(maxed, p + 1)
                dve.tensor_scalar(diagonal[:], c.ident[:], row_max[:], None, ALU.mult).then_inc(diagonal_set, 1)

            def make_bias(p):
                dve.wait_ge(max_spread, p + 1)
                dve.tensor_reduce(query_max[:], spread_max.rearrange("p (g q) -> p q g", q=ROWS), AX_X, ALU.max).then_inc(query_maxed, 1)
                dve.wait_ge(query_maxed, p + 1)
                dve.tensor_tensor(own_max[:], query_max[:], own_query[:, 0, :], ALU.mult).then_inc(own_set, 1)
                dve.wait_ge(own_set, p + 1)
                dve.tensor_reduce(bias[:], own_max[:], AX_X, ALU.add).then_inc(biased, 1)

            def keep_probs(b, before):
                keep(dve, "dve", lambda d, s: dve.tensor_copy(d, s[:].rearrange("p (k q) -> p k q", q=P)), b, before,
                     ("probs", 1), probT[:, PER:2 * PER, :])
                keep(dve, "dve", lambda d, s: dve.tensor_copy(d, s[0:SAMPLE, 0:ROWS]), b, before, ("new",), new_probT[0:SAMPLE, :])

            def normalise(p):
                dve.wait_ge(batch_done, p + 1)
                dve.reciprocal(inv[:], total).then_inc(inverted, 1)
                dve.wait_ge(inverted, p + 1)
                dve.tensor_scalar(out_rows[:], out_bank[:], inv[:], None, ALU.mult).then_inc(out_set, 1)

            def keep_out(b, p, before):
                keep(dve, "dve", lambda d, s: dve.tensor_copy(d, s[:, 0:LC * ROWS].rearrange("p (l h s) -> p l h s", l=LC, h=HEADS)),
                     b, before, ("out",), c.o_lat_s[:, :, :, bass.ds(p * DEC_SEQ, DEC_SEQ)])

            def set_queries(b, j, before):
                if before == 2:
                    dve.wait_ge(scored, PAIRS * b - PAIRS)
                at = bass.ds(b * DEC_SEQ, DEC_SEQ)
                dve.tensor_copy(q_b[j][:], c.q_lat_s[:, :, :, at]).then_inc(q_set, 1)
                dve.tensor_copy(qr_b[j][:], rope_both[:, :, :, at]).then_inc(q_set, 1)

            def batch(b, q, j, before):
                if before:
                    maximum(b - 1)
                set_queries(b, j, before)
                keep_keys(b, 0, before)
                if before:
                    make_bias(b - 1)
                keep_keys(b, 1, before)
                if before:
                    keep_probs(b, before)
                keep_keys(b, 2, before)
                if before:
                    normalise(b - 1)
                keep_half(b, 0, before)
                if before:
                    keep_out(b, b - 1, before)
                keep_keys(b, 3, before)
                keep_half(b, 1, before)
                keep_new(b)

            dve.memset(rope_both[:], 0.0).then_inc(zeroed, 1)
            dve.wait_ge(consts, 64)
            dve.tensor_scalar(run_ids[:], pages[:], float(RUNS_PER_PAGE), offset[:], ALU.mult, ALU.add).then_inc(ids_set, 1)
            dve.wait_ge(zeroed, 1)
            for j in range(2):
                dve.tensor_copy(rope_both[j * ROPE:(j + 1) * ROPE, j, j::2, :], c.q_rope_s[j * ROPE:(j + 1) * ROPE]).then_inc(q_half_set, 1)
            dve.memset(scores[:, KEYS:KEYS + SAMPLE], NEG).then_inc(new_empty, 1)
            dve.wait_ge(new_empty, 1)
            dve.wait_ge(crossed, 32)
            dve.wait_ge(q_half_set, 2)
            batches(dve, batch)
            maximum(LAST)
            make_bias(LAST)
            keep_probs(DEC_BATCH, "after")
            normalise(LAST)
            keep_out(DEC_BATCH, LAST, "after")


def sample_value_stage(nc, c, t):
    with ExitStack() as ctx:
        sem = lambda n: nc.alloc_semaphore(n)
        w_uv = ctx.enter_context(nc.sbuf_tensor("w_uv_all", [P, LC, HEADS * VDIM], F32))
        bank = ctx.enter_context(nc.psum_tensor("value_bank", [P, HEADS, SAMPLE], F32))
        landed, done, kept = sem("w_uv_all_landed"), sem("values_done"), sem("values_kept")
        block = ctx.enter_context(nc.Block())

        @block.sync
        def _(sp):
            sp.dma_start(w_uv[:], t["w_uv"].rearrange("l (k p) h n -> p (l k) (h n)", p=P)).then_inc(landed, 16)

        @block.tensor
        def _(pe):
            pe.wait_ge(landed, 16)
            for h in range(HEADS):
                for l in range(LC):
                    mm = pe.matmul(bank[:, h, :], w_uv[:, l, h * VDIM:(h + 1) * VDIM], c.o_lat_s[:, l, h, :],
                                   start=(l == 0), stop=(l == LC - 1))
            mm.then_inc(done, 1)

        HALF = DC // 2

        @block.scalar
        def _(act):
            act.copy(c.acc[:, 0:HALF, 0:SEQ], c.value[:, 0:HALF, :]).then_inc(kept, 1)

        @block.vector
        def _(dve):
            dve.tensor_copy(c.acc[:, HALF:DC, 0:SEQ], c.value[:, HALF:DC, :]).then_inc(kept, 1)
            dve.wait_ge(done, 1)
            dve.tensor_copy(c.acc[:, :, SEQ:TOKENS], bank[:]).then_inc(kept, 1)


def store_stage(nc, c, t):
    with ExitStack() as ctx:
        sem = lambda n: nc.alloc_semaphore(n)
        rows = ctx.enter_context(nc.sbuf_tensor("out_rows", [P, 2, D], F32))
        bank = [ctx.enter_context(nc.psum_tensor(f"out_bank{j}", [P, 512], F32)) for j in range(4)]
        turned, kept = sem("out_turned"), sem("out_kept")
        stored = [sem(f"out_stored{j}") for j in range(2)]
        block = ctx.enter_context(nc.Block())
        y = t["y_prompt"].rearrange("a (n p) d -> (a n) p d", p=P)
        tiles = [(i, P if i < QT else SAMPLE) for i in range(QT + 1)]

        @block.tensor
        def _(pe):
            for i, width in tiles:
                for half in range(2):
                    if i >= 2:
                        pe.wait_ge(kept, 2 * i - 3 + half)
                    for n in range(4):
                        mm = pe.transpose(bank[2 * (i % 2) + half][0:width, n * P:(n + 1) * P],
                                          c.y[:, 4 * half + n, i * P:i * P + width], c.ident[:])
                    mm.then_inc(turned, 1)

        @block.vector
        def _(dve):
            for i, width in tiles:
                for half in range(2):
                    dve.wait_ge(turned, 2 * i + half + 1)
                    if i >= 2:
                        dve.wait_ge(stored[i % 2], 16 * (i // 2))
                    dve.tensor_copy(rows[0:width, i % 2, half * 512:(half + 1) * 512],
                                    bank[2 * (i % 2) + half][0:width, :]).then_inc(kept, 1)

        @block.sync
        def _(sp):
            for i, width in tiles:
                sp.wait_ge(kept, 2 * i + 2)
                out = y[i] if i < QT else t["y_sample"].rearrange("b s d -> (b s) d")
                sp.dma_start(out, rows[0:width, i % 2, :]).then_inc(stored[i % 2], 16)
            sp.wait_ge(stored[0], 16 * 5)
            sp.wait_ge(stored[1], 16 * 4)


def operand_buffers(nc, ctx, c, tag):
    c.hi, c.lo = (ctx.enter_context(nc.sbuf_tensor(f"operand_{n}{tag}", [P, DC, TOKENS], F32R)) for n in ("hi", "lo"))


def trunk(nc, t):
    c = Chip()
    start = nc.snapshot_sems()
    with ExitStack() as ctx:
        sb = lambda n, s, d=F32: ctx.enter_context(nc.sbuf_tensor(n, s, d))
        c.ident, c.ones = sb("ident_sb", [P, P]), sb("ones_sb", [P, P])
        c.param = sb("params", [P, PARAM_ROWS + TAP_ROWS])
        c.y, c.acc = (sb(n, [P, DC, TOKENS]) for n in ("residual", "summed"))
        SA = DEC_BATCH * PAD_A
        with ExitStack() as layer0:
            operand_buffers(nc, layer0, c, "0")
            with ExitStack() as conv:
                csb = lambda n, s, d=F32: conv.enter_context(nc.sbuf_tensor(n, s, d))
                c.state = csb("states", [P, CC, SA + DEC_BATCH * PAD_B])
                c.tails = csb("state_tails", [P, CC, PAD_A + SA + PAD_B + DEC_BATCH * PAD_B])
                load_stage(nc, c, t)
                conv_stage(nc, c, t, c.acc)
                conv_norm_stage(nc, c, t, c.acc)
                project_stage(nc, c, "w_out", t["w_out_conv"][0], [P] * DC, c.acc)
            reuse_semaphores(nc, start)
            ffn_stage(nc, c, 0, t, dict(post=ROW_MIX_POST, pre=ROW_FFN_PRE))
            project_stage(nc, c, "w_mla", t["w_in_mla"][0], [P] * 6, c.acc, dict(post=ROW_FFN_POST, pre=ROW_MIX_PRE + DC), twice=True)
        with ExitStack() as mla:
            msb = lambda n, s, d=F32: mla.enter_context(nc.sbuf_tensor(n, s, d))
            c.value = msb("values", [P, DC, SEQ])
            c.new_latent, c.new_key, c.new_rows = msb("new_latent", [P, LC, SAMPLE]), msb("new_key", [P, SAMPLE]), msb("new_rows", [SAMPLE, KV_LORA])
            c.q_lat_s, c.q_rope_s = msb("q_lat_sample", [P, LC, HEADS, SAMPLE]), msb("q_rope_sample", [P, HEADS // 2, SAMPLE])
            c.o_lat_s = msb("o_lat_sample", [P, LC, HEADS, SAMPLE])
            with ExitStack() as prompt:
                psb = lambda n, s, d=F32: prompt.enter_context(nc.sbuf_tensor(n, s, d))
                k = Chip()
                k.latent, k.key = psb("latent", [P, LC, TOKENS]), [psb(f"key{j}", [P, TOKENS]) for j in range(2)]
                k.cos, k.sin = psb("cos_sb", [P, TOKENS]), psb("sin_sb", [P, TOKENS])
                k.swap, k.causal = psb("swap_sb", [P, P]), psb("causal_sb", [P, P])
                ckv = c.acc[:, QC:QC + LC, :]
                norm_stage(nc, c, "lat", [(c.acc, QC, ROW_QN, c.acc, None), (ckv, LC, ROW_KVN, k.latent, None)])
                reuse_semaphores(nc, start)
                latent_stage(nc, c, t, k)
                attention_stage(nc, c, t, k, c.acc)
            sample_stage(nc, c, t)
            sample_value_stage(nc, c, t)
        with ExitStack() as layer1:
            operand_buffers(nc, layer1, c, "1")
            project_stage(nc, c, "w_o", t["w_o_mla"][0], [P] * DC, c.acc, split=True)
            reuse_semaphores(nc, start)
            ffn_stage(nc, c, 1, t, dict(post=ROW_MIX_POST + DC, pre=ROW_FFN_PRE + DC))
        norm_stage(nc, c, "out", [(c.acc, DC, ROW_FFN_POST + DC, None, c.y)])
        store_stage(nc, c, t)


_OUTS = [("y_prompt", (1, SEQ, D)), ("y_sample", (DEC_BATCH, DEC_SEQ, D)),
         ("new_conv_a_prompt", (1, 1, PAD_A, CHAN)), ("new_conv_a_sample", (1, DEC_BATCH, PAD_A, CHAN)),
         ("new_conv_b_prompt", (1, 1, PAD_B, CHAN)), ("new_conv_b_sample", (1, DEC_BATCH, PAD_B, CHAN)),
         ("new_kv_latent_prompt", (1, 1, SEQ, KV_LORA)), ("new_kv_latent_sample", (1, DEC_BATCH, DEC_SEQ, KV_LORA)),
         ("new_k_rope_prompt", (1, 1, SEQ, ROPE)), ("new_k_rope_sample", (1, DEC_BATCH, DEC_SEQ, ROPE))]


def _constants():
    f = np.float32
    half = ROPE // 2
    inv_freq = (f(1.0) / (f(10000.0) ** (np.arange(half, dtype=f) * f(2.0 / ROPE)))).astype(f)
    pos = np.concatenate([np.arange(SEQ), np.tile(PAGES * PAGE + np.arange(DEC_SEQ), DEC_BATCH)]).astype(f)
    ang = (inv_freq[:, None] * pos[None, :]).astype(f)
    swap = np.zeros((ROPE, ROPE), f)
    for r in range(half):
        swap[half + r, r] = -1.0
        swap[r, half + r] = 1.0
    q = np.arange(P)
    row_step = np.arange(HEADS * DEC_SEQ) % DEC_SEQ
    key_batch, key_step = np.arange(SAMPLE) // DEC_SEQ, np.arange(SAMPLE) % DEC_SEQ
    ok = (key_batch[None, None, :] == np.arange(DEC_BATCH)[None, :, None]) & (key_step[None, None, :] <= row_step[:, None, None])
    own = np.tile(np.eye(HEADS * DEC_SEQ, dtype=f), (P // (HEADS * DEC_SEQ), 1))
    return {
        "ident": np.eye(P, dtype=f),
        "rope_cos": np.ascontiguousarray(np.tile(np.cos(ang), (4, 1))),
        "rope_sin": np.ascontiguousarray(np.tile(np.sin(ang), (4, 1))),
        "rope_swap": np.kron(np.eye(2, dtype=f), swap),
        "causal": np.where(q[None, :] <= q[:, None], 0.0, NEG).astype(f),
        "new_mask": np.where(ok, 0.0, NEG).astype(f),
        "own_query": np.ascontiguousarray(np.stack([own * f(-SM_SCALE), own], axis=1)),
        "run_offset": (q % RUNS_PER_PAGE).astype(f)[:, None],
    }


def kernel(**inputs):
    import concourse.bacc as _bacc
    from concourse.bass_utils import run_bass_kernel_spmd as _run

    nc = _bacc.Bacc("TRN2", target_bir_lowering=False, num_devices=1)
    given = {n: np.ascontiguousarray(a) for n, a in inputs.items() if n != "page_table"}
    given["pages"] = np.ascontiguousarray(np.repeat(np.asarray(inputs["page_table"]), RUNS_PER_PAGE, axis=1).T)
    given.update(_constants())
    arrays, t = {}, {}
    for name, a in given.items():
        arrays[f"in_{name}"] = a
        t[name] = nc.dram_tensor(f"in_{name}", a.shape, mybir.dt.from_np(a.dtype), kind="ExternalInput").ap()
    for name, shape in _OUTS:
        t[name] = nc.dram_tensor(f"out_{name}", shape, F32, kind="ExternalOutput").ap()
    trunk(nc, t)
    r = _run(nc, [arrays], core_ids=[0])
    return tuple(r.results[0][f"out_{name}"] for name, _ in _OUTS)
```

```python
from contextlib import ExitStack

import numpy as np

import concourse.bass as bass
from concourse import mybir

F32 = mybir.dt.float32
F32R = mybir.dt.float32r
I32 = mybir.dt.int32
U32 = mybir.dt.uint32
ALU = mybir.AluOpType
ACT = mybir.ActivationFunctionType
AX_X = mybir.AxisListType.X

P = 128
SEQ, DEC_BATCH, DEC_SEQ = 1024, 8, 4
SAMPLE = DEC_BATCH * DEC_SEQ
TOKENS = SEQ + SAMPLE
GROUPS = 3
GW = TOKENS // GROUPS
D = 1024
DC = D // P
D_FF = 2816
FC = D_FF // P
CHAN = 512
CC = CHAN // P
TAPS_A, TAPS_B = 31, 3
PAD_A, PAD_B = TAPS_A - 1, TAPS_B - 1
HEADS = 8
Q_LORA, KV_LORA, ROPE, NOPE, VDIM = 384, 256, 64, 128, 128
QC, LC = Q_LORA // P, KV_LORA // P
QT = SEQ // P
PAGE, PAGES = 128, 32
RUN = 32
RUNS_PER_PAGE = PAGE // RUN
SM_SCALE = float((NOPE + ROPE) ** -0.5)
RMS_EPS, LN_EPS = 1e-6, 1e-5
NEG = -1e30

ROW_MIX_PRE, ROW_MIX_POST, ROW_FFN_PRE, ROW_FFN_POST = 0, 16, 32, 48
ROW_CONV_B = 64
ROW_BIAS_A = ROW_CONV_B + TAPS_B * CC
ROW_LN_G = ROW_BIAS_A + CC
ROW_LN_B = ROW_LN_G + CC
ROW_QN = ROW_LN_B + CC
ROW_KVN = ROW_QN + QC
PARAM_ROWS = ROW_KVN + LC
TAP_ROWS = TAPS_A * CC


def group(t):
    return slice(t * GW, (t + 1) * GW)


def peeled(eng, n, body):
    body(0, True)
    if n > 1:
        with eng.Fori(1, n) as i:
            body(i, False)


def three_ends(eng, n, body):
    body(0, True, False)
    with eng.Fori(1, n - 1) as i:
        body(i, False, False)
    body(n - 1, False, True)


def split_product(pe, out, w_hi, w_lo, x_hi, x_lo, chunks):
    for k in range(chunks):
        pe.matmul(out, w_hi(k), x_hi(k), start=(k == 0), stop=False)
        pe.matmul(out, w_hi(k), x_lo(k), start=False, stop=False)
        mm = pe.matmul(out, w_lo(k), x_hi(k), start=False, stop=(k == chunks - 1))
    return mm


class Chip:
    pass


class Norm:

    SQUARES, ROWS = DC * GW, 2 * GW

    def __init__(self, nc, ctx, c, tag, rounds, space=None):
        self.c = c
        if [r[0] for r in rounds] == ["post", "pre"]:
            order = [(0, 0), (1, 0), (0, 1), (2, 0), (1, 1), (2, 1)]
        else:
            order = [(g, r) for g in range(GROUPS) for r in range(len(rounds))]
        self.units = [(g, *rounds[r]) for g, r in order]
        sem = lambda n: nc.alloc_semaphore(f"{n}_{tag}")
        squares, rows = space or [ctx.enter_context(nc.sbuf_tensor(f"norm_{n}_{tag}", [P, size], F32))[:]
                                  for n, size in (("squares", self.SQUARES), ("rows", self.ROWS))]
        half = DC // 2 * GW
        self.squares = [squares[:, j * half:(j + 1) * half].rearrange("p (k n) -> p k n", n=GW) for j in range(2)]
        self.root, self.rstd = (rows[:, a:a + GW] for a in range(0, self.ROWS, GW))
        self.total = ctx.enter_context(nc.psum_tensor(f"total_{tag}", [P, GW], F32))
        self.squared, self.half_summed, self.root_set = sem("squared"), sem("half_summed"), sem("root_set")
        self.rstd_set, self.scaled = sem("rstd_set"), sem("scaled")
        self.residual_set, self.residual_rest = sem("residual_set_pool"), sem("residual_set_dve")
        self.hi_set, self.lo_set, self.lo_rest = sem("normed_hi"), sem("normed_lo"), sem("last_normed_lo_rest")

    def count(self, u, kind):
        return sum(unit[1] == kind for unit in self.units[:u + 1])

    def post_unit(self, u):
        if self.units[u][1] == "pre":
            for v in range(u):
                if self.units[v][:2] == (self.units[u][0], "post"):
                    return v

    def wait_source(self, eng, u):
        v = self.post_unit(u)
        if v is not None:
            for half in (self.residual_set, self.residual_rest):
                eng.wait_ge(half, self.count(v, "post"))

    def halves(self, u):
        chunks = self.units[u][3]
        return (0, (chunks + 1) // 2), ((chunks + 1) // 2, chunks)

    def wait_group(self, eng, g):
        if self.units[-1][1] == "post":
            eng.wait_ge(self.residual_set, g + 1)
            eng.wait_ge(self.residual_rest, g + 1)
        else:
            eng.wait_ge(self.lo_set, g + 1)
            if g == GROUPS - 1:
                eng.wait_ge(self.lo_rest, 1)

    def act(self, act, weights=lambda: None):
        c, last = self.c, len(self.units) - 1

        def square(u, j):
            if j == 0:
                self.wait_source(act, u)
            if u:
                act.wait_ge(self.half_summed, 2 * u - 1 + j)
            g, _, src, _, _, _ = self.units[u]
            a, b = self.halves(u)[j]
            act.activation(self.squares[j][:, 0:b - a, :], src[:, a:b, group(g)], ACT.Square).then_inc(self.squared, 1)

        def split(u):
            g, kind, _, chunks, _, dst = self.units[u]
            if kind == "pre":
                act.wait_ge(self.scaled, u + 1)
                for a, b in self.halves(u) if u == last else [(0, chunks)]:
                    act.copy(c.hi[:, a:b, group(g)], dst[:, a:b, group(g)]).then_inc(self.hi_set, 1)

        square(0, 0)
        square(0, 1)
        for u in range(last + 1):
            v = self.post_unit(u + 1) if u < last else None
            early = u < last and (v is None or v <= u - 2)
            if early:
                square(u + 1, 0)
            act.wait_ge(self.half_summed, 2 * u + 2)
            if u:
                act.wait_ge(self.rstd_set, u)
            act.activation(self.root, self.total[:], ACT.Sqrt, bias=c.eps[:, 0:1], scale=1.0 / (self.units[u][3] * P)).then_inc(self.root_set, 1)
            if u < last:
                if not early:
                    square(u + 1, 0)
                square(u + 1, 1)
            if u:
                split(u - 1)
            else:
                weights()
        split(last)

    def pe(self, pe):
        for u, unit in enumerate(self.units):
            for j, (a, b) in enumerate(self.halves(u)):
                pe.wait_ge(self.squared, 2 * u + j + 1)
                if u and j == 0:
                    pe.wait_ge(self.root_set, u)
                for k in range(b - a):
                    mm = pe.matmul(self.total[:], self.c.ones[:], self.squares[j][:, k, :], start=(a + k == 0),
                                   stop=(a + k == unit[3] - 1))
                mm.then_inc(self.half_summed, 1)

    def dve(self, dve):
        c, last = self.c, len(self.units) - 1
        for u, (g, kind, src, chunks, col, dst) in enumerate(self.units):
            dve.wait_ge(self.root_set, u + 1)
            if u:
                dve.wait_ge(self.scaled, u)
            dve.reciprocal(self.rstd, self.root).then_inc(self.rstd_set, 1)
            dve.wait_ge(self.rstd_set, u + 1)
            self.wait_source(dve, u)
            for k in range(chunks):
                ins = dve.scalar_tensor_tensor(out=dst[:, k, group(g)], in0=src[:, k, group(g)],
                                               scalar=c.param[:, col + k:col + k + 1], in1=self.rstd,
                                               op0=ALU.mult, op1=ALU.mult)
            ins.then_inc(self.scaled, 1)
            a, b = self.halves(u)[1]
            if kind == "post":
                dve.wait_ge(self.scaled, u + 1)
                dve.tensor_tensor(c.y[:, a:b, group(g)], c.y[:, a:b, group(g)], dst[:, a:b, group(g)], ALU.add).then_inc(self.residual_rest, 1)
        if kind == "pre":
            dve.wait_ge(self.hi_set, self.count(last, "pre") + 1)
            dve.tensor_tensor(c.lo[:, a:b, group(g)], dst[:, a:b, group(g)], c.hi[:, a:b, group(g)].bitcast(F32),
                              ALU.subtract).then_inc(self.lo_rest, 1)

    def pool(self, pool, weights=lambda: None):
        c, last = self.c, len(self.units) - 1
        for u, (g, kind, _, chunks, _, dst) in enumerate(self.units):
            if kind == "post":
                a, b = self.halves(u)[0]
                pool.wait_ge(self.scaled, u + 1)
                pool.tensor_tensor(c.y[:, a:b, group(g)], c.y[:, a:b, group(g)], dst[:, a:b, group(g)], ALU.add).then_inc(self.residual_set, 1)
        weights()
        for u, (g, kind, _, chunks, _, dst) in enumerate(self.units):
            if kind == "pre":
                a, b = self.halves(u)[0] if u == last else (0, chunks)
                pool.wait_ge(self.hi_set, self.count(u, "pre"))
                pool.tensor_tensor(c.lo[:, a:b, group(g)], dst[:, a:b, group(g)], c.hi[:, a:b, group(g)].bitcast(F32),
                                   ALU.subtract).then_inc(self.lo_set, 1)


class LayerNorm:

    def __init__(self, nc, ctx, c, tag):
        self.c = c
        sb = lambda n, s: ctx.enter_context(nc.sbuf_tensor(f"ln_{n}", s, F32))
        sem = lambda n: nc.alloc_semaphore(f"ln_{n}")
        self.squares = [sb(f"squares{j}", [P, CC, GW]) for j in range(2)]
        self.mean, self.root, self.rstd = ([sb(f"{n}{g}", [P, GW]) for g in range(GROUPS)] for n in ("mean", "root", "rstd"))
        self.total, self.total2 = (ctx.enter_context(nc.psum_tensor(f"ln_{n}", [P, GW], F32)) for n in ("total", "total2"))
        self.summed, self.mean_set, self.centred, self.squared, self.summed2 = map(sem, ("summed", "mean_set", "centred", "squared", "summed2"))
        self.root_set, self.rstd_set, self.scaled, self.silu_done = map(sem, ("root_set", "rstd_set", "scaled", "silu_done"))
        self.hi_a, self.lo_a, self.hi_b, self.lo_b = map(sem, ("hi_a", "lo_a", "hi_b", "lo_b"))

    def wait_group(self, eng, g):
        eng.wait_ge(self.lo_a, g + 1)
        eng.wait_ge(self.lo_b, g + 1)

    def pe(self, pe):
        c = self.c

        def total(g):
            if g:
                pe.wait_ge(self.mean_set, g)
            for k in range(CC):
                mm = pe.matmul(self.total[:], c.ones[:], c.acc[:, k, group(g)], start=(k == 0), stop=(k == CC - 1))
            mm.then_inc(self.summed, 1)

        def total_squares(g):
            pe.wait_ge(self.squared, g + 1)
            if g:
                pe.wait_ge(self.root_set, g)
            for k in range(CC):
                mm = pe.matmul(self.total2[:], c.ones[:], self.squares[g % 2][:, k, :], start=(k == 0), stop=(k == CC - 1))
            mm.then_inc(self.summed2, 1)

        total(0)
        for g in range(GROUPS):
            if g + 1 < GROUPS:
                total(g + 1)
            total_squares(g)

    def act(self, act, weights=lambda: None):
        c = self.c

        def square(g):
            act.wait_ge(self.centred, g + 1)
            if g >= 2:
                act.wait_ge(self.summed2, g - 1)
            act.activation(self.squares[g % 2][:], c.acc[:, 0:CC, group(g)], ACT.Square).then_inc(self.squared, 1)

        def split_b(g):
            act.copy(c.hi[:, CC:DC, group(g)], c.acc[:, CC:DC, group(g)]).then_inc(self.hi_b, 1)

        split_b(0)
        square(0)
        for g in range(GROUPS):
            if g + 1 < GROUPS:
                split_b(g + 1)
                square(g + 1)
            else:
                weights()
            act.wait_ge(self.summed2, g + 1)
            act.activation(self.root[g][:], self.total2[:], ACT.Sqrt, bias=c.eps[:, 1:2], scale=1.0 / CHAN).then_inc(self.root_set, 1)
        for g in range(GROUPS):
            act.wait_ge(self.scaled, g + 1)
            for k in range(CC):
                act.activation(c.acc[:, k, group(g)], c.acc[:, k, group(g)], ACT.Silu,
                               bias=c.param[:, ROW_LN_B + k:ROW_LN_B + k + 1],
                               scale=c.param[:, ROW_LN_G + k:ROW_LN_G + k + 1]).then_inc(self.silu_done, 1)
            act.wait_ge(self.silu_done, CC * g + CC)
            act.copy(c.hi[:, 0:CC, group(g)], c.acc[:, 0:CC, group(g)]).then_inc(self.hi_a, 1)

    def dve(self, dve):
        c = self.c

        def across(x):
            return x[:].unsqueeze(1).to_broadcast([P, CC, GW])

        def centre(g):
            dve.wait_ge(self.summed, g + 1)
            dve.tensor_scalar(self.mean[g][:], self.total[:], 1.0 / CHAN, None, ALU.mult).then_inc(self.mean_set, 1)
            dve.wait_ge(self.mean_set, g + 1)
            part = c.acc[:, 0:CC, group(g)]
            dve.tensor_tensor(part, part, across(self.mean[g]), ALU.subtract).then_inc(self.centred, 1)

        centre(0)
        for g in range(GROUPS):
            if g + 1 < GROUPS:
                centre(g + 1)
            dve.wait_ge(self.root_set, g + 1)
            dve.reciprocal(self.rstd[g][:], self.root[g][:]).then_inc(self.rstd_set, 1)
            dve.wait_ge(self.rstd_set, g + 1)
            part = c.acc[:, 0:CC, group(g)]
            dve.tensor_tensor(part, part, across(self.rstd[g]), ALU.mult).then_inc(self.scaled, 1)
        for g in range(GROUPS):
            dve.wait_ge(self.hi_a, g + 1)
            dve.tensor_tensor(c.lo[:, 0:CC, group(g)], c.acc[:, 0:CC, group(g)], c.hi[:, 0:CC, group(g)].bitcast(F32),
                              ALU.subtract).then_inc(self.lo_a, 1)

    def pool(self, pool, weights=lambda: None):
        c = self.c
        for g in range(GROUPS):
            pool.wait_ge(self.hi_b, g + 1)
            pool.tensor_tensor(c.lo[:, CC:DC, group(g)], c.acc[:, CC:DC, group(g)], c.hi[:, CC:DC, group(g)].bitcast(F32),
                               ALU.subtract).then_inc(self.lo_b, 1)
        weights()


def sandwich(c, post, pre):
    return [("post", c.acc, DC, post, c.acc), ("pre", c.y, DC, pre, c.acc)]


class Split:

    def __init__(self, nc, ctx, c, tag):
        self.c = c
        self.hi_set, self.lo_set = nc.alloc_semaphore(f"values_hi_{tag}"), nc.alloc_semaphore(f"values_lo_{tag}")

    def act(self, act, weights):
        for g in range(GROUPS):
            act.copy(self.c.hi[:, :, group(g)], self.c.value[:, :, group(g)]).then_inc(self.hi_set, 1)
            if g == 0:
                weights()

    def wait_group(self, eng, g):
        eng.wait_ge(self.lo_set, g + 1)

    def pe(self, pe):
        pass

    def dve(self, dve):
        c = self.c
        for g in range(GROUPS):
            dve.wait_ge(self.hi_set, g + 1)
            dve.tensor_tensor(c.lo[:, :, group(g)], c.value[:, :, group(g)], c.hi[:, :, group(g)].bitcast(F32),
                              ALU.subtract).then_inc(self.lo_set, 1)

    def pool(self, pool, weights):
        weights()


def reuse_semaphores(nc, since):
    nc.clear_and_free_semaphores(nc.allocated_since(since))
    nc.all_engine_barrier()


def load_stage(nc, c, t):
    with ExitStack() as ctx:
        sb = lambda n, s, d=F32: ctx.enter_context(nc.sbuf_tensor(n, s, d))
        sem = lambda n: nc.alloc_semaphore(n)
        rows = sb("token_rows", [P, QT, D])
        tail_rows = sb("sample_rows", [SAMPLE, D])
        param_rows = sb("param_rows", [PARAM_ROWS, P])
        tap_rows = sb("tap_rows", [TAP_ROWS, P])
        state_a = sb("state_a_rows", [4 * PAD_A, 2, CHAN])
        state_b = sb("state_b_rows", [DEC_BATCH * PAD_B, CHAN])
        bank = [ctx.enter_context(nc.psum_tensor(f"turn{j}", [P, 512], F32)) for j in range(4)]
        landed = [sem(f"rows{i}_landed") for i in range(QT)]
        consts_landed, small_landed = sem("consts_landed"), sem("small_landed")
        ones_set = sem("ones_set")
        turned, kept = sem("block_turned"), sem("block_kept")
        small_turned, small_kept = sem("small_turned"), sem("small_kept")
        block = ctx.enter_context(nc.Block())
        x = t["x_prompt"].rearrange("a (n p) d -> (a n) p d", p=P)

        small_out = []
        small_in = []

        def small(b, pieces, dst, view):
            small_in.append((b, pieces))
            small_out.append((dst, b, None, view))

        for half in range(2):
            small(half, [(tail_rows[:, (4 * half + k) * P:(4 * half + k + 1) * P], SAMPLE, k * SAMPLE, SAMPLE) for k in range(4)],
                  c.y[:, 4 * half:4 * half + 4, SEQ:TOKENS],
                  lambda bk: bk[:, 0:4 * SAMPLE].rearrange("p (k n) -> p k n", k=4))
        small(2, [(param_rows[:], PARAM_ROWS, 0, PARAM_ROWS), (tap_rows[:], TAP_ROWS, PARAM_ROWS, TAP_ROWS)],
              c.param[:], lambda bk: bk[:, 0:PARAM_ROWS + TAP_ROWS])
        SA = 4 * PAD_A
        for k in range(CC):
            small(3 if k % 2 == 0 else 0,
                  [(state_a[:, g, k * P:(k + 1) * P], SA, g * SA, SA) for g in range(2)]
                  + [(state_b[:, k * P:(k + 1) * P], DEC_BATCH * PAD_B, 2 * SA, DEC_BATCH * PAD_B)],
                  c.state[:, k, :], lambda bk: bk[:, 0:2 * SA + DEC_BATCH * PAD_B])

        @block.sync
        def _(sp):
            sp.dma_start(c.ident[:], t["ident"]).then_inc(consts_landed, 16)

            for i in range(QT):
                sp.dma_start(rows[:, i, :], x[i]).then_inc(landed[i], 16)

        @block.scalar
        def _(act):
            act.dma_start(tail_rows[:], t["x_sample"].rearrange("b s d -> (b s) d")).then_inc(small_landed, 16)
            r = 0
            for name, n in (("mix_pre_gain", 16), ("mix_post_gain", 16), ("ffn_pre_gain", 16), ("ffn_post_gain", 16)):
                act.dma_start(param_rows[r:r + n, :], t[name].rearrange("l (k p) -> (l k) p", p=P)).then_inc(small_landed, 16)
                r += n
            for name, n in (("conv_b_w", TAPS_B * CC), ):
                act.dma_start(param_rows[r:r + n, :], t[name].rearrange("l w (k p) -> (l w k) p", p=P)).then_inc(small_landed, 16)
                r += n
            for name, n in (("conv_a_b", CC), ("ln_a_gain", CC), ("ln_a_bias", CC), ("q_norm_gain", QC), ("kv_norm_gain", LC)):
                act.dma_start(param_rows[r:r + n, :], t[name].rearrange("l (k p) -> (l k) p", p=P)).then_inc(small_landed, 16)
                r += n
            act.dma_start(tap_rows[:], t["conv_a_w"].rearrange("l w (k p) -> (l w k) p", p=P)).then_inc(small_landed, 16)
            act.dma_start(state_a[:], t["state_conv_a"].rearrange("l b w c -> (l b w) c").rearrange(
                "(g r) c -> r g c", g=2)).then_inc(small_landed, 16)
            act.dma_start(state_b[:], t["state_conv_b"].rearrange("l b w c -> (l b w) c")).then_inc(small_landed, 16)

            def step(i, first):
                for j in range(2):
                    act.wait_ge(turned, 4 * i + 2 * j + 2)
                    act.copy(c.y[:, 4:8, bass.ts(2 * i + j, P)],
                             bank[2 * j + 1][:].rearrange("p (k n) -> p k n", k=4)).then_inc(kept, 1)

            peeled(act, QT // 2, step)

        @block.gpsimd
        def _(pool):
            pool.memset(c.ones[:], 1.0).then_inc(ones_set, 1)
            for j, eps in enumerate((RMS_EPS, LN_EPS)):
                pool.memset(c.eps[:, j:j + 1], eps).then_inc(ones_set, 1)

        @block.vector
        def _(dve):
            def step(i, first):
                for j in range(2):
                    dve.wait_ge(turned, 4 * i + 2 * j + 1)
                    dve.tensor_copy(c.y[:, 0:4, bass.ts(2 * i + j, P)],
                                    bank[2 * j][:].rearrange("p (k n) -> p k n", k=4)).then_inc(small_kept, 1)

            peeled(dve, QT // 2, step)
            for n, (dst, b, w, v) in enumerate(small_out):
                dve.wait_ge(small_turned, n + 1)
                dve.tensor_copy(dst, v(bank[b])).then_inc(small_kept, 1)

        @block.tensor
        def _(pe):
            pe.wait_ge(consts_landed, 16)

            def step(i, first):
                for j in range(2):
                    pe.wait_ge(landed[2 * i + j], 16)
                    for half in range(2):
                        if not first:
                            if half == 0:
                                pe.wait_ge(small_kept, 2 * i + j - 1)
                            else:
                                pe.wait_ge(kept, 2 * i + j - 1)
                        for k in range(4):
                            mm = pe.transpose(bank[2 * j + half][:, k * P:(k + 1) * P],
                                              rows[:, 2 * i + j, (4 * half + k) * P:(4 * half + k + 1) * P], c.ident[:])
                        mm.then_inc(turned, 1)

            for i in range(QT // 2):
                step(i, i == 0)
            pe.wait_ge(small_landed, 16 * 14)
            pe.wait_ge(kept, QT)
            for n, (b, pieces) in enumerate(small_in):
                pe.wait_ge(small_kept, QT + max(0, n - 1))
                for src, k_rows, at, width in pieces:
                    mm = pe.transpose(bank[b][:, at:at + width], src, c.ident[0:k_rows, 0:k_rows])
                mm.then_inc(small_turned, 1)


def project_stage(nc, c, tag, w, widths, dst, norm=None, before=None, twice=False):
    pairs = (len(widths) - twice) // 2
    with ExitStack() as ctx:
        sem = lambda n: nc.alloc_semaphore(f"{n}_{tag}")
        sb = lambda n, d: [ctx.enter_context(nc.sbuf_tensor(f"{n}{j}_{tag}", [P, DC, P], d)) for j in range(2)]
        raw, w_hi, w_lo = sb("raw", F32), sb("w_hi", F32R), sb("w_lo", F32R)
        bank = [[ctx.enter_context(nc.psum_tensor(f"out{j}{g}_{tag}", [P, GW], F32)) for g in range(GROUPS)] for j in range(2)]
        norm = before(nc, ctx, c, tag) if before else norm and Norm(nc, ctx, c, tag, norm)
        landed = [sem(f"weights{j}_landed") for j in range(2)]
        hi_set = [sem(f"weights{j}_hi") for j in range(2)]
        lo_set = [sem(f"weights{j}_lo") for j in range(2)]
        done = [sem(f"product{j}_done") for j in range(2)]
        kept = [sem(f"product{j}_kept") for j in range(2)]
        block = ctx.enter_context(nc.Block())
        w_view = w.rearrange("(k p) n -> p k n", p=P)
        tail = [(j, x) for j, x in enumerate(widths[2 * pairs:])]

        def tiles(eng, one, around_first=lambda weights: weights()):
            def step(q, first):
                for j in range(2):
                    one(q, j, P, first)

            around_first(lambda: step(0, True))
            with eng.Fori(1, pairs) as q:
                step(q, False)
            for j, width in tail:
                one(pairs, j, width, False, twice and j == len(tail) - 1)

        @block.sync
        def _(sp):
            def load(q, j, width, first, double=False):
                if not first:
                    sp.wait_ge(lo_set[j], q)
                if double:
                    for i in range(2):
                        sp.dma_start(raw[j][:, :, i * ROPE:(i + 1) * ROPE], w_view[:, :, bass.ds((2 * q + j) * P, ROPE)]).then_inc(landed[j], 16)
                else:
                    sp.dma_start(raw[j][:, :, 0:width], w_view[:, :, bass.ds((2 * q + j) * P, width)]).then_inc(landed[j], 16)

            tiles(sp, load)

        @block.scalar
        def _(act):
            def round_hi(q, j, width, first, double=False):
                act.wait_ge(landed[j], 16 * q + (32 if double else 16))
                if not first:
                    act.wait_ge(done[j], 3 * q)
                act.copy(w_hi[j][:, :, 0:width], raw[j][:, :, 0:width]).then_inc(hi_set[j], 1)

            tiles(act, round_hi, lambda weights: norm.act(act, weights))

        @block.gpsimd
        def _(pool):
            def rest(q, j, width, first, double=False):
                pool.wait_ge(hi_set[j], q + 1)
                pool.tensor_tensor(w_lo[j][:, :, 0:width], raw[j][:, :, 0:width], w_hi[j][:, :, 0:width].bitcast(F32),
                                   ALU.subtract).then_inc(lo_set[j], 1)

            tiles(pool, rest, lambda weights: norm.pool(pool, weights))

        @block.tensor
        def _(pe):
            if norm:
                norm.pe(pe)

            def product(q, j, width, first, double=False):
                pe.wait_ge(lo_set[j], q + 1)
                for g in range(GROUPS):
                    if not first:
                        pe.wait_ge(kept[j], 3 * q - 2 + g)
                    elif norm and j == 0:
                        norm.wait_group(pe, g)
                    split_product(pe, bank[j][g][0:width, :], lambda k: w_hi[j][:, k, 0:width], lambda k: w_lo[j][:, k, 0:width],
                                  lambda k: c.hi[:, k, group(g)], lambda k: c.lo[:, k, group(g)], DC).then_inc(done[j], 1)

            tiles(pe, product)

        @block.vector
        def _(dve):
            if norm:
                norm.dve(dve)
                norm.wait_group(dve, GROUPS - 1)

            def keep(q, j, width, first, double=False):
                for g in range(GROUPS):
                    dve.wait_ge(done[j], 3 * q + g + 1)
                    dve.tensor_copy(dst[0:width, 2 * q + j, group(g)], bank[j][g][0:width, :]).then_inc(kept[j], 1)

            tiles(dve, keep)


def conv_stage(nc, c, t, mix):
    A_GATE, A_VAL, B_GATE, C_GATE, B_IN = range(5)
    column = {A_VAL: 0, A_GATE: 1, B_GATE: 2, C_GATE: 3, B_IN: 4}
    with ExitStack() as ctx:
        sb = lambda n, s, d=F32: ctx.enter_context(nc.sbuf_tensor(n, s, d))
        sem = lambda n: nc.alloc_semaphore(n)
        SLOT = (0, 1, 0, 1, 2)
        raw, w_hi, w_lo = ([sb(f"{n}{j}", [P, DC, P], d) for j in range(3)] for n, d in (("raw_in", F32), ("w_in_hi", F32R), ("w_in_lo", F32R)))
        gates = sb("gates", [P, 4 * TOKENS])[:]
        sig, bg, cg, bi = (gates[:, j * TOKENS:(j + 1) * TOKENS] for j in range(4))
        apad = sb("a_prompt", [P, PAD_A + SEQ])
        apad_s = sb("a_sample", [P, DEC_BATCH, PAD_A + DEC_SEQ])
        zpad = sb("z_prompt", [P, PAD_B + SEQ])
        zpad_s = sb("z_sample", [P, DEC_BATCH, PAD_B + DEC_SEQ])
        bank = [[ctx.enter_context(nc.psum_tensor(f"proj{j}{g}", [P, 512], F32)) for g in range(GROUPS)] for j in range(2)]
        landed = [sem(f"w_in{s}_landed") for s in range(5)]
        done, act_kept, glu_done = sem("projection_done"), sem("act_kept"), sem("glu_done")
        z_done, b_done = sem("z_done"), sem("b_conv_done")
        tap, tap_b = sem("tap_added"), sem("tap_b_added")
        state_set, pads_zero, tails_kept = sem("state_set"), sem("pads_zero"), sem("tails_kept")
        hi_set, lo_set = [sem(f"w_in{s}_hi") for s in range(5)], [sem(f"w_in{s}_lo") for s in range(5)]
        norm = Norm(nc, ctx, c, "mix0", [("pre", c.y, DC, ROW_MIX_PRE, c.acc)], space=(gates[:, 0:Norm.SQUARES], gates[:, Norm.SQUARES:Norm.SQUARES + Norm.ROWS]))
        turned, turned_kept, stored = sem("state_turned"), sem("state_kept"), sem("state_stored")
        block = ctx.enter_context(nc.Block())
        SA, SB = DEC_BATCH * PAD_A, DEC_BATCH * PAD_B
        pieces = [(0, PAD_A, sig[0:PAD_A, 0:CHAN]), (PAD_A, SA // 2, cg[0:SA // 2, 0:CHAN]), (PAD_A + SA // 2, SA // 2, cg[0:SA // 2, CHAN:2 * CHAN]),
                  (PAD_A + SA, PAD_B, bi[0:PAD_B, 0:CHAN]), (PAD_A + SA + PAD_B, SB, bi[0:SB, CHAN:2 * CHAN])]
        piece_bank = [bank[n // GROUPS][n % GROUPS] for n in range(len(pieces))]
        w_view = t["w_in_conv"].rearrange("l (k p) n -> p (l k) n", p=P)
        LAST = SEQ - (GROUPS - 1) * GW
        TA, TB_ = 2 * TAPS_A, 2 * TAPS_B

        @block.sync
        def _(sp):
            def step(i, first):
                for s in (A_GATE, A_VAL, B_IN, B_GATE, C_GATE):
                    if s in (B_GATE, C_GATE):
                        sp.wait_ge(lo_set[s - 2], i + 1)
                    elif not first:
                        sp.wait_ge(lo_set[s + 2 if s < 2 else s], i)
                    sp.dma_start(raw[SLOT[s]][:], w_view[:, :, bass.ds(column[s] * CHAN + i * P, P)]).then_inc(landed[s], 16)

            for i in range(CC):
                step(i, i == 0)
            sp.wait_ge(turned_kept, len(pieces))
            new = {n: t[n].rearrange("l b w c -> (l b w) c") for n in t if n.startswith("new_conv")}
            for out, (_, _, rows) in zip((new["new_conv_a_prompt"], new["new_conv_a_sample"][0:SA // 2, :], new["new_conv_a_sample"][SA // 2:SA, :],
                                          new["new_conv_b_prompt"], new["new_conv_b_sample"]), pieces):
                sp.dma_start(out, rows).then_inc(stored, 16)
            sp.wait_ge(stored, 16 * len(pieces))

        @block.tensor
        def _(pe):
            norm.pe(pe)

            def step(i, first):
                for s in range(5):
                    pe.wait_ge(lo_set[s], i + 1)
                    for g in range(GROUPS):
                        if s == 0 and first:
                            norm.wait_group(pe, g)
                        if s == A_GATE and not first:
                            pe.wait_ge(act_kept, 12 * i - 2 + g)
                        if s == A_VAL and not first:
                            pe.wait_ge(act_kept, 12 * i - 5 + g)
                        if s == B_GATE:
                            pe.wait_ge(act_kept, 12 * i + g + 1)
                        if s == C_GATE:
                            pe.wait_ge(glu_done, 4 * i + (g + 1 if g < 2 else 4))
                        if s == B_IN:
                            pe.wait_ge(act_kept, 12 * i + 3 + g + 1)
                        split_product(pe, bank[s % 2][g][:, 0:GW], lambda k: w_hi[SLOT[s]][:, k, :], lambda k: w_lo[SLOT[s]][:, k, :],
                                      lambda k: c.hi[:, k, group(g)], lambda k: c.lo[:, k, group(g)], DC).then_inc(done, 1)

            peeled(pe, CC, step)
            pe.wait_ge(act_kept, 12 * CC)
            pe.wait_ge(tails_kept, CC)
            for n, (at, width, _) in enumerate(pieces):
                for k in range(CC):
                    mm = pe.transpose(piece_bank[n][0:width, k * P:(k + 1) * P], c.tails[:, k, at:at + width], c.ident[:])
                mm.then_inc(turned, 1)

        @block.scalar
        def _(act):
            def round_hi(i, s, first):
                act.wait_ge(landed[s], 16 * i + 16)
                if s in (B_GATE, C_GATE):
                    act.wait_ge(done, 15 * i + 3 * (s - 2) + 3)
                elif not first:
                    act.wait_ge(done, 15 * i - 15 + 3 * (s + 2 if s < 2 else s) + 3)
                act.copy(w_hi[SLOT[s]][:], raw[SLOT[s]][:]).then_inc(hi_set[s], 1)

            def keep(i, s, out, func, first):
                for g in range(GROUPS):
                    act.wait_ge(done, 15 * i + 3 * s + g + 1)
                    if not first and g == 0:
                        if s == A_GATE:
                            act.wait_ge(glu_done, 4 * i)
                        elif s == B_GATE:
                            act.wait_ge(b_done, i)
                        else:
                            act.wait_ge(z_done, 4 * i)
                    act.activation(out[:, group(g)], bank[s % 2][g][:, 0:GW], func).then_inc(act_kept, 1)

            def step(i, first, last):
                keep(i, A_GATE, sig, ACT.Sigmoid, first)
                round_hi(i, B_GATE, first)
                round_hi(i, C_GATE, first)
                keep(i, B_GATE, bg, ACT.Copy, first)
                keep(i, C_GATE, cg, ACT.Copy, first)
                if not last:
                    round_hi(i + 1, A_GATE, False)
                    round_hi(i + 1, A_VAL, False)
                keep(i, B_IN, bi, ACT.Copy, first)
                if not last:
                    round_hi(i + 1, B_IN, False)

            norm.act(act, lambda: [round_hi(0, s, True) for s in (A_GATE, A_VAL, B_IN)])
            three_ends(act, CC, step)
            for n, (_, width, rows) in enumerate(pieces):
                act.wait_ge(turned, n + 1)
                act.copy(rows, piece_bank[n][0:width, 0:CHAN]).then_inc(turned_kept, 1)

        @block.gpsimd
        def _(pool):
            pool.memset(apad[:, 0:PAD_A], 0.0).then_inc(pads_zero, 1)
            pool.memset(zpad[:, 0:PAD_B], 0.0).then_inc(pads_zero, 1)

            def rest(i, s):
                pool.wait_ge(hi_set[s], i + 1)
                pool.tensor_tensor(w_lo[SLOT[s]][:], raw[SLOT[s]][:], w_hi[SLOT[s]][:].bitcast(F32), ALU.subtract).then_inc(lo_set[s], 1)

            def step(i, first, last):
                if not first:
                    pool.wait_ge(tails_kept, i)
                    pool.wait_ge(tap, TA * i)
                    pool.wait_ge(b_done, i)
                pool.tensor_copy(apad_s[:, :, 0:PAD_A],
                                 c.state[:, i, 0:SA].rearrange("p (b w) -> p b w", b=DEC_BATCH)).then_inc(state_set, 1)
                pool.tensor_copy(zpad_s[:, :, 0:PAD_B],
                                 c.state[:, i, SA:SA + DEC_BATCH * PAD_B].rearrange("p (b w) -> p b w", b=DEC_BATCH)
                                 ).then_inc(state_set, 1)
                rest(i, B_GATE)
                rest(i, C_GATE)
                pool.wait_ge(glu_done, 4 * i + 4)
                pool.wait_ge(state_set, 2 * i + 2)
                pool.tensor_copy(c.tails[:, i, 0:PAD_A], apad[:, SEQ:SEQ + PAD_A])
                pool.tensor_copy(c.tails[:, i, PAD_A:PAD_A + SA].rearrange("p (b w) -> p b w", b=DEC_BATCH),
                                 apad_s[:, :, DEC_SEQ:DEC_SEQ + PAD_A])
                if not last:
                    for s in (A_GATE, A_VAL, B_IN):
                        rest(i + 1, s)
                pool.wait_ge(z_done, 4 * i + 4)
                o = PAD_A + SA
                pool.tensor_copy(c.tails[:, i, o:o + PAD_B], zpad[:, SEQ:SEQ + PAD_B])
                pool.tensor_copy(c.tails[:, i, o + PAD_B:o + PAD_B + DEC_BATCH * PAD_B].rearrange("p (b w) -> p b w", b=DEC_BATCH),
                                 zpad_s[:, :, DEC_SEQ:DEC_SEQ + PAD_B]).then_inc(tails_kept, 1)

            norm.pool(pool, lambda: [rest(0, s) for s in (A_GATE, A_VAL, B_IN)])
            three_ends(pool, CC, step)

        @block.vector
        def _(dve):
            def steps_view(x):
                return x.rearrange("p (b s) -> p b s", b=DEC_BATCH)

            norm.dve(dve)

            def step(i, first):
                if first:
                    dve.wait_ge(pads_zero, 2)
                    norm.wait_group(dve, GROUPS - 1)
                else:
                    dve.wait_ge(tails_kept, i)
                for g in range(GROUPS):
                    dve.wait_ge(done, 15 * i + 3 * A_VAL + g + 1)
                    dve.wait_ge(act_kept, 12 * i + g + 1)
                    n = GW if g < GROUPS - 1 else LAST
                    dve.tensor_tensor(apad[:, PAD_A + g * GW:PAD_A + g * GW + n], bank[A_VAL % 2][g][:, 0:n],
                                      sig[:, g * GW:g * GW + n], ALU.mult).then_inc(glu_done, 1)
                dve.tensor_tensor(apad_s[:, :, PAD_A:], steps_view(bank[A_VAL % 2][GROUPS - 1][:, LAST:GW]),
                                  steps_view(sig[:, SEQ:]), ALU.mult).then_inc(glu_done, 1)
                dve.wait_ge(glu_done, 4 * i + 4)
                dve.wait_ge(state_set, 2 * i + 2)
                for w in range(TAPS_A):
                    wcol = c.param[:, bass.ds(PARAM_ROWS + w * CC + i, 1)]
                    for part, (src, out) in enumerate(((apad[:, w:w + SEQ], mix[:, i, 0:SEQ]),
                                                       (apad_s[:, :, w:w + DEC_SEQ], steps_view(mix[:, i, SEQ:TOKENS])))):
                        if w == 0:
                            dve.tensor_scalar(out, src, wcol, c.param[:, bass.ds(ROW_BIAS_A + i, 1)],
                                              ALU.mult, ALU.add).then_inc(tap, 1)
                        else:
                            dve.wait_ge(tap, TA * i + 2 * w + part - 1)
                            dve.scalar_tensor_tensor(out=out, in0=src, scalar=wcol, in1=out,
                                                     op0=ALU.mult, op1=ALU.add).then_inc(tap, 1)
                dve.wait_ge(act_kept, 12 * i + 12)
                for g in range(GROUPS):
                    n = GW if g < GROUPS - 1 else LAST
                    dve.tensor_tensor(zpad[:, PAD_B + g * GW:PAD_B + g * GW + n], cg[:, g * GW:g * GW + n],
                                      bi[:, g * GW:g * GW + n], ALU.mult).then_inc(z_done, 1)
                dve.tensor_tensor(zpad_s[:, :, PAD_B:], steps_view(cg[:, SEQ:]), steps_view(bi[:, SEQ:]),
                                  ALU.mult).then_inc(z_done, 1)
                dve.wait_ge(z_done, 4 * i + 4)
                for w in range(TAPS_B):
                    wcol = c.param[:, bass.ds(ROW_CONV_B + w * CC + i, 1)]
                    for part, (src, out) in enumerate(((zpad[:, w:w + SEQ], mix[:, CC + i, 0:SEQ]),
                                                       (zpad_s[:, :, w:w + DEC_SEQ], steps_view(mix[:, CC + i, SEQ:TOKENS])))):
                        if w == 0:
                            dve.tensor_scalar(out, src, wcol, None, ALU.mult).then_inc(tap_b, 1)
                        else:
                            dve.wait_ge(tap_b, TB_ * i + 2 * w + part - 1)
                            dve.scalar_tensor_tensor(out=out, in0=src, scalar=wcol, in1=out,
                                                     op0=ALU.mult, op1=ALU.add).then_inc(tap_b, 1)
                dve.wait_ge(tap_b, TB_ * i + TB_)
                dve.tensor_tensor(mix[:, CC + i, :], mix[:, CC + i, :], bg, ALU.mult).then_inc(b_done, 1)

            peeled(dve, CC, step)


def ffn_stage(nc, c, layer, t, norm):
    NB = DC * GROUPS
    PAIRS = FC // 2
    with ExitStack() as ctx:
        sb = lambda n, s, d=F32: ctx.enter_context(nc.sbuf_tensor(f"{n}{layer}", s, d))
        sem = lambda n: nc.alloc_semaphore(f"{n}{layer}")
        ps = lambda n, s: ctx.enter_context(nc.psum_tensor(f"{n}{layer}", s, F32))
        names = ("gate", "up")
        raw, w_hi, w_lo = ({n: sb(f"{what}_{n}", [P, DC, P], d)[:] for n in names}
                           for what, d in (("raw", F32), ("w_hi", F32R), ("w_lo", F32R)))
        down_space, hidden = sb("raw_down", [P, max(2 * D, Norm.SQUARES)]), sb("hidden", [P, max(TOKENS, Norm.ROWS)])
        raw["down"] = down_space[:, 0:2 * D].rearrange("p (j k n) -> p j k n", j=2, k=DC)
        w_hi["down"], w_lo["down"] = (sb(n, [P, 2, DC, P], F32R)[:] for n in ("w_hi_down", "w_lo_down"))
        hid_hi, hid_lo = sb("hidden_hi", [P, 2, TOKENS], F32R), sb("hidden_lo", [P, 2, TOKENS], F32R)
        norm = Norm(nc, ctx, c, f"ffn{layer}", norm, space=(down_space[:, 0:Norm.SQUARES], hidden[:, 0:Norm.ROWS]))
        gate_bank = [ps(f"gate_bank{g}_", [P, GW]) for g in range(GROUPS)]
        up_bank = [ps(f"up_bank{g}_", [P, GW]) for g in range(GROUPS)]
        down_bank = [norm.total, ps("down_bank1_", [P, GW])]
        landed, hi_set, lo_set = ({n: sem(f"{n}_{what}") for n in names + ("down",)} for what in ("landed", "hi", "lo"))
        gate_done, up_done, down_done = sem("gate_done"), sem("up_done"), sem("down_done")
        silu_done, hidden_set, hid_hi_set, hid_lo_set = sem("silu_done"), sem("hidden_set"), sem("hidden_hi_set"), sem("hidden_lo_set")
        down_free = sem("down_bank_free")
        block = ctx.enter_context(nc.Block())
        view = {n: t[f"w_ffn_{n}"][layer].rearrange("(k p) f -> p k f", p=P) for n in names}
        down_view = t["w_ffn_down"][layer].rearrange("(q j p) n -> q p j n", p=P, j=2)

        @block.sync
        def _(sp):
            def load(name, f, first):
                if not first:
                    sp.wait_ge(lo_set[name], f)
                sp.dma_start(raw[name], view[name][:, :, bass.ds(f * P, P)]).then_inc(landed[name], 16)

            def step(q, first, last):
                load("gate", 2 * q + 1, False)
                load("up", 2 * q + 1, False)
                if first:
                    sp.wait_ge(norm.scaled, len(norm.units))
                else:
                    sp.wait_ge(lo_set["down"], q)
                sp.dma_start(down_space[:, 0:2 * D].rearrange("p (j n) -> p j n", j=2), down_view[q]).then_inc(landed["down"], 16)
                if not last:
                    load("gate", 2 * q + 2, False)
                    load("up", 2 * q + 2, False)

            load("gate", 0, True)
            load("up", 0, True)
            three_ends(sp, PAIRS, step)

        @block.tensor
        def _(pe):
            norm.pe(pe)

            def down(q):
                pe.wait_ge(lo_set["down"], q + 1)
                for m in range(DC):
                    for g in range(GROUPS):
                        n = m * GROUPS + g
                        if m == 0:
                            pe.wait_ge(hid_lo_set, 6 * q + 3 + g + 1)
                        pe.wait_ge(down_free, NB * q + n + 1)
                        split_product(pe, down_bank[n % 2][:], lambda k: w_hi["down"][:, k, m, :], lambda k: w_lo["down"][:, k, m, :],
                                      lambda k: hid_hi[:, k, group(g)], lambda k: hid_lo[:, k, group(g)], 2).then_inc(down_done, 1)

            def half(f, first, name, bank, used, done):
                pe.wait_ge(lo_set[name], f + 1)
                for g in range(GROUPS):
                    if not first:
                        pe.wait_ge(used, 3 * f - 2 + g)
                    elif name == "gate":
                        norm.wait_group(pe, g)
                    split_product(pe, bank[g][:], lambda k: w_hi[name][:, k, :], lambda k: w_lo[name][:, k, :],
                                  lambda k: c.hi[:, k, group(g)], lambda k: c.lo[:, k, group(g)], DC).then_inc(done, 1)

            def step(q, first):
                half(2 * q, first, "gate", gate_bank, silu_done, gate_done)
                if not first:
                    down(q - 1)
                half(2 * q, first, "up", up_bank, hidden_set, up_done)
                half(2 * q + 1, False, "gate", gate_bank, silu_done, gate_done)
                half(2 * q + 1, False, "up", up_bank, hidden_set, up_done)

            peeled(pe, PAIRS, step)
            down(PAIRS - 1)

        @block.scalar
        def _(act):
            def round_hi(name, f, left=None, count=0):
                act.wait_ge(landed[name], 16 * f + 16)
                if left is not None:
                    act.wait_ge(left, count)
                act.copy(w_hi[name], raw[name]).then_inc(hi_set[name], 1)

            def step(q, first, last):
                for j in range(2):
                    f = 2 * q + j
                    for g in range(GROUPS):
                        act.wait_ge(gate_done, 3 * f + g + 1)
                        if j or not first:
                            act.wait_ge(hid_lo_set, 3 * f - 2 + g)
                        act.activation(hidden[:, group(g)], gate_bank[g][:], ACT.Silu).then_inc(silu_done, 1)
                    if not (last and j):
                        round_hi("gate", f + 1, gate_done, 3 * f + 3)
                    for g in range(GROUPS):
                        act.wait_ge(hidden_set, 3 * f + g + 1)
                        act.copy(hid_hi[:, j, group(g)], hidden[:, group(g)]).then_inc(hid_hi_set, 1)
                    if not (last and j):
                        round_hi("up", f + 1, up_done, 3 * f + 3)
                    if j == 0:
                        round_hi("down", q, *(() if first else (down_done, NB * q)))

            norm.act(act, lambda: [round_hi(name, 0) for name in names])
            three_ends(act, PAIRS, step)

        @block.gpsimd
        def _(pool):
            def rest(name, f):
                pool.wait_ge(hi_set[name], f + 1)
                pool.tensor_tensor(w_lo[name], raw[name], w_hi[name].bitcast(F32), ALU.subtract).then_inc(lo_set[name], 1)

            def step(q, first, last):
                rest("gate", 2 * q + 1)
                rest("up", 2 * q + 1)
                rest("down", q)
                if not last:
                    rest("gate", 2 * q + 2)
                    rest("up", 2 * q + 2)

            norm.pool(pool, lambda: [rest(name, 0) for name in names])
            three_ends(pool, PAIRS, step)

        @block.vector
        def _(dve):
            norm.dve(dve)
            norm.wait_group(dve, GROUPS - 1)
            for j in range(2):
                dve.memset(c.acc[:, j * DC // 2:(j + 1) * DC // 2, :], 0.0).then_inc(down_free, 1)

            def add(q):
                dve.wait_ge(down_free, NB * q + 2)
                for m in range(DC):
                    for g in range(GROUPS):
                        n = m * GROUPS + g
                        dve.wait_ge(down_done, NB * q + n + 1)
                        dve.tensor_tensor(c.acc[:, m, group(g)], c.acc[:, m, group(g)], down_bank[n % 2][:],
                                          ALU.add).then_inc(down_free, 1)

            def step(q, first):
                if not first:
                    add(q - 1)
                for j in range(2):
                    f = 2 * q + j
                    for g in range(GROUPS):
                        dve.wait_ge(up_done, 3 * f + g + 1)
                        dve.wait_ge(silu_done, 3 * f + g + 1)
                        dve.tensor_tensor(hidden[:, group(g)], up_bank[g][:], hidden[:, group(g)], ALU.mult).then_inc(hidden_set, 1)
                    for g in range(GROUPS):
                        dve.wait_ge(hid_hi_set, 3 * f + g + 1)
                        dve.tensor_tensor(hid_lo[:, j, group(g)], hidden[:, group(g)], hid_hi[:, j, group(g)].bitcast(F32),
                                          ALU.subtract).then_inc(hid_lo_set, 1)

            peeled(dve, PAIRS, step)
            add(PAIRS - 1)


def latent_stage(nc, c, t, k):
    with ExitStack() as ctx:
        sb = lambda n, s, d=F32: ctx.enter_context(nc.sbuf_tensor(n, s, d))
        sem = lambda n: nc.alloc_semaphore(n)
        by_cos, by_sin = sb("key_by_cos", [P, TOKENS]), sb("key_by_sin", [P, TOKENS])
        key_rows, latent_rows = sb("key_rows", [P, QT + 1, ROPE]), sb("latent_rows", [P, QT + 1, KV_LORA])
        pages, offset = sb("pages", [P, DEC_BATCH], I32), sb("run_offset", [P, 3])
        rot = [ctx.enter_context(nc.psum_tensor(f"key_rotated{g}", [P, GW], F32)) for g in range(GROUPS)]
        bank = [ctx.enter_context(nc.psum_tensor(f"latent_turn{j}", [P, 512], F32)) for j in range(2)]
        norm = Norm(nc, ctx, c, "lat", [("plain", c.acc, QC, ROW_QN, c.acc), ("plain", c.acc[:, QC:QC + LC, :], LC, ROW_KVN, k.latent)])
        consts, rotated, key_set = sem("rope_consts"), sem("key_turned"), sem("key_set")
        cos_set, sin_set = sem("key_by_cos_set"), sem("key_by_sin_set")
        turned, kept, stored = sem("latent_turned"), sem("latent_kept"), sem("latent_stored")
        copied, zeroed = sem("sample_keys_copied"), sem("rows_zeroed")
        index_landed, ids_set = sem("page_table_landed"), sem("run_ids_set")
        block = ctx.enter_context(nc.Block())
        raw = c.acc[:, QC + LC, :]
        uses = []
        for i in range(0, QT, 2):
            uses.append(([(k.latent[:, l, (i + j) * P:(i + j + 1) * P], P, (LC * j + l) * P) for j in range(2) for l in range(LC)],
                         P, 2 * KV_LORA, latent_rows[:, i:i + 2, :].rearrange("p a d -> p (a d)")))
        uses.append(([(k.latent[:, l, SEQ:TOKENS], P, l * P) for l in range(LC)], SAMPLE, KV_LORA, latent_rows[0:SAMPLE, QT, :]))
        LATENT_USES = len(uses)
        uses.append(([(k.key[0][0:ROPE, i * P:(i + 1) * P], ROPE, i * ROPE) for i in range(QT)], P, QT * ROPE,
                     key_rows[:, 0:QT, :].rearrange("p a d -> p (a d)")))
        uses.append(([(k.key[0][0:ROPE, SEQ:TOKENS], ROPE, 0)], SAMPLE, ROPE, key_rows[0:SAMPLE, QT, :]))

        @block.scalar
        def _(act):
            act.dma_start(k.swap[:], t["rope_swap"]).then_inc(consts, 16)
            act.dma_start(k.cos[:], t["rope_cos"]).then_inc(consts, 16)
            act.dma_start(k.sin[:], t["rope_sin"]).then_inc(consts, 16)
            act.dma_start(k.causal[:], t["causal"]).then_inc(consts, 16)
            norm.act(act)
            for n, (_, rows, columns, dst) in enumerate(uses):
                act.wait_ge(turned, n + 1)
                act.copy(dst, bank[n % 2][0:rows, 0:columns]).then_inc(kept, 1)

        @block.tensor
        def _(pe):
            norm.pe(pe)
            pe.wait_ge(consts, 64)
            for g in range(GROUPS):
                pe.matmul(rot[g][:], k.swap[:], raw[:, group(g)], start=True, stop=True).then_inc(rotated, 1)
            for n, (sources, out_rows, _, _) in enumerate(uses):
                if n == 0:
                    pe.wait_ge(norm.scaled, len(norm.units))
                if n == LATENT_USES:
                    pe.wait_ge(key_set, 2)
                if n >= 2:
                    pe.wait_ge(kept, n - 1)
                for src, rows, at in sources:
                    mm = pe.transpose(bank[n % 2][0:out_rows, at:at + rows], src, c.ident[0:rows, 0:rows])
                mm.then_inc(turned, 1)

        @block.vector
        def _(dve):
            norm.dve(dve)
            dve.wait_ge(consts, 64)
            for g in range(GROUPS):
                dve.wait_ge(rotated, g + 1)
                dve.tensor_tensor(by_sin[:, group(g)], rot[g][:], k.sin[:, group(g)], ALU.mult).then_inc(sin_set, 1)
            dve.wait_ge(sin_set, GROUPS)
            dve.wait_ge(cos_set, 1)
            for j in range(2):
                own = slice(j * ROPE, (j + 1) * ROPE)
                dve.tensor_tensor(k.key[j][own, :], by_cos[own, :], by_sin[own, :], ALU.add).then_inc(key_set, 1)
            dve.wait_ge(index_landed, 32)
            for n, per_page in enumerate((2 * RUNS_PER_PAGE, 2 * RUNS_PER_PAGE, RUNS_PER_PAGE)):
                dve.tensor_scalar(c.run_ids[:, n, :], pages[:], float(per_page), offset[:, n:n + 1], ALU.mult, ALU.add).then_inc(ids_set, 1)

        @block.gpsimd
        def _(pool):
            pool.memset(k.key[0][ROPE:P, :], 0.0).then_inc(zeroed, 1)
            pool.memset(k.key[1][0:ROPE, :], 0.0).then_inc(zeroed, 1)
            pool.wait_ge(zeroed, 2)
            pool.wait_ge(consts, 64)
            pool.tensor_tensor(by_cos[:], raw, k.cos[:], ALU.mult).then_inc(cos_set, 1)
            pool.wait_ge(cos_set, 1)
            pool.wait_ge(norm.scaled, len(norm.units))
            pool.tensor_copy(c.new_latent[:], k.latent[:, :, SEQ:TOKENS]).then_inc(copied, 1)
            pool.wait_ge(key_set, 2)
            pool.wait_ge(copied, 1)
            pool.tensor_copy(c.new_key[:], k.key[0][:, SEQ:TOKENS]).then_inc(copied, 1)
            pool.wait_ge(kept, LATENT_USES)
            pool.wait_ge(copied, 2)
            pool.tensor_copy(c.new_rows[:], latent_rows[0:SAMPLE, QT, :]).then_inc(copied, 1)

        @block.sync
        def _(sp):
            sp.dma_start(pages[:], t["pages"]).then_inc(index_landed, 16)
            sp.dma_start(offset[:], t["run_offset"]).then_inc(index_landed, 16)
            sp.wait_ge(kept, LATENT_USES)
            sp.dma_start(t["new_kv_latent_prompt"].rearrange("l b (n p) d -> p (l b n) d", p=P), latent_rows[:, 0:QT, :]).then_inc(stored, 16)
            sp.dma_start(t["new_kv_latent_sample"].rearrange("l b s d -> (l b s) d"), latent_rows[0:SAMPLE, QT, :]).then_inc(stored, 16)
            sp.wait_ge(kept, len(uses))
            sp.dma_start(t["new_k_rope_prompt"].rearrange("l b (n p) d -> p (l b n) d", p=P), key_rows[:, 0:QT, :]).then_inc(stored, 16)
            sp.dma_start(t["new_k_rope_sample"].rearrange("l b s d -> (l b s) d"), key_rows[0:SAMPLE, QT, :]).then_inc(stored, 16)
            sp.wait_ge(stored, 64)


ORDER = ("S0 M0 E0 S1 M1 E1 N0 F0 F1 S2 M2 T0 N1 E2 F2 S3 M3 T1 N2 E3 F3 S4 M4 T2 N3 E4 F4 S5 M5 T3 N4 E5 F5 "
         "P0 O0 S6 M6 T4 N5 E6 F6 S7 M7 T5 N6 E7 F7 T6 N7 A0 T7 F8 P1 O1").split()
PREPARE = [("QN0", "QN1"), ("QN2", "QR0"), ("KN0", "QR1"), ("KN1", "QR2"), ("SW0",), ("SW1", "V0"), ("SW2", "UK"), ("V1",), ("LAT",)]


def banks_of(i):
    return [list(range(a, min(a + 4, i + 1))) for a in range(0, i + 1, 4)]


def prepare_items(f, pair_first):
    return [x for x in PREPARE[f] if pair_first or x[:2] not in ("QR", "SW")]


def attention_stage(nc, c, t, k, cq):
    with ExitStack() as ctx:
        sb = lambda n, s, d=F32: ctx.enter_context(nc.sbuf_tensor(n, s, d))
        sem = lambda n: nc.alloc_semaphore(n)
        ps = lambda n, s: ctx.enter_context(nc.psum_tensor(n, s, F32))
        two = lambda n, s: [sb(f"{n}{j}", s) for j in range(2)]
        w_qn, w_uk, w_uv = two("w_q_nope", [P, QC, NOPE]), two("w_uk", [P, LC, NOPE]), two("w_uv", [P, LC, VDIM])
        w_qr, w_ukT = sb("w_q_rope", [P, QC, 2, ROPE]), sb("w_uk_turned", [P, LC, P])
        q_nope, q_rope, q_raw, by_sin = [c.acc[:, QC + j, :] for j in range(2)], c.acc[:, QC + 2, :], c.acc[:, QC + 3, :], c.acc[:, QC + 4, :]
        k_nope, v_rows = two("k_nope", [P, SEQ]), two("v_rows", [P, QT, VDIM])
        prob = two("prob", [P, SEQ])
        probT = [sb(f"prob_turned{i}", [P, 4 * (i + 1), 512]) for i in range(2)]
        top, bias, total, inv = (sb(n, [P, QT]) for n in ("row_max", "row_bias", "row_total", "row_inverse"))
        score = [ps(f"score{j}", [P, SEQ]) for j in range(2)]
        sum_bank = [ps(f"sum_bank{j}", [P, 512]) for j in range(2)]
        misc = [ps(f"misc{j}", [P, 512]) for j in range(2)]
        w_landed, w_qr_landed = [sem(f"head_weights{j}_landed") for j in range(2)], sem("rope_weights_landed")
        misc_done, kept = sem("misc_done"), {"act": sem("misc_kept_act"), "dve": sem("misc_kept_dve")}
        sum_done, sum_kept = sem("sum_done"), sem("sum_kept")
        by_cos_set, rope_added, stashed = sem("by_cos_set"), sem("rope_added"), sem("stashed")
        scored, masked, topped, biased = sem("scored"), sem("masked"), sem("topped"), sem("biased")
        exp_done, inverted, prob_set = sem("exp_done"), sem("inverted"), sem("prob_set")
        block = ctx.enter_context(nc.Block())
        PAIRS = HEADS // 2

        def keeper(name):
            return "dve" if name[:2] == "SW" else "act"

        FIRST = [(1, x) for f in range(len(PREPARE)) for x in prepare_items(f, True)]
        PAIR = []
        for j in range(2):
            for what in ORDER:
                if what[0] == "F":
                    PAIR += [(j, x) for x in prepare_items(int(what[1]), j == 1)]
                elif what[0] == "T":
                    PAIR += [(j, f"{what}.{n}") for n in range(len(banks_of(int(what[1]))))]
        LAST = [u for u in PAIR if u[0] == 0 or u[1][0] == "T"]
        assert len(PAIR) % 2 == 0 and all(keeper(u[1]) == "act" for u in FIRST[-2:] + PAIR[-2:])

        class Use:

            def __init__(self, p, j, name):
                self.uses = FIRST if p is None else LAST if isinstance(p, int) and p == PAIRS - 1 else PAIR
                self.p, self.n = p, self.uses.index((j, name))
                self.keeper = keeper(name)
                self.index = self.n if p is None else len(PAIR) * p + len(FIRST) + self.n
                self.bank = misc[(self.n + (0 if p is None else len(FIRST))) % 2]
                self.done = self.index + 1

            def kept_with(self, n, who):
                of = lambda uses: sum(keeper(x) == who for _, x in uses)
                start = 0 if self.p is None else of(PAIR) * self.p + of(FIRST)
                return start + (of(self.uses[:n + 1]) if n >= 0 else -of(PAIR[len(PAIR) + n + 1:]))

            def wait_free(self, pe):
                n = self.n - 2
                if n >= 0 or self.p is not None:
                    who = keeper((self.uses if n >= 0 else PAIR)[n][1])
                    pe.wait_ge(kept[who], self.kept_with(n, who))

            def wait_kept(self, eng):
                eng.wait_ge(kept[self.keeper], self.kept_with(self.n, self.keeper))

        def prepared_in(p, j, first, name):
            if j == 1:
                return Use(p, 0, name)
            return Use(None, 1, name) if first else Use(p - 1, 1, name)

        w_uq = t["w_uq"].rearrange("l (k p) n -> p (l k) n", p=P)
        uk_view = t["w_uk"].rearrange("l (k p) h n -> p (l k) (h n)", p=P)
        uv_view = t["w_uv"].rearrange("l (k p) h n -> p (l k) (h n)", p=P)

        @block.sync
        def _(sp):
            def load_head(h):
                j = h % 2
                if h >= 2:
                    sp.wait_ge(misc_done, prepared_in(h // 2 - 1, j, h == 2, "LAT").done)
                at = h * (NOPE + ROPE)
                sp.dma_start(w_qn[j][:], w_uq[:, :, at:at + NOPE]).then_inc(w_landed[j], 16)
                sp.dma_start(w_uk[j][:], uk_view[:, :, h * NOPE:(h + 1) * NOPE]).then_inc(w_landed[j], 16)
                sp.dma_start(w_uv[j][:], uv_view[:, :, h * VDIM:(h + 1) * VDIM]).then_inc(w_landed[j], 16)
                if j == 0:
                    for i in range(2):
                        at = (h + i) * (NOPE + ROPE) + NOPE
                        sp.dma_start(w_qr[:, :, i, :], w_uq[:, :, at:at + ROPE]).then_inc(w_qr_landed, 16)

            for h in range(HEADS):
                load_head(h)

        @block.gpsimd
        def _(pool):
            pool.wait_ge(scored, QT)
            pool.indirect_dma_start(c.first_latents[:], None, half_runs(t),
                                    bass.IndirectOffsetOnAxis(ap=c.run_ids[:, 0, 0:1], axis=0)).then_inc(c.first_landed, 16)

        @block.tensor
        def _(pe):
            def item(p, j, name, n, s):
                use = Use(p, j, name)
                if name == "QN0":
                    pe.wait_ge(w_landed[s], 48 * n + 48)
                if name == "QR0":
                    pe.wait_ge(w_qr_landed, 32 * n + 32)
                if name == "LAT":
                    Use(p, j, "UK").wait_kept(pe)
                if name[:2] == "SW":
                    Use(p, j, "QR" + name[2]).wait_kept(pe)
                use.wait_free(pe)
                b, g = use.bank, int(name[-1]) if name[-1].isdigit() else 0
                if name[:2] in ("QN", "QR"):
                    for i in range(QC):
                        w = w_qn[s][:, i, :] if name[1] == "N" else w_qr[:, i].rearrange("p j n -> p (j n)")
                        mm = pe.matmul(b[:, 0:GW], w, cq[:, i, group(g)], start=(i == 0), stop=(i == QC - 1))
                elif name[:2] == "SW":
                    mm = pe.matmul(b[:, 0:GW], k.swap[:], q_raw[:, group(g)], start=True, stop=True)
                elif name[:2] == "KN":
                    for l in range(LC):
                        mm = pe.matmul(b[:], w_uk[s][:, l, :], k.latent[:, l, g * 512:(g + 1) * 512], start=(l == 0), stop=(l == LC - 1))
                elif name[0] == "V":
                    for i in range(4):
                        keys = slice((4 * g + i) * P, (4 * g + i + 1) * P)
                        for l in range(LC):
                            mm = pe.matmul(b[:, i * P:(i + 1) * P], k.latent[:, l, keys], w_uv[s][:, l, :], start=(l == 0), stop=(l == LC - 1))
                elif name == "UK":
                    for l in range(LC):
                        mm = pe.transpose(b[:, l * P:(l + 1) * P], w_uk[s][:, l, :], c.ident[:])
                else:
                    for l in range(LC):
                        mm = pe.matmul(b[:, l * SAMPLE:(l + 1) * SAMPLE], w_ukT[:, l, :], q_nope[s][:, SEQ:TOKENS], start=True, stop=True)
                mm.then_inc(misc_done, 1)

            def head(p, j, first, last):
                prepared_in(p, j, first, "LAT").wait_kept(pe)
                if j == 0:
                    pe.wait_ge(rope_added, p + 1)
                n = 2 * QT * p + QT * j
                for what in ORDER:
                    i = int(what[1])
                    if what[0] == "S":
                        if not (first and j == 0 and i < 2):
                            pe.wait_ge(exp_done, n + i - 1)
                        q = slice(i * P, (i + 1) * P)
                        for a in range(0, (i + 1) * P, 512):
                            keys = slice(a, min(a + 512, (i + 1) * P))
                            pe.matmul(score[i % 2][:, keys], q_nope[j][:, q], k_nope[j][:, keys], start=True, stop=False)
                            mm = pe.matmul(score[i % 2][:, keys], q_rope[:, q], k.key[j][:, keys], start=False, stop=True)
                        mm.then_inc(scored, 1)
                    elif what[0] == "T":
                        pe.wait_ge(prob_set, n + i + 1)
                        for m, tiles in enumerate(banks_of(i)):
                            use = Use(p, j, f"{what}.{m}")
                            use.wait_free(pe)
                            for x, kt in enumerate(tiles):
                                mm = pe.transpose(use.bank[:, x * P:(x + 1) * P], prob[i % 2][:, kt * P:(kt + 1) * P], c.ident[:])
                            mm.then_inc(misc_done, 1)
                    elif what[0] == "P":
                        Use(p, j, f"T{4 * i + 3}.{i}").wait_kept(pe)
                        if not (first and j == 0):
                            pe.wait_ge(sum_kept, 4 * p + 2 * j + i - 1)
                        tiles = 4 * (i + 1)
                        for kt in range(tiles):
                            q0 = max(kt - 4 * i, 0) * P
                            mm = pe.matmul(sum_bank[i][:, q0:512], v_rows[j][:, kt, :], probT[i][:, kt, q0:512],
                                           start=(kt == 0), stop=(kt == tiles - 1))
                        mm.then_inc(sum_done, 1)
                    elif what[0] == "F" and not (last and j == 1):
                        for name in prepare_items(i, j == 1):
                            item(p, j, name, p + j, 1 - j)

            for _, name in FIRST:
                item(None, 1, name, 0, 0)

            def pair(p, first, last):
                for j in range(2):
                    head(p, j, first, last)

            three_ends(pe, PAIRS, pair)

        @block.scalar
        def _(act):
            def item(p, j, name, n, s, first):
                use = Use(p, j, name)
                if use.keeper != "act":
                    return
                b, g = use.bank, int(name[-1]) if name[-1].isdigit() else 0
                act.wait_ge(misc_done, use.done)
                if name == "QR0" and not first:
                    act.wait_ge(rope_added, n)
                if name[:2] in ("QN", "QR"):
                    dst, src = (q_nope[s] if name[1] == "N" else q_raw)[:, group(g)], b[:, 0:GW]
                elif name[:2] == "KN":
                    dst, src = k_nope[s][:, g * 512:(g + 1) * 512], b[:]
                elif name[0] == "V":
                    dst, src = v_rows[s][:, 4 * g:4 * g + 4, :], b[:].rearrange("p (k n) -> p k n", k=4)
                elif name == "UK":
                    dst, src = w_ukT[:], b[:, 0:LC * P].rearrange("p (l n) -> p l n", l=LC)
                else:
                    dst = c.q_lat_s[:, :, bass.ds(2 * n + s, 1), :].rearrange("p l h n -> p l (h n)")
                    src = b[:, 0:LC * SAMPLE].rearrange("p (l n) -> p l n", l=LC)
                act.copy(dst, src).then_inc(kept["act"], 1)

            def pair(p, first, last):
                for j in range(2):
                    for what in ORDER:
                        i = int(what[1])
                        if what[0] == "E":
                            act.wait_ge(biased, 2 * QT * p + QT * j + i + 1)
                            act.activation(prob[i % 2][:, 0:(i + 1) * P], score[i % 2][:, 0:(i + 1) * P], ACT.Exp,
                                           bias=bias[:, i:i + 1], scale=SM_SCALE, accum_out=total[:, i:i + 1]).then_inc(exp_done, 1)
                        elif what[0] == "T":
                            for m, tiles in enumerate(banks_of(i)):
                                use, n = Use(p, j, f"{what}.{m}"), len(tiles)
                                act.wait_ge(misc_done, use.done)
                                act.copy(probT[i // 4][:, tiles[0]:tiles[0] + n, (i % 4) * P:(i % 4 + 1) * P],
                                         use.bank[:, 0:n * P].rearrange("p (n q) -> p n q", n=n)).then_inc(kept["act"], 1)
                        elif what[0] == "F" and not (last and j == 1):
                            for name in prepare_items(i, j == 1):
                                item(p, j, name, p + j, 1 - j, False)

            for _, name in FIRST:
                item(None, 1, name, 0, 0, True)
            three_ends(act, PAIRS, pair)

        @block.vector
        def _(dve):
            def rotate(p, name, n, first):
                use, g = Use(p, 1, name), int(name[2])
                dve.wait_ge(misc_done, use.done)
                if g == 0 and not first:
                    dve.wait_ge(rope_added, n)
                dve.tensor_tensor(by_sin[:, group(g)], use.bank[:, 0:GW], k.sin[:, group(g)], ALU.mult).then_inc(kept["dve"], 1)
                dve.tensor_tensor(q_raw[:, group(g)], q_raw[:, group(g)], k.cos[:, group(g)], ALU.mult).then_inc(by_cos_set, 1)

            def add(n):
                dve.wait_ge(kept["dve"], GROUPS * n + GROUPS)
                dve.wait_ge(by_cos_set, GROUPS * n + GROUPS)
                dve.tensor_tensor(q_rope, q_raw, by_sin, ALU.add).then_inc(rope_added, 1)
                dve.wait_ge(rope_added, n + 1)
                dve.tensor_copy(c.q_rope_s[:, bass.ds(n, 1), :].rearrange("p h n -> p (h n)"), q_rope[:, SEQ:TOKENS]).then_inc(stashed, 1)

            def pair(p, first, last):
                for j in range(2):
                    base = 2 * QT * p + QT * j
                    for what in ORDER:
                        i = int(what[1])
                        n = base + i + 1
                        if what[0] == "M":
                            dve.wait_ge(scored, n)
                            own = slice(i * P, (i + 1) * P)
                            dve.tensor_tensor(score[i % 2][:, own], score[i % 2][:, own], k.causal[:], ALU.add).then_inc(masked, 1)
                            dve.wait_ge(masked, n)
                            dve.tensor_reduce(top[:, i:i + 1], score[i % 2][:, 0:(i + 1) * P], AX_X, ALU.max).then_inc(topped, 1)
                            dve.wait_ge(topped, n)
                            dve.tensor_scalar(bias[:, i:i + 1], top[:, i:i + 1], -SM_SCALE, None, ALU.mult).then_inc(biased, 1)
                        elif what[0] == "N":
                            dve.wait_ge(exp_done, n)
                            dve.reciprocal(inv[:, i:i + 1], total[:, i:i + 1]).then_inc(inverted, 1)
                            dve.wait_ge(inverted, n)
                            dve.tensor_scalar(prob[i % 2][:, 0:(i + 1) * P], prob[i % 2][:, 0:(i + 1) * P], inv[:, i:i + 1], None,
                                              ALU.mult).then_inc(prob_set, 1)
                        elif what[0] == "O":
                            dve.wait_ge(sum_done, 4 * p + 2 * j + i + 1)
                            dve.tensor_copy(c.value[:, bass.ds(2 * p + j, 1), i * 512:(i + 1) * 512].rearrange("p h n -> p (h n)"),
                                            sum_bank[i][:]).then_inc(sum_kept, 1)
                        elif j == 1 and not last:
                            if what[0] == "F":
                                for name in prepare_items(i, True):
                                    if keeper(name) == "dve":
                                        rotate(p, name, p + 1, False)
                            elif what[0] == "A":
                                add(p + 1)

            for g in range(GROUPS):
                rotate(None, f"SW{g}", 0, True)
            add(0)
            three_ends(dve, PAIRS, pair)


def half_runs(t):
    return t["cache_kv_latent"].rearrange("l n (r s) d -> (l n r) (s d)", s=RUN // 2)


def sample_stage(nc, c, t):
    PER = 4
    PAIRS = RUN // (2 * PER)
    ROWS = HEADS * DEC_SEQ
    HALF = PER * P
    KEYS = 2 * HALF
    with ExitStack() as ctx:
        sb = lambda n, s, d=F32: ctx.enter_context(nc.sbuf_tensor(n, s, d))
        sem = lambda n: nc.alloc_semaphore(n)
        ps = lambda n, s: ctx.enter_context(nc.psum_tensor(n, s, F32))
        ids = c.run_ids
        new_mask = sb("new_mask", [ROWS, DEC_BATCH, SAMPLE])
        own_query = sb("own_query", [P, 2, ROWS])
        latent = [[sb(f"cache_latent{j}_{part}", [P, RUN // 2 * KV_LORA]) if (j, part) != (0, "first") else c.first_latents
                   for part in ("first", "second")] for j in range(2)]
        rope = [sb(f"cache_rope{j}", [P, RUN * ROPE]) for j in range(2)]
        rope_both = sb("q_rope_both", [P, 2, HEADS, SAMPLE])
        q_b = [sb(f"q_lat_batch{j}", [P, LC, HEADS, DEC_SEQ]) for j in range(2)]
        qr_b = [sb(f"q_rope_batch{j}", [P, 2, HEADS, DEC_SEQ]) for j in range(2)]
        row_max, bias, row_total = sb("s_row_max", [P, 1]), sb("s_bias", [P, 1]), sb("s_row_total", [P, 1])
        diagonal, query_max, own_max = sb("s_max_diagonal", [P, P]), sb("s_query_max", [P, ROWS]), sb("s_own_max", [P, ROWS])
        inv, out_rows = sb("s_inverse", [ROWS, 1]), sb("s_out_rows", [ROWS, KV_LORA])
        flat = c.acc[:].rearrange("p a n -> p (a n)")
        at = iter(range(0, DC * TOKENS, ROWS))

        def scratch(n):
            taken = [next(at) for _ in range(n // ROWS)]
            return flat[:, taken[0]:taken[0] + n]

        scores, probs = scratch(KEYS + SAMPLE), scratch(KEYS + SAMPLE)
        probT, new_probT = scratch(KEYS).rearrange("p (k q) -> p k q", q=P), scratch(ROWS)
        keysT = [{k: scratch(HALF) for k in ((0, 0), (0, 1), (1, 0), (1, 1), "rope")} for _ in range(2)]
        ring = [ps(f"turn_bank{s}", [P, HALF]) for s in range(4)]
        score = [ps(f"s_score{s}", [P, HALF]) for s in range(2)]
        value_bank = score[0][:, 0:HEADS * SAMPLE].rearrange("p (h n) -> p h n", h=HEADS)
        w_uv = sb("w_uv_all", [P, LC, HEADS * VDIM])
        w_uv_landed, values_done, values_kept = sem("w_uv_all_landed"), sem("values_done"), sem("values_kept")
        out_bank, work = ps("s_out", [ROWS, KV_LORA]), ps("s_work", [P, 512])
        spread_max, total, new_score = work[:, 0:P], work[0:ROWS, P:P + 1], work[0:ROWS, 160:160 + SAMPLE]
        consts, crossed = sem("s_consts"), sem("q_rope_crossed")
        landed = [[sem(f"latent{j}_first_landed") if j else c.first_landed, sem(f"latent{j}_second_landed"), sem(f"rope{j}_landed")] for j in range(2)]
        half_left = sem("latent_first_left")
        zeroed, q_half_set, q_set, new_empty = sem("s_zeroed"), sem("q_rope_half_set"), sem("s_q_set"), sem("s_new_empty")
        turned = sem("s_turned")
        kept = {"act": sem("s_turned_kept_act"), "dve": sem("s_turned_kept_dve")}
        scored, score_kept = sem("s_scored"), sem("s_score_kept")
        maxed, diagonal_set, max_spread, query_maxed, own_set, biased = (sem(f"s_{n}") for n in (
            "row_maxed", "diagonal_set", "max_spread", "query_maxed", "own_max_set", "biased"))
        exp_done, batch_done, inverted, out_set = sem("s_exp_done"), sem("s_batch_done"), sem("s_inverted"), sem("s_out_set")
        block = ctx.enter_context(nc.Block())
        cache_l = half_runs(t)
        cache_r = t["cache_k_rope"].rearrange("l n (r s) d -> (l n r) (s d)", s=RUN)

        def keys_uses(m):
            return [(("keys", m, (0, 0)), "act"), (("keys", m, (0, 1)), "dve"), (("keys", m, (1, 0)), "act"),
                    (("keys", m, (1, 1)), "dve"), (("keys", m, "rope"), "act")]

        EARLIER = [(("probs", 0), "act"), (("probs", 1), "dve"), (("new",), "dve")]
        OUT = [(("out",), "dve")]
        USES = keys_uses(0) + keys_uses(1) + EARLIER + keys_uses(2) + OUT + keys_uses(3)
        FIRST = sum((keys_uses(m) for m in range(PAIRS)), [])
        LISTS = {0: FIRST, 1: USES, 2: USES, "after": EARLIER + OUT}
        assert USES[-4:] == FIRST[-4:] and len(FIRST) % 4 == 0 and len(USES) % 4 == 0

        class Use:

            def __init__(self, b, before, key):
                uses = LISTS[before]
                n = [k for k, _ in uses].index(key)
                self.base = len(USES) * b + len(FIRST) - len(USES) if before else 0
                self.uses, self.b, self.before, self.n = uses, b, before, n
                self.bank, self.keeper, self.done = ring[n % 4], uses[n][1], self.base + n + 1

            def kept_with(self, n, who):
                of = lambda uses: sum(e == who for _, e in uses)
                start = of(USES) * self.b + of(FIRST) - of(USES) if self.before else 0
                return start + (of(self.uses[:n + 1]) if n >= 0 else -of(USES[len(USES) + n + 1:]))

            def wait_kept(self, pe):
                pe.wait_ge(kept[self.keeper], self.kept_with(self.n, self.keeper))

            def wait_free(self, pe):
                n = self.n - 4
                if n >= 0 or self.before:
                    who = (self.uses if n >= 0 else USES)[n][1]
                    pe.wait_ge(kept[who], self.kept_with(n, who))

        def batches(eng, batch):
            batch(0, 0, 0, 0)
            batch(1, 0, 1, 1)
            with eng.Fori(1, DEC_BATCH // 2) as q:
                for j in range(2):
                    batch(2 * q + j, q, j, 2)

        LAST = DEC_BATCH - 1

        @block.sync
        def _(sp):
            sp.wait_ge(zeroed, 1)
            for j in range(2):
                sp.dma_start(rope_both[(1 - j) * ROPE:(2 - j) * ROPE, 1 - j, j::2, :], c.q_rope_s[j * ROPE:(j + 1) * ROPE]).then_inc(crossed, 16)
            sp.dma_start(new_mask[:], t["new_mask"]).then_inc(consts, 16)
            sp.dma_start(own_query[:], t["own_query"]).then_inc(consts, 16)
            sp.dma_start(w_uv[:], t["w_uv"].rearrange("l (k p) h n -> p (l k) (h n)", p=P)).then_inc(w_uv_landed, 16)

        @block.gpsimd
        def _(pool):
            for b in range(DEC_BATCH):
                j = b % 2
                places = ((rope[j][:], cache_r, 2, scored, PAIRS * (b - 1)), (latent[j][0][:], cache_l, 0, half_left, b - 1),
                          (latent[j][1][:], cache_l, 1, batch_done, b - 1))
                for dst, src, n, left, count in places:
                    if (b, n) == (0, 0):
                        pool.wait_ge(crossed, 32)
                        continue
                    if b >= 2:
                        pool.wait_ge(left, count)
                    pool.indirect_dma_start(dst, None, src, bass.IndirectOffsetOnAxis(ap=ids[:, n, b:b + 1], axis=0)
                                            ).then_inc(landed[j][n], 16)

        @block.tensor
        def _(pe):
            def latent_row(j, row):
                at = row % (RUN // 2) * KV_LORA
                return latent[j][row // (RUN // 2)][:, at:at + KV_LORA]

            def turn_keys(b, j, m, before):
                for (_, _, what), _ in keys_uses(m):
                    use = Use(b, before, ("keys", m, what))
                    use.wait_free(pe)
                    for i in range(PER):
                        row = 2 * PER * m + 2 * i
                        if what == "rope":
                            src = rope[j][:, row * ROPE:(row + 2) * ROPE]
                        else:
                            odd, l = what
                            src = latent_row(j, row + odd)[:, l * P:(l + 1) * P]
                        mm = pe.transpose(use.bank[:, i * P:(i + 1) * P], src, c.ident[:])
                    mm.then_inc(turned, 1)

            def score_pair(b, j, m, before):
                for what in ((1, 1), "rope"):
                    use = Use(b, before, ("keys", m, what))
                    use.wait_kept(pe)
                if m == 0:
                    pe.wait_ge(q_set, 2 * b + 2)
                if before and m in (0, PAIRS // 2):
                    pe.wait_ge(score_kept, 3 * b - 2 + (m != 0))
                half, g = score[m // 2], 2 * (m % 2)
                keys = keysT[m % 2]
                pe.matmul(half[g * ROWS:(g + 2) * ROWS, :], qr_b[j][:].rearrange("p j h s -> p (j h s)"), keys["rope"],
                          start=True, stop=False)
                for odd in range(2):
                    for l in range(LC):
                        mm = pe.matmul(half[(g + odd) * ROWS:(g + odd + 1) * ROWS, :], q_b[j][:, l].rearrange("p h s -> p (h s)"),
                                       keys[odd, l], start=False, stop=(l == LC - 1))
                if m == PAIRS - 1:
                    for l in range(LC):
                        pe.matmul(new_score, q_b[j][:, l].rearrange("p h s -> p (h s)"), c.new_latent[:, l, :],
                                  start=(l == 0), stop=False)
                    mm = pe.matmul(new_score, qr_b[j][:, 0].rearrange("p h s -> p (h s)"), c.new_key[:], start=False, stop=True)
                mm.then_inc(scored, 1)

            def spread(p):
                pe.wait_ge(diagonal_set, p + 1)
                pe.matmul(spread_max, c.ones[:], diagonal[:], start=True, stop=True).then_inc(max_spread, 1)

            def turn_probs(b, p, before):
                pe.wait_ge(exp_done, p + 1)
                for a in range(2):
                    use = Use(b, before, ("probs", a))
                    use.wait_free(pe)
                    for i in range(PER):
                        mm = pe.transpose(use.bank[:, i * P:(i + 1) * P], probs[:, (PER * a + i) * P:(PER * a + i + 1) * P], c.ident[:])
                    mm.then_inc(turned, 1)
                use = Use(b, before, ("new",))
                use.wait_free(pe)
                pe.matmul(use.bank[0:SAMPLE, 0:ROWS], probs[:, KEYS:KEYS + SAMPLE], c.ident[:, 0:ROWS],
                          start=True, stop=True).then_inc(turned, 1)

            def sum_latents(b, p, j, before):
                for key in (("probs", 0), ("new",)):
                    use = Use(b, before, key)
                    use.wait_kept(pe)
                for k in range(2 * PER):
                    for g in range(PER):
                        row = 16 * (k // PER) + 8 * (g // 2) + 2 * (k % PER) + g % 2
                        mm = pe.matmul(out_bank[:], probT[:, k, g * ROWS:(g + 1) * ROWS],
                                  latent_row(j, row), start=(k + g == 0), stop=False)
                    if k == PER - 1:
                        mm.then_inc(half_left, 1)
                pe.matmul(out_bank[:], new_probT[0:SAMPLE, :], c.new_rows[:], start=False, stop=True)
                pe.matmul(total, own_query[:, 1, :], row_total[:], start=True, stop=True).then_inc(batch_done, 1)

            def turn_out(b, p, before):
                use = Use(b, before, ("out",))
                use.wait_free(pe)
                pe.wait_ge(out_set, p + 1)
                for l in range(LC):
                    mm = pe.matmul(use.bank[:, l * ROWS:(l + 1) * ROWS], out_rows[:, l * P:(l + 1) * P], c.ident[0:ROWS, 0:ROWS],
                                   start=True, stop=True)
                mm.then_inc(turned, 1)

            def batch(b, q, j, before):
                for n in (2, 0):
                    pe.wait_ge(landed[j][n], 16 * q + 16)
                turn_keys(b, j, 0, before)
                if before:
                    spread(b - 1)
                turn_keys(b, j, 1, before)
                score_pair(b, j, 0, before)
                if before:
                    turn_probs(b, b - 1, before)
                    sum_latents(b, b - 1, 1 - j, before)
                pe.wait_ge(landed[j][1], 16 * q + 16)
                turn_keys(b, j, 2, before)
                score_pair(b, j, 1, before)
                if before:
                    turn_out(b, b - 1, before)
                turn_keys(b, j, 3, before)
                score_pair(b, j, 2, before)
                score_pair(b, j, 3, before)

            pe.wait_ge(consts, 32)
            batches(pe, batch)
            spread(LAST)
            turn_probs(DEC_BATCH, LAST, "after")
            sum_latents(DEC_BATCH, LAST, LAST % 2, "after")
            turn_out(DEC_BATCH, LAST, "after")
            pe.wait_ge(w_uv_landed, 16)
            Use(DEC_BATCH, "after", ("out",)).wait_kept(pe)
            for h in range(HEADS):
                for l in range(LC):
                    mm = pe.matmul(value_bank[:, h, :], w_uv[:, l, h * VDIM:(h + 1) * VDIM], c.o_lat_s[:, l, h, :],
                                   start=(l == 0), stop=(l == LC - 1))
            mm.then_inc(values_done, 1)

        def keep(eng, who, copy, b, before, key, dst):
            use = Use(b, before, key)
            if use.keeper == who:
                eng.wait_ge(turned, use.done)
                if key[0] == "keys" and (before or key[1] >= 2):
                    eng.wait_ge(scored, PAIRS * b + key[1] - 1)
                copy(dst, use.bank).then_inc(kept[who], 1)

        @block.scalar
        def _(act):
            def keep_keys(b, m, before):
                for (_, _, what), who in keys_uses(m):
                    keep(act, "act", lambda d, s: act.copy(d, s[:]), b, before, ("keys", m, what), keysT[m % 2][what])

            def exponential(p):
                act.wait_ge(biased, p + 1)
                act.activation(probs, scores, ACT.Exp, bias=bias[:], scale=SM_SCALE, accum_out=row_total[:]).then_inc(exp_done, 1)

            def keep_probs(b, before):
                keep(act, "act", lambda d, s: act.copy(d, s[:].rearrange("p (k q) -> p k q", q=P)), b, before, ("probs", 0), probT[:, 0:PER, :])

            def batch(b, q, j, before):
                keep_keys(b, 0, before)
                keep_keys(b, 1, before)
                if before:
                    exponential(b - 1)
                    keep_probs(b, before)
                keep_keys(b, 2, before)
                keep_keys(b, 3, before)

            batches(act, batch)
            exponential(LAST)
            keep_probs(DEC_BATCH, "after")

        @block.vector
        def _(dve):
            def keep_keys(b, m, before):
                for (_, _, what), who in keys_uses(m):
                    keep(dve, "dve", lambda d, s: dve.tensor_copy(d, s[:]), b, before, ("keys", m, what), keysT[m % 2][what])

            def keep_half(b, half, before):
                dve.wait_ge(scored, PAIRS * b + 2 * half + 2)
                if before:
                    dve.wait_ge(exp_done, b)
                dve.tensor_copy(scores[:, half * HALF:(half + 1) * HALF], score[half][:]).then_inc(score_kept, 1)

            def keep_new(b):
                dve.tensor_tensor(scores[0:ROWS, KEYS:KEYS + SAMPLE], new_score,
                                  new_mask[:, bass.ds(b, 1), :].rearrange("p b n -> p (b n)"), ALU.add).then_inc(score_kept, 1)

            def maximum(p):
                dve.wait_ge(score_kept, 3 * p + 3)
                dve.tensor_reduce(row_max[:], scores, AX_X, ALU.max).then_inc(maxed, 1)
                dve.wait_ge(maxed, p + 1)
                dve.tensor_scalar(diagonal[:], c.ident[:], row_max[:], None, ALU.mult).then_inc(diagonal_set, 1)

            def make_bias(p):
                dve.wait_ge(max_spread, p + 1)
                dve.tensor_reduce(query_max[:], spread_max.rearrange("p (g q) -> p q g", q=ROWS), AX_X, ALU.max).then_inc(query_maxed, 1)
                dve.wait_ge(query_maxed, p + 1)
                dve.tensor_tensor(own_max[:], query_max[:], own_query[:, 0, :], ALU.mult).then_inc(own_set, 1)
                dve.wait_ge(own_set, p + 1)
                dve.tensor_reduce(bias[:], own_max[:], AX_X, ALU.add).then_inc(biased, 1)

            def keep_probs(b, before):
                keep(dve, "dve", lambda d, s: dve.tensor_copy(d, s[:].rearrange("p (k q) -> p k q", q=P)), b, before,
                     ("probs", 1), probT[:, PER:2 * PER, :])
                keep(dve, "dve", lambda d, s: dve.tensor_copy(d, s[0:SAMPLE, 0:ROWS]), b, before, ("new",), new_probT[0:SAMPLE, :])

            def normalise(p):
                dve.wait_ge(batch_done, p + 1)
                dve.reciprocal(inv[:], total).then_inc(inverted, 1)
                dve.wait_ge(inverted, p + 1)
                dve.tensor_scalar(out_rows[:], out_bank[:], inv[:], None, ALU.mult).then_inc(out_set, 1)

            def keep_out(b, p, before):
                keep(dve, "dve", lambda d, s: dve.tensor_copy(d, s[:, 0:LC * ROWS].rearrange("p (l h s) -> p l h s", l=LC, h=HEADS)),
                     b, before, ("out",), c.o_lat_s[:, :, :, bass.ds(p * DEC_SEQ, DEC_SEQ)])

            def set_queries(b, j, before):
                if before == 2:
                    dve.wait_ge(scored, PAIRS * b - PAIRS)
                at = bass.ds(b * DEC_SEQ, DEC_SEQ)
                dve.tensor_copy(q_b[j][:], c.q_lat_s[:, :, :, at]).then_inc(q_set, 1)
                dve.tensor_copy(qr_b[j][:], rope_both[:, :, :, at]).then_inc(q_set, 1)

            def batch(b, q, j, before):
                if before:
                    maximum(b - 1)
                set_queries(b, j, before)
                keep_keys(b, 0, before)
                if before:
                    make_bias(b - 1)
                keep_keys(b, 1, before)
                if before:
                    keep_probs(b, before)
                if before:
                    normalise(b - 1)
                keep_keys(b, 2, before)
                keep_half(b, 0, before)
                if before:
                    keep_out(b, b - 1, before)
                keep_keys(b, 3, before)
                keep_half(b, 1, before)
                keep_new(b)

            dve.memset(rope_both[:], 0.0).then_inc(zeroed, 1)
            dve.wait_ge(consts, 32)
            dve.wait_ge(zeroed, 1)
            for j in range(2):
                dve.tensor_copy(rope_both[j * ROPE:(j + 1) * ROPE, j, j::2, :], c.q_rope_s[j * ROPE:(j + 1) * ROPE]).then_inc(q_half_set, 1)
            dve.memset(scores[:, KEYS:KEYS + SAMPLE], NEG).then_inc(new_empty, 1)
            dve.wait_ge(new_empty, 1)
            dve.wait_ge(crossed, 32)
            dve.wait_ge(q_half_set, 2)
            batches(dve, batch)
            maximum(LAST)
            make_bias(LAST)
            keep_probs(DEC_BATCH, "after")
            normalise(LAST)
            keep_out(DEC_BATCH, LAST, "after")
            dve.wait_ge(values_done, 1)
            dve.tensor_copy(c.value[:, :, SEQ:TOKENS], value_bank).then_inc(values_kept, 1)


def store_stage(nc, c, t):
    SLOTS = 4
    with ExitStack() as ctx:
        sem = lambda n: nc.alloc_semaphore(n)
        rows = ctx.enter_context(nc.sbuf_tensor("out_rows", [P, SLOTS, D], F32))
        bank = [ctx.enter_context(nc.psum_tensor(f"out_bank{j}", [P, 512], F32)) for j in range(4)]
        turned, kept = sem("out_turned"), [sem(f"out_kept{j}") for j in range(2)]
        stored = [sem(f"out_stored{j}") for j in range(SLOTS)]
        norm = Norm(nc, ctx, c, "out", [("post", c.acc, DC, ROW_FFN_POST + DC, c.acc)])
        block = ctx.enter_context(nc.Block())
        y = t["y_prompt"].rearrange("a (n p) d -> (a n) p d", p=P)
        tiles = [(i, P if i < QT else SAMPLE) for i in range(QT + 1)]

        @block.tensor
        def _(pe):
            norm.pe(pe)
            for i, width in tiles:
                norm.wait_group(pe, (i * P + width - 1) // GW)
                for half in range(2):
                    if i >= 2:
                        pe.wait_ge(kept[half], i - 1)
                    for n in range(4):
                        mm = pe.transpose(bank[2 * (i % 2) + half][0:width, n * P:(n + 1) * P],
                                          c.y[:, 4 * half + n, i * P:i * P + width], c.ident[:])
                    mm.then_inc(turned, 1)

        def keep(eng, copy, half):
            for i, width in tiles:
                eng.wait_ge(turned, 2 * i + half + 1)
                if i >= SLOTS:
                    eng.wait_ge(stored[i % SLOTS], 16 * (i // SLOTS))
                copy(rows[0:width, i % SLOTS, half * 512:(half + 1) * 512],
                     bank[2 * (i % 2) + half][0:width, :]).then_inc(kept[half], 1)

        @block.scalar
        def _(act):
            norm.act(act)
            keep(act, act.copy, 0)

        @block.vector
        def _(dve):
            norm.dve(dve)
            keep(dve, dve.tensor_copy, 1)

        @block.gpsimd
        def _(pool):
            norm.pool(pool)

        @block.sync
        def _(sp):
            for i, width in tiles:
                for half in range(2):
                    sp.wait_ge(kept[half], i + 1)
                out = y[i] if i < QT else t["y_sample"].rearrange("b s d -> (b s) d")
                sp.dma_start(out, rows[0:width, i % SLOTS, :]).then_inc(stored[i % SLOTS], 16)
            for j in range(SLOTS):
                sp.wait_ge(stored[j], 16 * len(range(j, QT + 1, SLOTS)))


def operand_buffers(nc, ctx, c, tag):
    c.hi, c.lo = (ctx.enter_context(nc.sbuf_tensor(f"operand_{n}{tag}", [P, DC, TOKENS], F32R)) for n in ("hi", "lo"))


def trunk(nc, t):
    c = Chip()
    start = nc.snapshot_sems()
    with ExitStack() as ctx:
        sb = lambda n, s, d=F32: ctx.enter_context(nc.sbuf_tensor(n, s, d))
        c.ident, c.ones, c.eps = sb("ident_sb", [P, P]), sb("ones_sb", [P, P]), sb("rms_and_layer_eps", [P, 2])
        c.param = sb("params", [P, PARAM_ROWS + TAP_ROWS])
        c.y, c.acc = (sb(n, [P, DC, TOKENS]) for n in ("residual", "summed"))
        SA = DEC_BATCH * PAD_A
        with ExitStack() as layer0:
            operand_buffers(nc, layer0, c, "0")
            with ExitStack() as conv:
                csb = lambda n, s, d=F32: conv.enter_context(nc.sbuf_tensor(n, s, d))
                c.state = csb("states", [P, CC, SA + DEC_BATCH * PAD_B])
                c.tails = csb("state_tails", [P, CC, PAD_A + SA + PAD_B + DEC_BATCH * PAD_B])
                load_stage(nc, c, t)
                conv_stage(nc, c, t, c.acc)
                project_stage(nc, c, "w_out", t["w_out_conv"][0], [P] * DC, c.acc, before=LayerNorm)
            reuse_semaphores(nc, start)
            ffn_stage(nc, c, 0, t, sandwich(c, ROW_MIX_POST, ROW_FFN_PRE))
            project_stage(nc, c, "w_mla", t["w_in_mla"][0], [P] * 6, c.acc, sandwich(c, ROW_FFN_POST, ROW_MIX_PRE + DC), twice=True)
        values = ExitStack()
        c.value = values.enter_context(nc.sbuf_tensor("values", [P, DC, TOKENS], F32))
        with ExitStack() as mla:
            msb = lambda n, s, d=F32: mla.enter_context(nc.sbuf_tensor(n, s, d))
            c.new_latent, c.new_key, c.new_rows = msb("new_latent", [P, LC, SAMPLE]), msb("new_key", [P, SAMPLE]), msb("new_rows", [SAMPLE, KV_LORA])
            c.q_lat_s, c.q_rope_s = msb("q_lat_sample", [P, LC, HEADS, SAMPLE]), msb("q_rope_sample", [P, HEADS // 2, SAMPLE])
            c.run_ids = msb("run_ids", [P, 3, DEC_BATCH], U32)
            reuse_semaphores(nc, start)
            c.first_latents, c.first_landed = msb("cache_latent0_first", [P, RUN // 2 * KV_LORA]), nc.alloc_semaphore("latent0_first_landed")
            c.o_lat_s = msb("o_lat_sample", [P, LC, HEADS, SAMPLE])
            with ExitStack() as prompt:
                psb = lambda n, s, d=F32: prompt.enter_context(nc.sbuf_tensor(n, s, d))
                k = Chip()
                k.latent, k.key = psb("latent", [P, LC, TOKENS]), [psb(f"key{j}", [P, TOKENS]) for j in range(2)]
                k.cos, k.sin = psb("cos_sb", [P, TOKENS]), psb("sin_sb", [P, TOKENS])
                k.swap, k.causal = psb("swap_sb", [P, P]), psb("causal_sb", [P, P])
                latent_stage(nc, c, t, k)
                attention_stage(nc, c, t, k, c.acc)
            sample_stage(nc, c, t)
        with values:
            operand_buffers(nc, values, c, "_values")
            project_stage(nc, c, "w_o", t["w_o_mla"][0], [P] * DC, c.acc, before=Split)
        with ExitStack() as layer1:
            operand_buffers(nc, layer1, c, "1")
            reuse_semaphores(nc, start)
            ffn_stage(nc, c, 1, t, sandwich(c, ROW_MIX_POST + DC, ROW_FFN_PRE + DC))
        store_stage(nc, c, t)


_OUTS = [("y_prompt", (1, SEQ, D)), ("y_sample", (DEC_BATCH, DEC_SEQ, D)),
         ("new_conv_a_prompt", (1, 1, PAD_A, CHAN)), ("new_conv_a_sample", (1, DEC_BATCH, PAD_A, CHAN)),
         ("new_conv_b_prompt", (1, 1, PAD_B, CHAN)), ("new_conv_b_sample", (1, DEC_BATCH, PAD_B, CHAN)),
         ("new_kv_latent_prompt", (1, 1, SEQ, KV_LORA)), ("new_kv_latent_sample", (1, DEC_BATCH, DEC_SEQ, KV_LORA)),
         ("new_k_rope_prompt", (1, 1, SEQ, ROPE)), ("new_k_rope_sample", (1, DEC_BATCH, DEC_SEQ, ROPE))]


def _constants():
    f = np.float32
    half = ROPE // 2
    inv_freq = (f(1.0) / (f(10000.0) ** (np.arange(half, dtype=f) * f(2.0 / ROPE)))).astype(f)
    pos = np.concatenate([np.arange(SEQ), np.tile(PAGES * PAGE + np.arange(DEC_SEQ), DEC_BATCH)]).astype(f)
    ang = (inv_freq[:, None] * pos[None, :]).astype(f)
    swap = np.zeros((ROPE, ROPE), f)
    for r in range(half):
        swap[half + r, r] = -1.0
        swap[r, half + r] = 1.0
    q = np.arange(P)
    row_step = np.arange(HEADS * DEC_SEQ) % DEC_SEQ
    key_batch, key_step = np.arange(SAMPLE) // DEC_SEQ, np.arange(SAMPLE) % DEC_SEQ
    ok = (key_batch[None, None, :] == np.arange(DEC_BATCH)[None, :, None]) & (key_step[None, None, :] <= row_step[:, None, None])
    own = np.tile(np.eye(HEADS * DEC_SEQ, dtype=f), (P // (HEADS * DEC_SEQ), 1))
    return {
        "ident": np.eye(P, dtype=f),
        "rope_cos": np.ascontiguousarray(np.tile(np.cos(ang), (4, 1))),
        "rope_sin": np.ascontiguousarray(np.tile(np.sin(ang), (4, 1))),
        "rope_swap": np.kron(np.eye(2, dtype=f), swap),
        "causal": np.where(q[None, :] <= q[:, None], 0.0, NEG).astype(f),
        "new_mask": np.where(ok, 0.0, NEG).astype(f),
        "own_query": np.ascontiguousarray(np.stack([own * f(-SM_SCALE), own], axis=1)),
        "run_offset": (q[:, None] % RUNS_PER_PAGE * np.array([2, 2, 1]) + np.array([0, 1, 0])).astype(f),
    }


def kernel(**inputs):
    import concourse.bacc as _bacc
    from concourse.bass_utils import run_bass_kernel_spmd as _run

    nc = _bacc.Bacc("TRN2", target_bir_lowering=False, num_devices=1)
    given = {n: np.ascontiguousarray(a) for n, a in inputs.items() if n != "page_table"}
    given["pages"] = np.ascontiguousarray(np.repeat(np.asarray(inputs["page_table"]), RUNS_PER_PAGE, axis=1).T)
    given.update(_constants())
    arrays, t = {}, {}
    for name, a in given.items():
        arrays[f"in_{name}"] = a
        t[name] = nc.dram_tensor(f"in_{name}", a.shape, mybir.dt.from_np(a.dtype), kind="ExternalInput").ap()
    for name, shape in _OUTS:
        t[name] = nc.dram_tensor(f"out_{name}", shape, F32, kind="ExternalOutput").ap()
    trunk(nc, t)
    r = _run(nc, [arrays], core_ids=[0])
    return tuple(r.results[0][f"out_{name}"] for name, _ in _OUTS)
```
